# Optimizing a Trainium2 kernel written in Bass

```python
import jax, jax.numpy as jnp
from jax import lax
import numpy as np

D_MODEL = 1024
BATCH = 1
SEQ = 2048
DEPTH = 1
DEC_BATCH = 8
DEC_SEQ = 8
PAST_LEN = 2048
PAGE_SIZE = 128

HEAD_DIM = 64
HEADS_PER_GROUP = D_MODEL // 128
ATTN_GROUPS = ((128, 1), (512, 4), (2048, 16))
N_GROUPS = 3
ATTN_HEADS = N_GROUPS * HEADS_PER_GROUP
ATTN_QKV_WIDTH = ATTN_HEADS * HEAD_DIM
ATTN_WIDTH = HEADS_PER_GROUP * HEAD_DIM
ROPE_DIM = HEAD_DIM // 4
ROPE_THETA = 500000.0
BAND_BLOCK = 128

GLA_HEADS = 4
GLA_DK = D_MODEL // 16
GLA_DV = D_MODEL // 8
GLA_KEY_WIDTH = GLA_HEADS * GLA_DK
GLA_VAL_WIDTH = GLA_HEADS * GLA_DV
GLA_GATE_RANK = 16
GLA_TAU = 16.0
GLA_CHUNK = 64

NORM_EPS = 1e-6
IN_WIDTH = 3 * ATTN_QKV_WIDTH + ATTN_WIDTH + 2 * GLA_KEY_WIDTH + 2 * GLA_VAL_WIDTH + GLA_GATE_RANK + 2 * D_MODEL

kernel_name = "dilated_window_gla_hybrid_step"

def rms_norm(x, w):
    xf = x.astype(jnp.float32)
    y = xf * lax.rsqrt(jnp.mean(xf * xf, axis=-1, keepdims=True) + NORM_EPS)
    return (y * w.astype(jnp.float32)).astype(x.dtype)

def partial_rope(x, pos):
    half = ROPE_DIM // 2
    inv_freq = 1.0 / (ROPE_THETA ** (jnp.arange(half, dtype=jnp.float32) * (2.0 / ROPE_DIM)))
    ang = pos.astype(jnp.float32)[:, None] * inv_freq[None, :]
    cos = jnp.cos(ang)[:, None, :]
    sin = jnp.sin(ang)[:, None, :]
    xr = x[..., :ROPE_DIM].astype(jnp.float32)
    x1, x2 = xr[..., :half], xr[..., half:]
    rot = jnp.concatenate([x1 * cos - x2 * sin, x2 * cos + x1 * sin], axis=-1)
    return jnp.concatenate([rot.astype(x.dtype), x[..., ROPE_DIM:]], axis=-1)

def project_in(x, pos, ln_w, w_in, w_gla_a2, b_gla_a):
    B, S, _ = x.shape
    h = rms_norm(x, ln_w)
    proj = jnp.einsum('bsd,de->bse', h, w_in)
    widths = (ATTN_QKV_WIDTH, ATTN_QKV_WIDTH, ATTN_QKV_WIDTH, ATTN_WIDTH,
              GLA_KEY_WIDTH, GLA_KEY_WIDTH, GLA_VAL_WIDTH, GLA_VAL_WIDTH, GLA_GATE_RANK,
              D_MODEL, D_MODEL)
    splits = [int(c) for c in np.cumsum(widths)[:-1]]
    aq, ak, av, az, gq, gk, gv, gz, glr, mg_a, mg_b = jnp.split(proj, splits, axis=-1)
    aq = partial_rope(aq.reshape(B, S, ATTN_HEADS, HEAD_DIM), pos) * (HEAD_DIM ** -0.5)
    ak = partial_rope(ak.reshape(B, S, ATTN_HEADS, HEAD_DIM), pos)
    av = av.reshape(B, S, ATTN_HEADS, HEAD_DIM)
    gq = gq.reshape(B, S, GLA_HEADS, GLA_DK).astype(jnp.float32) * (GLA_DK ** -0.5)
    gk = gk.reshape(B, S, GLA_HEADS, GLA_DK).astype(jnp.float32)
    gv = gv.reshape(B, S, GLA_HEADS, GLA_DV).astype(jnp.float32)
    gate_pre = (jnp.einsum('bsr,rk->bsk', glr, w_gla_a2) + b_gla_a).astype(jnp.float32)
    log_a = (jax.nn.log_sigmoid(gate_pre) / GLA_TAU).reshape(B, S, GLA_HEADS, GLA_DK)
    return aq, ak, av, az, gq, gk, gv, log_a, gz, mg_a, mg_b

def dilated_window_attn_prompt(q, k, v, window, dilation):
    B, S, H, dh = q.shape
    L = S // dilation
    reach = window // dilation
    blk = BAND_BLOCK
    nblk = -(-L // blk)
    Lp = nblk * blk
    BD = B * dilation

    def to_residue_blocks(t):
        t = t.reshape(B, L, dilation, H, dh).transpose(0, 2, 1, 3, 4).reshape(BD, L, H, dh)
        t = jnp.pad(t, ((0, 0), (0, Lp - L), (0, 0), (0, 0)))
        return t.reshape(BD, nblk, blk, H, dh)

    def with_prev_block(t):
        prev = jnp.pad(t, ((0, 0), (1, 0), (0, 0), (0, 0), (0, 0)))[:, :-1]
        return jnp.concatenate([prev, t], axis=2)

    qb = to_residue_blocks(q)
    kk = with_prev_block(to_residue_blocks(k))
    vv = with_prev_block(to_residue_blocks(v))
    s = jnp.einsum('bnqhd,bnkhd->bnhqk', qb, kk).astype(jnp.float32)
    qi = jnp.arange(blk)[:, None] + blk
    ki = jnp.arange(2 * blk)[None, :]
    dist = qi - ki
    band = (dist >= 0) & (dist <= reach)
    inside = (jnp.arange(nblk)[:, None, None] > 0) | (ki[None] >= blk)
    mask = band[None] & inside
    s = jnp.where(mask[None, :, None], s, -jnp.inf)
    m = jnp.max(s, axis=-1, keepdims=True)
    p = jnp.exp(s - m)
    den = jnp.sum(p, axis=-1, keepdims=True)
    o = jnp.einsum('bnhqk,bnkhd->bnqhd', p / den, vv.astype(jnp.float32))
    lse = (m + jnp.log(den))[..., 0]
    o = o.reshape(BD, Lp, H, dh)[:, :L]
    lse = lse.transpose(0, 1, 3, 2).reshape(BD, Lp, H)[:, :L]
    o = o.reshape(B, dilation, L, H, dh).transpose(0, 2, 1, 3, 4).reshape(B, S, H, dh)
    lse = lse.reshape(B, dilation, L, H).transpose(0, 2, 1, 3).reshape(B, S, H)
    return o, lse

def dilated_window_attn_sample(q, k, v, kv_buf, window, dilation):
    DB, T, H, dh = q.shape
    W_len = kv_buf.shape[1]
    k_all = jnp.concatenate([kv_buf[:, :, 0].astype(k.dtype), k], axis=1)
    v_all = jnp.concatenate([kv_buf[:, :, 1].astype(v.dtype), v], axis=1)
    reach = window // dilation
    idx = W_len + jnp.arange(T)[:, None] - dilation * jnp.arange(reach + 1)[None, :]
    valid = idx >= 0
    idx = jnp.maximum(idx, 0)
    kg = k_all[:, idx]
    vg = v_all[:, idx]
    s = jnp.einsum('bthd,btrhd->bthr', q, kg).astype(jnp.float32)
    s = jnp.where(valid[None, :, None, :], s, -jnp.inf)
    m = jnp.max(s, axis=-1, keepdims=True)
    p = jnp.exp(s - m)
    den = jnp.sum(p, axis=-1, keepdims=True)
    o = jnp.einsum('bthr,btrhd->bthd', p / den, vg.astype(jnp.float32))
    lse = (m + jnp.log(den))[..., 0]
    return o, lse

def combine_groups(outs, lses):
    o = jnp.stack(outs, axis=0)
    w = jax.nn.softmax(jnp.stack(lses, axis=0), axis=0)
    comb = jnp.einsum('gbsh,gbshd->bshd', w, o)
    B, S = comb.shape[0], comb.shape[1]
    return comb.reshape(B, S, ATTN_WIDTH)

def gla_recurrence(q, k, v, log_a, s0, chunk):
    B, S, H, dk = q.shape
    dv = v.shape[-1]
    nc = S // chunk

    def to_chunks(t):
        return t.reshape(B, nc, chunk, H, t.shape[-1]).transpose(1, 0, 3, 2, 4)

    qc, kc, vc, gc = to_chunks(q), to_chunks(k), to_chunks(v), to_chunks(log_a)
    bc = jnp.cumsum(gc, axis=3)
    causal = jnp.tril(jnp.ones((chunk, chunk), dtype=bool))

    def step(state, inp):
        q_, k_, v_, b_ = inp
        b_last = b_[:, :, -1:, :]
        qe = q_ * jnp.exp(b_)
        ke = k_ * jnp.exp(-b_)
        att = jnp.where(causal, jnp.einsum('bhtk,bhsk->bhts', qe, ke), 0.0)
        o = jnp.einsum('bhts,bhsv->bhtv', att, v_) + jnp.einsum('bhtk,bhkv->bhtv', qe, state)
        kd = k_ * jnp.exp(b_last - b_)
        new_state = jnp.exp(b_last[:, :, 0, :, None]) * state + jnp.einsum('bhsk,bhsv->bhkv', kd, v_)
        return new_state, o

    s_fin, o = lax.scan(step, s0, (qc, kc, vc, bc))
    o = o.transpose(1, 0, 3, 2, 4).reshape(B, S, H, dv)
    return o, s_fin

def merge_out(x, o_attn, az, o_gla, gz, mg_a, mg_b, gla_norm_w, w_attn_out, w_gla_out, w_out):
    B, S, _ = x.shape
    o_gla = rms_norm(o_gla, gla_norm_w).reshape(B, S, GLA_VAL_WIDTH).astype(x.dtype)
    ya = jnp.einsum('bsc,cd->bsd', o_attn.astype(x.dtype) * jax.nn.silu(az), w_attn_out)
    yb = jnp.einsum('bsc,cd->bsd', o_gla * jax.nn.silu(gz), w_gla_out)
    mixed = jax.nn.sigmoid(mg_a) * ya + jax.nn.sigmoid(mg_b) * yb
    return x + jnp.einsum('bsd,de->bse', mixed, w_out)

def setup_inputs(seed: int = 0) -> dict:
    key = jax.random.key(seed)
    ks = jax.random.split(key, 16)
    f32 = jnp.float32
    w_lens = [min(w, PAST_LEN) for w, _ in ATTN_GROUPS]
    return {
        'x_prompt': jax.random.normal(ks[0], (BATCH, SEQ, D_MODEL), f32),
        'x_sample': jax.random.normal(ks[1], (DEC_BATCH, DEC_SEQ, D_MODEL), f32),
        'cache_kv_w128': jax.random.normal(ks[2], (DEPTH, DEC_BATCH, w_lens[0], 2, HEADS_PER_GROUP, HEAD_DIM), f32),
        'cache_kv_w512': jax.random.normal(ks[3], (DEPTH, DEC_BATCH, w_lens[1], 2, HEADS_PER_GROUP, HEAD_DIM), f32),
        'cache_kv_w2048': jax.random.normal(ks[4], (DEPTH, DEC_BATCH, w_lens[2], 2, HEADS_PER_GROUP, HEAD_DIM), f32),
        'state_gla': jax.random.normal(ks[5], (DEPTH, DEC_BATCH, GLA_HEADS, GLA_DK, GLA_DV), f32),
        'ln_w': 1.0 + 0.01 * jax.random.normal(ks[6], (DEPTH, D_MODEL), f32),
        'w_in': jax.random.normal(ks[7], (DEPTH, D_MODEL, IN_WIDTH), f32) * D_MODEL ** -0.5,
        'w_gla_a2': jax.random.normal(ks[8], (DEPTH, GLA_GATE_RANK, GLA_KEY_WIDTH), f32) * GLA_GATE_RANK ** -0.5,
        'b_gla_a': 0.1 * jax.random.normal(ks[9], (DEPTH, GLA_KEY_WIDTH), f32),
        'gla_norm_w': 1.0 + 0.01 * jax.random.normal(ks[10], (DEPTH, GLA_DV), f32),
        'w_attn_out': jax.random.normal(ks[11], (DEPTH, ATTN_WIDTH, D_MODEL), f32) * ATTN_WIDTH ** -0.5,
        'w_gla_out': jax.random.normal(ks[12], (DEPTH, GLA_VAL_WIDTH, D_MODEL), f32) * GLA_VAL_WIDTH ** -0.5,
        'w_out': jax.random.normal(ks[13], (DEPTH, D_MODEL, D_MODEL), f32) * D_MODEL ** -0.5,
        'final_norm_w': 1.0 + 0.01 * jax.random.normal(ks[14], (D_MODEL,), f32),
    }

def reference(x_prompt, x_sample, cache_kv_w128, cache_kv_w512, cache_kv_w2048, state_gla,
              ln_w, w_in, w_gla_a2, b_gla_a, gla_norm_w, w_attn_out, w_gla_out, w_out, final_norm_w):
    B, S, _ = x_prompt.shape
    DB, T, _ = x_sample.shape
    pos_p = jnp.arange(S, dtype=jnp.int32)
    pos_s = PAST_LEN + jnp.arange(T, dtype=jnp.int32)
    caches = (cache_kv_w128, cache_kv_w512, cache_kv_w2048)
    hp, hs = x_prompt, x_sample
    kv_p = [[] for _ in range(N_GROUPS)]
    kv_s = [[] for _ in range(N_GROUPS)]
    gla_p, gla_s = [], []
    for layer in range(DEPTH):
        aq, ak, av, az, gq, gk, gv, ga, gz, ma, mb = project_in(
            hp, pos_p, ln_w[layer], w_in[layer], w_gla_a2[layer], b_gla_a[layer])
        outs, lses = [], []
        for g, (win, dil) in enumerate(ATTN_GROUPS):
            hs_ = slice(g * HEADS_PER_GROUP, (g + 1) * HEADS_PER_GROUP)
            o, l = dilated_window_attn_prompt(aq[:, :, hs_], ak[:, :, hs_], av[:, :, hs_], win, dil)
            outs.append(o)
            lses.append(l)
            kv_p[g].append(jnp.stack([ak[:, :, hs_], av[:, :, hs_]], axis=2)[:, S - min(win, S):])
        o_attn = combine_groups(outs, lses)
        s0 = jnp.zeros((B, GLA_HEADS, GLA_DK, GLA_DV), jnp.float32)
        o_gla, s_fin = gla_recurrence(gq, gk, gv, ga, s0, min(GLA_CHUNK, S))
        gla_p.append(s_fin)
        hp = merge_out(hp, o_attn, az, o_gla, gz, ma, mb, gla_norm_w[layer],
                       w_attn_out[layer], w_gla_out[layer], w_out[layer])
        aq, ak, av, az, gq, gk, gv, ga, gz, ma, mb = project_in(
            hs, pos_s, ln_w[layer], w_in[layer], w_gla_a2[layer], b_gla_a[layer])
        outs, lses = [], []
        for g, (win, dil) in enumerate(ATTN_GROUPS):
            hs_ = slice(g * HEADS_PER_GROUP, (g + 1) * HEADS_PER_GROUP)
            o, l = dilated_window_attn_sample(aq[:, :, hs_], ak[:, :, hs_], av[:, :, hs_],
                                              caches[g][layer], win, dil)
            outs.append(o)
            lses.append(l)
            kv_s[g].append(jnp.stack([ak[:, :, hs_], av[:, :, hs_]], axis=2))
        o_attn = combine_groups(outs, lses)
        o_gla, s_new = gla_recurrence(gq, gk, gv, ga, state_gla[layer].astype(jnp.float32), T)
        gla_s.append(s_new)
        hs = merge_out(hs, o_attn, az, o_gla, gz, ma, mb, gla_norm_w[layer],
                       w_attn_out[layer], w_gla_out[layer], w_out[layer])
    y_prompt = rms_norm(hp, final_norm_w)
    y_sample = rms_norm(hs, final_norm_w)
    kv128_p, kv512_p, kv2048_p = (jnp.stack(kv_p[0]), jnp.stack(kv_p[1]), jnp.stack(kv_p[2]))
    kv128_s, kv512_s, kv2048_s = (jnp.stack(kv_s[0]), jnp.stack(kv_s[1]), jnp.stack(kv_s[2]))
    gla_prompt = jnp.stack(gla_p)
    gla_sample = jnp.stack(gla_s)
    return (y_prompt, y_sample, kv128_p, kv512_p, kv2048_p, gla_prompt, kv128_s, kv512_s, kv2048_s, gla_sample)


_drawn_inputs = setup_inputs


def setup_inputs(seed=0):
    import zlib

    import numpy as np

    out = dict(_drawn_inputs(seed))
    spreads = {}
    factors = {'cache_kv_w128': 3.84,
     'cache_kv_w512': 3.854,
     'cache_kv_w2048': 3.788,
     'ln_w': 3.761,
     'gla_norm_w': 8.0,
     'final_norm_w': 5.743}
    for name, (base, spread) in spreads.items():
        noise = np.random.default_rng([zlib.crc32(name.encode()), seed]).standard_normal(out[name].shape)
        drawn = base * np.exp(spread * noise) if base else spread * noise
        out[name] = __import__('jax').numpy.asarray(drawn.astype(out[name].dtype))
    for name, factor in factors.items():
        out[name] = (out[name] * factor).astype(out[name].dtype)
    return out
```

```python
from contextlib import ExitStack

import concourse.bass as bass
from concourse import mybir

F32 = mybir.dt.float32
F32R = mybir.dt.float32r
U32 = mybir.dt.uint32
ALU = mybir.AluOpType
ACT = mybir.ActivationFunctionType
AX_X = mybir.AxisListType.X
ds = bass.ds

D = 1024
SEQ = 2048
DB, T = 8, 8
NS = DB * T
TOK = SEQ + NS
P = 128
KC = D // P
NT = SEQ // P
CH = 512
HD = 64
NH = 8
HALF = 8
EPS = 1e-6

COL_AZ, COL_GQK, COL_GV, COL_GZ, COL_GLR, COL_MGA = 4608, 5120, 5632, 6144, 6656, 6672
RANK = 16
IN_W = 8720

N_ROPED, N_TM = 6, 16
TM_GV, TM_AZ, TM_GZ, TM_MG = 9, 10, 11, 12
TM_W = N_TM * CH
N_CHUNK = N_TM + 1
FM_GQ, FM_GK = 0, 256
TS_W = CH + RANK


def scope(nc):
    st = ExitStack()
    sems = []

    def sb(name, shape, dt=F32):
        return st.enter_context(nc.sbuf_tensor(name, shape, dt))

    def pb(name, shape, dt=F32):
        return st.enter_context(nc.psum_tensor(name, shape, dt))

    def sem(name):
        sems.append(nc.alloc_semaphore(name))
        return sems[-1]

    def clear():
        if sems:
            nc.clear_and_free_semaphores(sems)
            nc.all_engine_barrier()

    st.callback(clear)
    return st, sb, pb, sem


def rsqrt_steps(nc, dve, done, before, m):
    nc.vector.reciprocal(m[3], m[2]).then_inc(done, 1)
    dve.wait_ge(done, before + 1)
    nc.vector.tensor_scalar(m[4], m[1], m[3], m[3], ALU.mult, ALU.mult).then_inc(done, 1)
    dve.wait_ge(done, before + 2)
    nc.vector.tensor_scalar(m[5], m[4], -0.5, 1.5, ALU.mult, ALU.add).then_inc(done, 1)
    dve.wait_ge(done, before + 3)
    nc.vector.tensor_tensor(m[2], m[3], m[5], ALU.mult).then_inc(done, 1)
    dve.wait_ge(done, before + 4)


def norm_and_transpose(nc, A, hT_hi, hT_lo, ident):
    st, sb, pb, sem = scope(nc)
    with st:
        xs = sb("a_x", [P, 2, D])
        junk = sb("a_junk", [P, D])
        hf = sb("a_hf", [P, 2, KC, P])
        lnw = sb("a_lnw", [P, KC])
        ms = sb("a_ms", [P, 2, 6])
        pt = pb("a_pt", [P, 2, 2, 4, P])
        x_in = [sem("a_x_in0"), sem("a_x_in1")]
        w_in = sem("a_w_in")
        x_free = sem("a_x_free")
        sq_done = sem("a_sq_done")
        stat = sem("a_stat")
        rooted = sem("a_rooted")
        scaled = sem("a_scaled")
        tr_done = sem("a_tr_done")
        weighted = sem("a_weighted")
        hi_done = sem("a_hi_done")
        lo_done = sem("a_lo_done")
        xp = A["x_prompt"].rearrange("a s d -> (a s) d")
        xq = A["x_sample"].rearrange("a s d -> (a s) d")
        with nc.Block() as block:

            @block.sync
            def _(sp):
                sp.dma_start(lnw[:, :], A["ln_w"]).then_inc(w_in, 16)
                sp.sem_inc(x_free, 2)
                with sp.Fori(0, NT // 2) as i:
                    for s in range(2):
                        sp.wait_ge(x_free, 2 * i + s + 1)
                        sp.dma_start(xs[:, s, :], xp[ds((2 * i + s) * P, P), :]).then_inc(x_in[s], 16)
                sp.wait_ge(x_free, NT + 1)
                sp.dma_start(xs[0:NS, 0, :], xq).then_inc(x_in[0], 16)

            @block.scalar
            def _(act):
                def square(i, s, n, rows):
                    act.wait_ge(x_in[s], 16 * i + 16)
                    nc.scalar.activation(junk[0:rows, :], xs[0:rows, s, :], ACT.Square,
                                         accum_out=ms[0:rows, s, 0:1]).then_inc(sq_done, 1)

                def root(n, s, rows):
                    act.wait_ge(stat, 5 * n + 1)
                    nc.scalar.activation(ms[0:rows, s, 2:3], ms[0:rows, s, 1:2], ACT.Sqrt).then_inc(rooted, 1)

                def round_hi(n, s, off, cols):
                    act.wait_ge(weighted, 2 * n + 2)
                    nc.scalar.copy(hT_hi[:, :, ds(off, cols)], hf[:, s, :, 0:cols]).then_inc(hi_done, 1)

                with act.Fori(0, NT // 2) as i:
                    for s in range(2):
                        square(i, s, 2 * i + s, P)
                        root(2 * i + s, s, P)
                        round_hi(2 * i + s, s, (2 * i + s) * P, P)
                square(NT // 2, 0, NT, NS)
                root(NT, 0, NS)
                round_hi(NT, 0, SEQ, NS)

            @block.vector
            def _(dve):
                dve.wait_ge(w_in, 16)
                dve.sem_inc(lo_done, 1)

                def tile(n, s, off, rows):
                    dve.wait_ge(sq_done, n + 1)
                    m = [ms[0:rows, s, j:j + 1] for j in range(6)]
                    nc.vector.tensor_scalar(m[1], m[0], 1.0 / D, EPS, ALU.mult, ALU.add).then_inc(stat, 1)
                    dve.wait_ge(rooted, n + 1)
                    rsqrt_steps(nc, dve, stat, 5 * n + 1, m)
                    nc.vector.tensor_scalar(xs[0:rows, s, :], xs[0:rows, s, :], ms[0:rows, s, 2:3], None,
                                            ALU.mult).then_inc(scaled, 1)
                    for h in range(2):
                        dve.wait_ge(tr_done, 2 * n + h + 1)
                        nc.vector.tensor_tensor(
                            hf[:, s, 4 * h:4 * h + 4, 0:rows], pt[:, s, h, :, 0:rows],
                            lnw[:, 4 * h:4 * h + 4].unsqueeze(2).to_broadcast([P, 4, rows]),
                            ALU.mult).then_inc(weighted, 1)
                    dve.wait_ge(hi_done, n + 1)
                    nc.vector.tensor_tensor(hT_lo[:, :, ds(off, rows)], hf[:, s, :, 0:rows],
                                            hT_hi[:, :, ds(off, rows)].bitcast(F32),
                                            ALU.subtract).then_inc(lo_done, 1)

                with dve.Fori(0, NT // 2) as i:
                    for s in range(2):
                        tile(2 * i + s, s, (2 * i + s) * P, P)
                tile(NT, 0, SEQ, NS)
                dve.wait_ge(lo_done, NT + 2)

            @block.tensor
            def _(pe):
                def tile(n, s, rows):
                    pe.wait_ge(scaled, n + 1)
                    for h in range(2):
                        for c in range(4):
                            k = 4 * h + c
                            last = nc.tensor.transpose(pt[:, s, h, c, 0:rows], xs[0:rows, s, k * P:(k + 1) * P],
                                                       ident[0:rows, 0:rows])
                        last.then_inc(tr_done, 1)
                    pe.wait_ge(tr_done, 2 * n + 2)
                    pe.sem_inc(x_free, 1)

                with pe.Fori(0, NT // 2) as i:
                    for s in range(2):
                        tile(2 * i + s, s, P)
                tile(NT, 0, NS)


def project(nc, A, S, hT_hi, hT_lo):
    TMs, TSs, FMs, GLs = S["tm"], S["ts"], S["fm"], S["gl"]
    TILES = NT + 1
    LASTS = TOK - P
    st, sb, pb, sem = scope(nc)
    with st:
        raw = sb("b_raw", [P, KC, CH])
        whi = sb("b_whi", [P, KC, CH], F32R)
        wlo = sb("b_wlo", [P, KC, CH], F32R)
        stage = sb("b_stage", [P, 5, CH])
        cs = sb("b_cs", [P, TILES, 2, HALF])
        rc = sb("b_rc", [P, NH, 2, HALF])
        rs = sb("b_rs", [P, NH, 2, HALF])
        acc = pb("b_acc", [P, 5, CH])
        cs_in = sem("b_cs_in")
        w_in = [sem("b_w_in0"), sem("b_w_in1")]
        hi_done = sem("b_hi_done")
        lo_done = sem("b_lo_done")
        w_used = sem("b_w_used")
        mm_done = sem("b_mm_done")
        evacd = sem("b_evacd")
        roped = sem("b_roped")
        rmul = sem("b_rmul")
        stored = [sem(f"b_stored{k}") for k in range(5)]
        W = A["w_in"].rearrange("a (c p) e -> p (a c) e", p=P)
        slot = lambda t: t % 4 if t < NT else 4
        EV0 = 4
        N_ALL = N_CHUNK * TILES

        with nc.Block() as block:

            @block.sync
            def _(sp):
                sp.dma_start(cs[:, :, :, :], A["rope"].rearrange("(t p) (a f) -> p t a f", p=P, a=2)).then_inc(cs_in, 16)
                for k in range(5):
                    sp.sem_inc(stored[k], 16)

                def load(i, col, width=CH):
                    for h in range(2):
                        if not (isinstance(i, int) and i == 0):
                            sp.wait_ge(lo_done, 8 * i - 4 + 4 * h)
                        sp.dma_start(raw[:, 4 * h:4 * h + 4, 0:width],
                                     W[:, 4 * h:4 * h + 4, ds(col, width)]).then_inc(w_in[h], 16)

                def store(i, t, dst, src):
                    sp.dma_start(dst, src).then_inc(stored[slot(t)], 16)

                def tm_chunk(i, ready):
                    for t in range(TILES):
                        ready(TILES * i + t)
                        if t < NT:
                            store(i, t, TMs[t * P:(t + 1) * P, ds(i * CH, CH)], stage[:, slot(t), :])
                        else:
                            store(i, t, TMs[SEQ:TOK, ds(i * CH, CH)], stage[NS:P, 4, :])

                rotated = lambda n: sp.wait_ge(roped, n + 2)
                copied = lambda n: sp.wait_ge(evacd, EV0 + n + 1)
                load(0, 0)
                with sp.Fori(0, N_ROPED) as i:
                    load(i + 1, (i + 1) * CH)
                    tm_chunk(i, rotated)
                with sp.Fori(N_ROPED, TM_GV - 1) as i:
                    load(i + 1, (i + 1) * CH)
                    tm_chunk(i, copied)
                for i, col in ((TM_GV - 1, COL_GV), (TM_GV, COL_AZ), (TM_AZ, COL_GZ)):
                    load(i + 1, col)
                    tm_chunk(i, copied)
                with sp.Fori(TM_GZ, N_TM - 1) as i:
                    load(i + 1, COL_MGA + CH * (i - TM_GZ))
                    tm_chunk(i, copied)
                load(N_TM, COL_GQK)
                tm_chunk(N_TM - 1, copied)
                load(N_CHUNK, COL_GLR, P)
                for t in range(NT):
                    copied(TILES * N_TM + t)
                    store(N_TM, t, FMs[(t // 4) * P:(t // 4 + 1) * P, (t % 4) * CH:(t % 4 + 1) * CH], stage[:, slot(t), :])
                copied(TILES * N_TM + NT)
                store(N_TM, NT, TSs[:, 0:CH], stage[NS:P, 4, :])
                for tb in range(4):
                    copied(N_ALL + tb)
                    store(N_CHUNK, tb, GLs[:, tb * CH:(tb + 1) * CH], stage[0:RANK, tb, :])
                copied(N_ALL + 4)
                store(N_CHUNK, NT, TSs[:, CH:TS_W], stage[NS:P, 4, 0:RANK])
                for k in range(4):
                    sp.wait_ge(stored[k], 16 + 16 * (4 * N_CHUNK + 1))
                sp.wait_ge(stored[4], 16 + 16 * (N_CHUNK + 1))

            @block.scalar
            def _(act):
                def split_hi(i, width=CH):
                    for k in range(KC):
                        if k % 4 == 0:
                            act.wait_ge(w_in[k // 4], 16 * i + 16)
                        if not (isinstance(i, int) and i == 0):
                            act.wait_ge(w_used, 8 * i - 8 + k + 1)
                        nc.scalar.copy(whi[:, k, 0:width], raw[:, k, 0:width]).then_inc(hi_done, 1)

                def evac(i, t, width=CH):
                    act.wait_ge(mm_done, TILES * i + t + 1)
                    uses = 4 * i + t // 4 if t < NT else i
                    act.wait_ge(stored[slot(t)], 16 * uses + 16)
                    nc.scalar.copy(stage[:, slot(t), 0:width], acc[:, slot(t), 0:width]).then_inc(evacd, 1)

                act.sem_inc(evacd, EV0)
                split_hi(0)
                with act.Fori(0, N_CHUNK - 1) as i:
                    for t in range(NT):
                        evac(i, t)
                    split_hi(i + 1)
                    evac(i, NT)
                i = N_CHUNK - 1
                for t in range(NT):
                    evac(i, t)
                split_hi(N_CHUNK, P)
                evac(i, NT)
                for tb in range(4):
                    act.wait_ge(mm_done, N_ALL + tb + 1)
                    act.wait_ge(stored[tb], 16 + 16 * 4 * N_CHUNK)
                    nc.scalar.copy(stage[:, tb, :], acc[:, tb, :]).then_inc(evacd, 1)
                act.wait_ge(mm_done, N_ALL + 5)
                act.wait_ge(stored[4], 16 + 16 * N_CHUNK)
                nc.scalar.copy(stage[:, 4, 0:RANK], acc[:, 4, 0:RANK]).then_inc(evacd, 1)

            @block.vector
            def _(dve):
                def split_lo(i, width=CH):
                    for k in range(KC):
                        dve.wait_ge(hi_done, 8 * i + k + 1)
                        nc.vector.tensor_tensor(wlo[:, k, 0:width], raw[:, k, 0:width],
                                                whi[:, k, 0:width].bitcast(F32), ALU.subtract).then_inc(lo_done, 1)

                def rope(i, t):
                    n = TILES * i + t
                    dve.wait_ge(evacd, EV0 + n + 1)
                    dve.wait_ge(roped, n + 1)
                    x = stage[:, slot(t), :].rearrange("p (h e) -> p h e", h=NH)[:, :, 0:2 * HALF].rearrange(
                        "p h (a f) -> p h a f", a=2)
                    full = [P, NH, 2, HALF]
                    cos = cs[:, t, 0:1, :].unsqueeze(1).to_broadcast(full)
                    sin = cs[:, t, 1:2, :].unsqueeze(1).to_broadcast(full)
                    nc.vector.tensor_tensor(rc[:, :, :, :], x, cos, ALU.mult).then_inc(rmul, 1)
                    nc.vector.tensor_tensor(rs[:, :, :, :], x, sin, ALU.mult).then_inc(rmul, 1)
                    dve.wait_ge(rmul, 2 * n + 2)
                    nc.vector.tensor_tensor(x[:, :, 0, :], rc[:, :, 0, :], rs[:, :, 1, :], ALU.subtract)
                    nc.vector.tensor_tensor(x[:, :, 1, :], rc[:, :, 1, :], rs[:, :, 0, :], ALU.add).then_inc(roped, 1)

                dve.wait_ge(cs_in, 16)
                dve.sem_inc(roped, 1)
                split_lo(0)
                with dve.Fori(0, N_ROPED) as i:
                    for t in range(NT):
                        rope(i, t)
                    split_lo(i + 1)
                    rope(i, NT)
                with dve.Fori(N_ROPED, N_CHUNK - 1) as i:
                    split_lo(i + 1)
                split_lo(N_CHUNK, P)

            @block.tensor
            def _(pe):
                def product(out, k, stat_hi, stat_lo, mov_hi, mov_lo):
                    nc.tensor.matmul(out, stat_hi, mov_hi, start=(k == 0), stop=False)
                    nc.tensor.matmul(out, stat_hi, mov_lo, start=False, stop=False)
                    return nc.tensor.matmul(out, stat_lo, mov_hi, start=False, stop=(k == KC - 1))

                def tile(i, t, out, stat, mov):
                    pe.wait_ge(evacd, TILES * i + t + 1)
                    for k in range(KC):
                        if t == 0:
                            pe.wait_ge(lo_done, 8 * i + k + 1)
                        last = product(out, k, *stat(k), *mov(k))
                        if t == NT and k < KC - 1:
                            last.then_inc(w_used, 1)
                    last.then_inc(mm_done, 1)
                    if t == NT:
                        pe.wait_ge(mm_done, TILES * i + t + 1)
                        pe.sem_inc(w_used, 1)

                def tokens(off, width):
                    return lambda k: (hT_hi[:, k, off:off + width], hT_lo[:, k, off:off + width])

                def weights(off, width):
                    return lambda k: (whi[:, k, off:off + width], wlo[:, k, off:off + width])

                with pe.Fori(0, N_TM) as i:
                    for t in range(TILES):
                        tile(i, t, acc[:, slot(t), :], tokens(t * P if t < NT else LASTS, P), weights(0, CH))
                for t in range(NT):
                    tile(N_TM, t, acc[:, slot(t), :], weights((t // 4) * P, P), tokens((t % 4) * CH, CH))
                tile(N_TM, NT, acc[:, 4, :], tokens(LASTS, P), weights(0, CH))
                for tb in range(4):
                    tile(N_CHUNK, tb, acc[:, tb, :], weights(0, P), tokens(tb * CH, CH))
                pe.wait_ge(evacd, N_ALL + 5)
                for k in range(KC):
                    last = product(acc[:, 4, 0:RANK], k, *tokens(LASTS, P)(k), *weights(0, RANK)(k))
                last.then_inc(mm_done, 1)


NEG = -3.0e38
LOWEST = -3.4e38
WINDOWS = (128, 512, 2048)
GROUPS = ((1, 16), (4, 4), (16, 1))
LEAD = 8
OG_W = CH + 2 * NH


def attend_prompt(nc, A, S, O, ident):
    TMs, OG = S["tm"], S["og"]
    UNROLL = 4
    st, sb, pb, sem = scope(nc)
    with st:
        qk = sb("c_qk", [P, 2, 2, CH])
        v = sb("c_v", [P, UNROLL, CH])
        qT = sb("c_qT", [P, 2, 4, P])
        kT = sb("c_kT", [P, 4, UNROLL + 1, P])
        sm = sb("c_sm", [P, 2, 2, 2 * P])
        p = sb("c_p", [P, 2, 2, 2 * P])
        pT = sb("c_pT", [P, 2, 4, P])
        mx = sb("c_mx", [P, 2, 2])
        og = sb("c_og", [P, UNROLL, OG_W])
        mask = sb("c_mask", [P, 2, 2 * P])
        first = sb("c_first", [P, 2 * P])
        p_qk = pb("c_p_qk", [P, CH])
        p_s = pb("c_p_s", [P, 2, 2, CH])
        p_t = pb("c_p_t", [P, 2, 4, P])
        p_o = pb("c_p_o", [P, NH, HD])

        mask_in = sem("c_mask_in")
        qk_in = [sem("c_qk_in0"), sem("c_qk_in1")]
        v_in = [sem(f"c_v_in{j}") for j in range(UNROLL)]
        stored = [sem(f"c_stored{j}") for j in range(UNROLL)]
        zeroed = sem("c_zeroed")
        windows_out = sem("c_windows_out")
        first_set = sem("c_first_set")
        tqk_done = sem("c_tqk_done")
        q_evacd = sem("c_q_evacd")
        k_evacd = sem("c_k_evacd")
        o_evacd = sem("c_o_evacd")
        qk_done = sem("c_qk_done")
        turns = sem("c_turns")
        masked = sem("c_masked")
        maxed = sem("c_maxed")
        exp_done = sem("c_exp_done")
        pt_done = sem("c_pt_done")
        pt_evacd_act = sem("c_pt_evacd_act")
        pt_evacd_dve = sem("c_pt_evacd_dve")
        pv_done = sem("c_pv_done")

        def loops(eng, body):
            for nth, g in enumerate((1, 0, 2)):
                with eng.Fori(0, NT // UNROLL) as i:
                    body(g, NT * nth + UNROLL * i, i)

        with nc.Block() as block:
            def evac_of(n0, w):
                return (pt_evacd_dve if w % 2 else pt_evacd_act), LEAD + 2 * n0 + w // 2 + 1

            def evac(eng, copy, n0, w, done, near):
                eng.wait_ge(pt_done, LEAD + 4 * n0 + w + 1)
                eng.wait_ge(pv_done, LEAD + 4 * n0 + w - 1)
                if near:
                    copy(pT[:, w % 2, 1::2, :], p_t[:, w % 2, 1::2, :]).then_inc(done, 1)
                else:
                    copy(pT[:, w % 2, :, :], p_t[:, w % 2, :, :]).then_inc(done, 1)


            @block.sync
            def _(sp):
                sp.dma_start(mask[:, :, :], A["masks"]).then_inc(mask_in, 16)

                def body(g, n0, i):
                    dil, nblk = GROUPS[g]
                    for j in range(UNROLL):
                        n = n0 + j
                        if g == 0:
                            rows = TMs[ds((UNROLL * i + j) * P, P), :]
                        elif g == 1:
                            rows = TMs[0:SEQ, :].rearrange("(a r) e -> r a e", r=dil)[ds(i, 1), j * P:(j + 1) * P, :]
                            rows = rows.rearrange("r a e -> (r a) e")
                        else:
                            rows = TMs[0:SEQ, :].rearrange("(a r) e -> r a e", r=dil)[ds(UNROLL * i + j, 1), :, :]
                            rows = rows.rearrange("r a e -> (r a) e")
                        sp.wait_ge(tqk_done, LEAD + 2 * (n - 2) + 2)
                        for a in range(2):
                            sp.dma_start(qk[:, j % 2, a, :], rows[:, (3 * a + g) * CH:(3 * a + g + 1) * CH]
                                         ).then_inc(qk_in[j % 2], 16)
                        sp.wait_ge(pv_done, LEAD + 4 * (n - 3) + 4)
                        if j == UNROLL - 1:
                            sp.wait_ge(zeroed, 2)
                        sp.dma_start(v[:, j, :], rows[:, (6 + g) * CH:(7 + g) * CH]).then_inc(v_in[j], 16)

                for j in range(UNROLL):
                    sp.sem_inc(stored[j], 16)
                loops(sp, body)
                for j in range(UNROLL):
                    sp.wait_ge(stored[j], 16 + 16 * 3 * NT // UNROLL)

            @block.gpsimd
            def _(pool):
                nc.gpsimd.memset(kT[:, :, 0, :], 0.0).then_inc(zeroed, 1)
                nc.gpsimd.memset(v[:, UNROLL - 1, :], 0.0).then_inc(zeroed, 1)
                store_windows(pool, S, O, windows_out)
                pool.wait_ge(windows_out, 12 * 16)

            @block.tensor
            def _(pe):
                for s in (tqk_done, qk_done, pt_done, pv_done):
                    pe.sem_inc(s, LEAD)
                pe.wait_ge(zeroed, 2)

                def transposes(n, j, a):
                    if a == 0:
                        pe.wait_ge(qk_in[j % 2], 16 * (n - j) + 32 * (j // 2) + 32)
                        pe.wait_ge(k_evacd, LEAD + n)
                    else:
                        pe.wait_ge(q_evacd, LEAD + n + 1)
                    for c in range(4):
                        last = nc.tensor.transpose(p_qk[:, c * P:(c + 1) * P],
                                                   qk[:, j % 2, a, c * P:(c + 1) * P], ident[:, :])
                    last.then_inc(tqk_done, 1)

                def body(g, n0, i):
                    near = g == 2

                    def scores(w):
                        j, c = divmod(w, 4)
                        if c == 0:
                            pe.wait_ge(q_evacd, LEAD + n0 + j + 1)
                            pe.wait_ge(k_evacd, LEAD + n0 + j + 1)
                        pe.wait_ge(masked, LEAD + 4 * n0 + w - 1)
                        for h in range(2):
                            rows = slice(HD * h, HD * h + HD)
                            keys = kT[rows, c, j + 1:j + 2, :] if near else kT[rows, c, j:j + 2, :]
                            out = p_s[:, h, w % 2, P if near else 0:2 * P]
                            last = nc.tensor.matmul(out, qT[rows, j % 2, c, :], keys, start=True, stop=True)
                        last.then_inc(qk_done, 1)

                    def transpose_p(w):
                        pe.wait_ge(exp_done, LEAD + 4 * n0 + w + 1)
                        pe.wait_ge(*evac_of(n0, w - 2))
                        for h in range(2):
                            for b in ((1,) if near else (0, 1)):
                                last = nc.tensor.transpose(p_t[:, w % 2, 2 * h + b, :],
                                                           p[:, w % 2, h, b * P:(b + 1) * P], ident[:, :])
                        last.then_inc(pt_done, 1)

                    def sums(w):
                        j, c = divmod(w, 4)
                        pe.wait_ge(*evac_of(n0, w))
                        if c == 0:
                            pe.wait_ge(v_in[j], 4 * n0 + 16)
                            pe.wait_ge(o_evacd, LEAD + n0 + j)
                        for h in range(2):
                            cols = slice((2 * c + h) * HD, (2 * c + h + 1) * HD)
                            for b in ((1,) if near else (0, 1)):
                                vb = v[:, j if b else (j - 1) % UNROLL, cols]
                                last = nc.tensor.matmul(p_o[:, 2 * c + h, :], pT[:, w % 2, 2 * h + b, :], vb,
                                                        start=(b == 1 if near else b == 0), stop=(b == 1))
                        last.then_inc(pv_done, 1)

                    transposes(n0, 0, 0)
                    transposes(n0, 0, 1)
                    N = 4 * UNROLL
                    for w in range(N + 2):
                        if w < N:
                            scores(w)
                        if w % 4 in (1, 2) and w // 4 + 1 < UNROLL:
                            transposes(n0 + w // 4 + 1, w // 4 + 1, w % 4 - 1)
                        if 1 <= w <= N:
                            transpose_p(w - 1)
                        if w >= 2:
                            sums(w - 2)

                loops(pe, body)

            @block.scalar
            def _(act):
                for s in (q_evacd, o_evacd, exp_done, pt_evacd_act):
                    act.sem_inc(s, LEAD)

                def store(g, n, i, j):
                    dil, _ = GROUPS[g]
                    act.wait_ge(o_evacd, LEAD + n + 1)
                    out = OG[0:SEQ, g, :]
                    if g == 0:
                        out = out[ds((UNROLL * i + j) * P, P), :]
                    else:
                        out = out.rearrange("(a r) e -> r a e", r=dil)
                        out = out[ds(i, 1), j * P:(j + 1) * P, :] if g == 1 else out[ds(UNROLL * i + j, 1), :, :]
                        out = out.rearrange("r a e -> (r a) e")
                    act.dma_start(out, og[:, j, :]).then_inc(stored[j], 16)

                def body(g, n0, i):
                    near = g == 2

                    def q_evac(n, j):
                        act.wait_ge(tqk_done, LEAD + 2 * n + 1)
                        act.wait_ge(qk_done, LEAD + 4 * (n - 1))
                        nc.scalar.copy(qT[:, j % 2, :, :], p_qk[:, :]).then_inc(q_evacd, 1)

                    def exps(w):
                        j, c = divmod(w, 4)
                        act.wait_ge(maxed, LEAD + 4 * n0 + w + 1)
                        act.wait_ge(pt_done, LEAD + 4 * n0 + w - 1)
                        lo = P if near else 0
                        for h in range(2):
                            hh = 2 * c + h
                            last = nc.scalar.activation(p[:, w % 2, h, lo:], sm[:, w % 2, h, lo:], ACT.Exp,
                                                        bias=og[:, j, CH + hh:CH + hh + 1],
                                                        accum_out=og[:, j, CH + NH + hh:CH + NH + hh + 1])
                        last.then_inc(exp_done, 1)

                    def o_evac(j):
                        act.wait_ge(pv_done, LEAD + 4 * (n0 + j) + 4)
                        nc.scalar.copy(og[:, j, 0:CH], p_o[:, :, :]).then_inc(o_evacd, 1)

                    q_evac(n0, 0)
                    N = 4 * UNROLL
                    for w in range(N + 2):
                        if w < N:
                            exps(w)
                        if w % 4 == 1 and w // 4 + 1 < UNROLL:
                            q_evac(n0 + w // 4 + 1, w // 4 + 1)
                        if 1 <= w <= N and (w - 1) % 2 == 0:
                            evac(act, nc.scalar.copy, n0, w - 1, pt_evacd_act, near)
                        if w >= 2 and (w - 2) % 4 == 3:
                            o_evac((w - 2) // 4)
                            store(g, n0 + (w - 2) // 4, i, (w - 2) // 4)

                loops(act, body)

            @block.vector
            def _(dve):
                for s in (k_evacd, masked, maxed, pt_evacd_dve):
                    dve.sem_inc(s, LEAD)
                dve.wait_ge(mask_in, 16)
                dve.wait_ge(zeroed, 2)
                nc.vector.tensor_copy(first[:, :], mask[:, 0, :]).then_inc(first_set, 1)
                dve.wait_ge(first_set, 1)

                def body(g, n0, i):
                    near = g == 2

                    def k_evac(n, j):
                        dve.wait_ge(tqk_done, LEAD + 2 * n + 2)
                        dve.wait_ge(qk_done, LEAD + 4 * n - 4 * (UNROLL - 2))
                        src = p_qk[:, :].rearrange("p (c k) -> p c k", c=4)
                        last = nc.vector.tensor_copy(kT[:, :, j + 1, :], src)
                        if j == UNROLL - 1:
                            last = nc.vector.tensor_copy(kT[:, :, 0, :], src)
                        last.then_inc(k_evacd, 1)

                    def mask_and_max(w):
                        j, c = divmod(w, 4)
                        dve.wait_ge(qk_done, LEAD + 4 * n0 + w + 1)
                        dve.wait_ge(exp_done, LEAD + 4 * n0 + w - 1)
                        if c == 0:
                            dve.wait_ge(stored[j], 4 * n0 + 16)
                        dve.sem_inc(turns, 1)
                        lo = P if near else 0
                        m = first[:, lo:] if j == 0 else mask[:, 1, lo:]
                        for h in range(2):
                            last = nc.vector.tensor_tensor_reduce(
                                out=sm[:, w % 2, h, lo:], in0=p_s[:, h, w % 2, lo:2 * P], in1=m, scale=HD ** -0.5,
                                scalar=LOWEST, op0=ALU.add, op1=ALU.max, accum_out=mx[:, w % 2, h:h + 1])
                        last.then_inc(masked, 1)
                        dve.wait_ge(masked, LEAD + 4 * n0 + w + 1)
                        nc.vector.tensor_scalar(og[:, j, CH + 2 * c:CH + 2 * c + 2], mx[:, w % 2, :], -1.0, None,
                                                ALU.mult).then_inc(maxed, 1)

                    k_evac(n0, 0)
                    N = 4 * UNROLL
                    for w in range(N + 2):
                        if w < N:
                            mask_and_max(w)
                        if w % 4 == 2 and w // 4 + 1 < UNROLL:
                            k_evac(n0 + w // 4 + 1, w // 4 + 1)
                        if 1 <= w <= N and (w - 1) % 2 == 1:
                            evac(dve, nc.vector.tensor_copy, n0, w - 1, pt_evacd_dve, near)
                        if w == 4 and g == 0:
                            nc.vector.tensor_copy(first[:, :], mask[:, 1, :])

                loops(dve, body)


GH, GK, GV_W = 4, 64, 128
CHUNK = 64
TAU = 16.0


def log_gates(nc, act, dve, z, e, done, z_ready, base=0):
    if dve is not None:
        nc.vector.scalar_tensor_tensor(out=e, in0=z, scalar=-1.0, in1=z, op0=ALU.mult, op1=ALU.min
                                       ).then_inc(done, 1)
        dve.wait_ge(done, base + 3)
        nc.vector.scalar_tensor_tensor(out=z, in0=z, scalar=0.0, in1=e, op0=ALU.min,
                                       op1=ALU.subtract).then_inc(done, 1)
        dve.wait_ge(done, base + 4)
    if act is not None:
        act.wait_ge(done, base + 1)
        nc.scalar.activation(e, e, ACT.Exp).then_inc(done, 1)
        act.wait_ge(done, base + 2)
        nc.scalar.activation(e, e, ACT.Ln, bias=1.0).then_inc(done, 1)


def gla_prompt(nc, A, S, O, ident):
    TMs, FMs, GLs, OL = S["tm"], S["fm"], S["gl"], S["ol"]
    NP = GH // 2
    st, sb, pb, sem = scope(nc)
    with st:
        wa = sb("d_wa", [RANK, GH * GK])
        ba = sb("d_ba", [P, NP])
        glr = sb("d_glr", [RANK, SEQ])
        z = sb("d_z", [P, NP, SEQ])
        e = sb("d_e", [P, NP, SEQ])
        keep = sb("d_keep", [P, NP, SEQ])
        b = sb("d_b", [P, NP, SEQ])
        eb = sb("d_eb", [P, NP, SEQ])
        enb = sb("d_enb", [P, NP, SEQ])
        ed = sb("d_ed", [P, NP, SEQ])
        decay = sb("d_decay", [P, NP, SEQ // CHUNK])
        qk = sb("d_qk", [P, 2, 2, NP, P])
        v = sb("d_v", [P, 2, GH * GV_W])
        qe = sb("d_qe", [P, 2, NP, P])
        ke = sb("d_ke", [P, 2, NP, P])
        kd = sb("d_kd", [P, 2, NP, P])
        kdT = sb("d_kdT", [P, 2, NP, P])
        att = sb("d_att", [P, 2, 2, NP, P])
        state = sb("d_state", [P, NP, 2 * GV_W])
        out = sb("d_out", [P, 2, GH * GV_W])
        cmask = sb("d_cmask", [P, P], U32)
        p_kd = pb("d_p_kd", [P, NP, P])
        p_att = pb("d_p_att", [P, 2, CH])
        p_o = pb("d_p_o", [P, 2, GH * GV_W])
        p_u = pb("d_p_u", [P, NP, 2 * GV_W])
        const_in = sem("d_const_in")
        qk_in = [sem("d_qk_in0"), sem("d_qk_in1")]
        v_in = [sem("d_v_in0"), sem("d_v_in1")]
        stored = [sem("d_stored0"), sem("d_stored1")]
        state_out = sem("d_state_out")
        cleared = sem("d_cleared")
        gate_mm = sem("d_gate_mm")
        gate_z = sem("d_gate_z")
        gate = sem("d_gate")
        summed = sem("d_summed")
        e_ready = sem("d_e_ready")
        scaled = sem("d_scaled")
        turns = sem("d_turns")
        kd_done = sem("d_kd_done")
        kd_evacd = sem("d_kd_evacd")
        att_done = sem("d_att_done")
        att_masked = sem("d_att_masked")
        o_done = sem("d_o_done")
        o_evacd = sem("d_o_evacd")
        u_done = sem("d_u_done")
        st_done = sem("d_st_done")

        with nc.Block() as block:

            @block.sync
            def _(sp):
                for dst, src in ((glr, GLs), (wa, A["w_gla_a2"].rearrange("a r k -> (a r) k")), (ba, A["b_gla_a"]),
                                 (cmask, A["chunk_mask"])):
                    sp.dma_start(dst[:, :], src).then_inc(const_in, 16)
                for s in range(2):
                    sp.sem_inc(stored[s], 16)
                with sp.Fori(0, NT // 2) as i:
                    for s in range(2):
                        n = 2 * i + s
                        sp.wait_ge(scaled, LEAD + n - 1)
                        for a, row in ((0, FM_GQ), (1, FM_GK)):
                            sp.dma_start(qk[:, s, a, :, :], FMs[row:row + NP * P, :].rearrange(
                                "(a p) t -> p a t", p=P)[:, :, ds(n * P, P)]).then_inc(qk_in[s], 16)
                        sp.wait_ge(o_done, LEAD + n - 1)
                        sp.dma_start(v[:, s, :], TMs[ds(n * P, P), TM_GV * CH:(TM_GV + 1) * CH]).then_inc(v_in[s], 16)
                sp.wait_ge(st_done, LEAD + 2 * NT)
                for h in range(GH):
                    r = slice(GK * (h % 2), GK * (h % 2) + GK)
                    sp.dma_start(O["gla_prompt"][0, 0, h], state[r, h // 2, GV_W * (h % 2):GV_W * (h % 2) + GV_W]
                                 ).then_inc(state_out, 16)
                sp.wait_ge(state_out, 16 * GH)
                for s in range(2):
                    sp.wait_ge(stored[s], 16 + 16 * NT // 2)

            @block.gpsimd
            def _(pool):
                nc.gpsimd.memset(keep[:, :, :], 1.0).then_inc(cleared, 1)
                pool.wait_ge(cleared, 1)
                nc.gpsimd.memset(keep[:, :, :].rearrange("p a (c t) -> p (a c) t", t=CHUNK)[:, :, 0:1], 0.0
                                 ).then_inc(cleared, 1)
                nc.gpsimd.memset(att[:, :, :, :, :], 0.0).then_inc(cleared, 1)
                nc.gpsimd.memset(state[:, :, :], 0.0).then_inc(cleared, 1)

            @block.tensor
            def _(pe):
                for s in (kd_done, att_done, o_done, u_done):
                    pe.sem_inc(s, LEAD)
                pe.wait_ge(const_in, 64)
                for a in range(NP):
                    for c in range(SEQ // CH):
                        k = (SEQ // CH) * a + c
                        if k >= 2:
                            pe.wait_ge(gate_z, k - 1)
                        nc.tensor.matmul(p_o[:, k % 2, :], wa[:, a * P:(a + 1) * P], glr[:, c * CH:(c + 1) * CH],
                                         start=True, stop=True).then_inc(gate_mm, 1)
                pe.wait_ge(gate_z, NP * SEQ // CH)
                pe.wait_ge(cleared, 4)
                with pe.Fori(0, NT // 2) as i:
                    for s in range(2):
                        n = 2 * i + s
                        pe.wait_ge(scaled, LEAD + n + 1)
                        pe.wait_ge(kd_evacd, LEAD + n)
                        for a in range(NP):
                            last = nc.tensor.transpose(p_kd[:, a, :], kd[:, s, a, :], ident[:, :])
                        last.then_inc(kd_done, 1)
                        pe.wait_ge(att_masked, LEAD + n)
                        for a in range(NP):
                            for h in range(2):
                                r = slice(GK * h, GK * h + GK)
                                last = nc.tensor.matmul(p_att[:, h, a * P:(a + 1) * P], ke[r, s, a, :], qe[r, s, a, :],
                                                        start=True, stop=True)
                        last.then_inc(att_done, 1)
                        pe.wait_ge(v_in[s], 16 * i + 16)
                        pe.wait_ge(o_evacd, LEAD + n - 1)
                        pe.wait_ge(kd_evacd, LEAD + n + 1)
                        for c in range(2):
                            t = slice(CHUNK * c, CHUNK * c + CHUNK)
                            pe.wait_ge(st_done, LEAD + 2 * n + c)
                            for a in range(NP):
                                cols = slice(2 * GV_W * a, 2 * GV_W * (a + 1))
                                nc.tensor.matmul(p_o[t, s, cols], qe[:, s, a, t], state[:, a, :], start=(a == 0),
                                                 stop=False)
                            for a in range(NP):
                                cols = slice(2 * GV_W * a, 2 * GV_W * (a + 1))
                                last = nc.tensor.matmul(p_u[:, a, :], kdT[t, s, a, :], v[t, s, cols], start=True,
                                                        stop=True)
                            last.then_inc(u_done, 1)
                        pe.wait_ge(att_masked, LEAD + n + 1)
                        for h in range(GH):
                            cols = slice(GV_W * h, GV_W * (h + 1))
                            last = nc.tensor.matmul(p_o[:, s, cols], att[:, s, h % 2, h // 2, :], v[:, s, cols],
                                                    start=False, stop=(h == GH - 1))
                        last.then_inc(o_done, 1)

            @block.scalar
            def _(act):
                for s in (kd_evacd, o_evacd):
                    act.sem_inc(s, LEAD)
                log_gates(nc, act, None, z[:, :, :], e[:, :, :], gate, None)
                act.wait_ge(summed, 1)
                nc.scalar.activation(eb[:, :, :], b[:, :, :], ACT.Exp, scale=1.0 / TAU).then_inc(e_ready, 1)
                nc.scalar.activation(enb[:, :, :], b[:, :, :], ACT.Exp, scale=-1.0 / TAU).then_inc(e_ready, 1)
                ends = b[:, :, :].rearrange("p a (c t) -> p a c t", t=CHUNK)[:, :, :, CHUNK - 1]
                nc.scalar.activation(decay[:, :, :], ends, ACT.Exp, scale=1.0 / TAU).then_inc(e_ready, 1)
                act.wait_ge(summed, 2)
                nc.scalar.activation(ed[:, :, :], e[:, :, :], ACT.Exp, scale=-1.0 / TAU).then_inc(e_ready, 1)

                with act.Fori(0, NT // 2) as i:
                    for s in range(2):
                        n = 2 * i + s
                        act.wait_ge(kd_done, LEAD + n + 1)
                        act.wait_ge(u_done, LEAD + 2 * (n - 1))
                        nc.scalar.copy(kdT[:, s, :, :], p_kd[:, :, :]).then_inc(kd_evacd, 1)
                        act.wait_ge(o_done, LEAD + n + 1)
                        act.wait_ge(stored[s], 16 * i + 16)
                        nc.scalar.copy(out[:, s, :], p_o[:, s, :]).then_inc(o_evacd, 1)
                        act.wait_ge(o_evacd, LEAD + n + 1)
                        act.dma_start(OL[ds(n * P, P), :], out[:, s, :]).then_inc(stored[s], 16)

            @block.vector
            def _(dve):
                for s in (scaled, att_masked, st_done):
                    dve.sem_inc(s, LEAD)
                for k in range(NP * SEQ // CH):
                    a, c = divmod(k, SEQ // CH)
                    dve.wait_ge(gate_mm, k + 1)
                    nc.vector.tensor_scalar(z[:, a, c * CH:(c + 1) * CH], p_o[:, k % 2, :], ba[:, a:a + 1], None,
                                            ALU.add).then_inc(gate_z, 1)
                dve.wait_ge(gate_z, NP * SEQ // CH)
                log_gates(nc, None, dve, z[:, :, :], e[:, :, :], gate, None)
                dve.wait_ge(cleared, 4)
                flat = lambda x: x[:, :, :].rearrange("p a t -> p (a t)")
                nc.vector.tensor_tensor_scan(flat(b), flat(keep), flat(z), 0.0, ALU.mult, ALU.add).then_inc(summed, 1)
                dve.wait_ge(summed, 1)
                chunks = lambda x: x[:, :, :].rearrange("p a (c t) -> p (a c) t", t=CHUNK)
                nc.vector.tensor_tensor(chunks(e), chunks(b), chunks(b)[:, :, CHUNK - 1:CHUNK].to_broadcast(
                    [P, NP * SEQ // CHUNK, CHUNK]), ALU.subtract).then_inc(summed, 1)
                dve.wait_ge(e_ready, 4)
                with dve.Fori(0, NT // 2) as i:
                    for s in range(2):
                        n = 2 * i + s
                        dve.wait_ge(qk_in[s], 32 * i + 32)
                        dve.wait_ge(o_done, LEAD + n - 1)
                        t = ds(n * P, P)
                        nc.vector.scalar_tensor_tensor(out=qe[:, s, :, :], in0=qk[:, s, 0, :, :], scalar=GK ** -0.5,
                                                       in1=eb[:, :, t], op0=ALU.mult, op1=ALU.mult)
                        nc.vector.tensor_tensor(ke[:, s, :, :], qk[:, s, 1, :, :], enb[:, :, t], ALU.mult)
                        nc.vector.tensor_tensor(kd[:, s, :, :], qk[:, s, 1, :, :], ed[:, :, t],
                                                ALU.mult).then_inc(scaled, 1)
                        dve.wait_ge(att_done, LEAD + n + 1)
                        dve.sem_inc(turns, 1)
                        for h in range(2):
                            last = nc.vector.copy_predicated(
                                att[:, s, h, :, :], cmask[:, :].unsqueeze(1).to_broadcast([P, NP, P]),
                                p_att[:, h, 0:NP * P].rearrange("p (a t) -> p a t", a=NP))
                        last.then_inc(att_masked, 1)
                        for c in range(2):
                            dve.wait_ge(u_done, LEAD + 2 * n + c + 1)
                            for h in range(GH):
                                a, r = h // 2, slice(GK * (h % 2), GK * (h % 2) + GK)
                                cols = slice(GV_W * (h % 2), GV_W * (h % 2) + GV_W)
                                last = nc.vector.scalar_tensor_tensor(
                                    out=state[r, a, cols], in0=state[r, a, cols], scalar=decay[r, a, ds(2 * n + c, 1)],
                                    in1=p_u[r, a, cols], op0=ALU.mult, op1=ALU.add)
                            last.then_inc(st_done, 1)
                            dve.wait_ge(st_done, LEAD + 2 * n + c + 1)


class Chain:

    def __init__(self, eng, done, at):
        self.eng, self.done, self.at, self.links = eng, done, at, 0

    def __call__(self, instruction):
        instruction.then_inc(self.done, 1)
        self.links += 1
        self.eng.wait_ge(self.done, self.at + self.links)


def merge(nc, A, S, O, ident):
    TMs, OG, OL = S["tm"], S["og"], S["ol"]
    TILES = NT + 1
    G4 = D // 2 // P
    st, sb, pb, sem = scope(nc)
    with st:
        wb_hi = sb("f_wb_hi", [P, 2, G4, D], F32R)
        wb_lo = sb("f_wb_lo", [P, 2, G4, D], F32R)
        wo_hi = sb("f_wo_hi", [P, KC, D], F32R)
        wo_lo = sb("f_wo_lo", [P, KC, D], F32R)
        gates = sb("f_gates", [P, 2, 6 * CH])
        og = sb("f_og", [P, 3, OG_W])
        ol = sb("f_ol", [P, CH])
        x = sb("f_x", [P, 2, D])
        sg = sb("f_sg", [P, 2 * CH])
        bT_hi = sb("f_bT_hi", [P, 2, G4, P], F32R)
        bT_lo = sb("f_bT_lo", [P, 2, G4, P], F32R)
        mT_hi = sb("f_mT_hi", [P, KC, P], F32R)
        mT_lo = sb("f_mT_lo", [P, KC, P], F32R)
        y = sb("f_y", [P, D])
        fw = sb("f_fw", [P, D])
        gw = sb("f_gw", [P, 1])
        junk = sb("f_junk", [P, GV_W])
        low = sb("f_low", [P, NH])
        wg = sb("f_wg", [P, 3, NH])
        wd = sb("f_wd", [P, 3, NH])
        den = sb("f_den", [P, 2, NH])
        gn = sb("f_gn", [P, 6, GH])
        fn = sb("f_fn", [P, 6])
        p_t = pb("f_p_t", [P, 2, CH])
        p_b = pb("f_p_b", [P, 2, D])
        p_z = pb("f_p_z", [P, D])

        const_in = sem("f_const_in")
        raw_in = [sem("f_raw_in0"), sem("f_raw_in1")]
        w_hi_done = sem("f_w_hi_done")
        w_lo_done = sem("f_w_lo_done")
        gw_done = sem("f_gw_done")
        gates_in = [sem("f_gates_in0"), sem("f_gates_in1")]
        x_in = [sem("f_x_in0"), sem("f_x_in1")]
        og_in = sem("f_og_in")
        ol_in = sem("f_ol_in")
        stored = sem("f_stored")
        sig_done = sem("f_sig_done")
        diff_done = sem("f_diff_done")
        wexp_done = sem("f_wexp_done")
        gms_done = sem("f_gms_done")
        groot_done = sem("f_groot_done")
        branches = sem("f_branches")
        prep = sem("f_prep")
        t1_done = sem("f_t1_done")
        hi1_done = sem("f_hi1_done")
        lo1_done = sem("f_lo1_done")
        g1_done = sem("f_g1_done")
        mixing = sem("f_mixing")
        silu_done = sem("f_silu_done")
        turns = sem("f_turns")
        mixed = sem("f_mixed")
        t2_done = sem("f_t2_done")
        hi2_done = sem("f_hi2_done")
        lo2_done = sem("f_lo2_done")
        g2_done = sem("f_g2_done")
        y_done = sem("f_y_done")
        sq_done = sem("f_sq_done")
        fms_done = sem("f_fms_done")
        froot_done = sem("f_froot_done")
        fin = sem("f_fin")
        y_ready = sem("f_y_ready")
        L = LEAD
        PREP, FIN = 17, 4

        def rows(t):
            return slice(SEQ - NS, TOK) if isinstance(t, int) and t == NT else ds(t * P, P)

        def has(t):
            return not isinstance(t, int) or 0 <= t < TILES

        pieces = [("b", a, c) for a in range(2) for c in range(0, G4, 2)] + [("o", 0, c) for c in range(0, KC, 2)]

        def piece(n):
            kind, a, c = pieces[n]
            raw = gates[:, n % 2, 0:2 * D].rearrange("p (c e) -> p c e", c=2)
            if kind == "b":
                return raw, wb_hi[:, a, c:c + 2, :], wb_lo[:, a, c:c + 2, :], \
                    A["w_attn_out" if a == 0 else "w_gla_out"], c
            return raw, wo_hi[:, c:c + 2, :], wo_lo[:, c:c + 2, :], A["w_out"], c

        with nc.Block() as block:

            @block.sync
            def _(sp):
                sp.dma_start(fw[:, :], A["final_norm_w"].rearrange("(a d) -> a d", a=1).to_broadcast([P, D])
                             ).then_inc(const_in, 16)
                sp.dma_start(gw[:, :], A["gla_norm_w"].rearrange("a (p b) -> p (a b)", b=1)).then_inc(const_in, 16)
                for n in range(len(pieces)):
                    raw, _, _, src, c = piece(n)
                    if n >= 2:
                        sp.wait_ge(w_lo_done, n - 1)
                    sp.dma_start(raw, src.rearrange("a (c p) e -> p (a c) e", p=P)[:, c:c + 2, :]
                                 ).then_inc(raw_in[n % 2], 16)

                def load(t, s):
                    sp.wait_ge(t2_done, L + t - 1)
                    sp.dma_start(gates[:, s, :], TMs[rows(t), TM_AZ * CH:]).then_inc(gates_in[s], 16)
                    sp.wait_ge(branches, L + t)
                    sp.dma_start(og[:, :, :], OG[rows(t), :, :]).then_inc(og_in, 16)
                    sp.dma_start(ol[:, :], OL[rows(t), :]).then_inc(ol_in, 16)

                def load_x(t, s):
                    sp.wait_ge(sq_done, L + t - 1)
                    if isinstance(t, int) and t == NT:
                        sp.dma_start(x[0:NS, s, :], A["x_prompt"][0, SEQ - NS:SEQ, :]).then_inc(x_in[s], 16)
                        sp.dma_start(x[NS:P, s, :], A["x_sample"].rearrange("b t d -> (b t) d")).then_inc(x_in[s], 16)
                    else:
                        sp.dma_start(x[:, s, :], A["x_prompt"][0, rows(t), :]).then_inc(x_in[s], 16)

                sp.wait_ge(w_lo_done, len(pieces))
                load(0, 0)
                load(1, 1)
                load_x(0, 0)

                def step(t, s):
                    if has(t + 2):
                        load(t + 2, s)
                    if has(t + 1):
                        load_x(t + 1, 1 - s)

                step(0, 0)
                with sp.Fori(0, (TILES - 5) // 2) as i:
                    step(2 * i + 1, 1)
                    step(2 * i + 2, 0)
                for t in range(TILES - 4, TILES):
                    step(t, t % 2)
                sp.wait_ge(stored, 16 + 16 * TILES)

            @block.tensor
            def _(pe):
                for s in (t1_done, g1_done, t2_done, g2_done):
                    pe.sem_inc(s, L)

                def transpose_branches(t, s):
                    pe.wait_ge(branches, L + t + 1)
                    for a in range(2):
                        if a == 0:
                            pe.wait_ge(lo2_done, L + t - 1)
                        for c in range(G4):
                            last = nc.tensor.transpose(p_t[:, a, c * P:(c + 1) * P],
                                                       gates[:, s, (G4 * a + c) * P:(G4 * a + c + 1) * P], ident[:, :])
                    last.then_inc(t1_done, 1)

                def product(out, stat_hi, stat_lo, mov_hi, mov_lo, first, last):
                    nc.tensor.matmul(out, stat_hi, mov_hi, start=first, stop=False)
                    nc.tensor.matmul(out, stat_hi, mov_lo, start=False, stop=False)
                    return nc.tensor.matmul(out, stat_lo, mov_hi, start=False, stop=last)

                def step(t, s):
                    if isinstance(t, int) and t == 0:
                        pe.wait_ge(w_lo_done, len(pieces))
                        transpose_branches(0, 0)
                    pe.wait_ge(lo1_done, L + t + 1)
                    pe.wait_ge(mixed, L + t)
                    for a in range(2):
                        for e in range(0, D, CH):
                            for c in range(G4):
                                last = product(p_b[:, a, e:e + CH], bT_hi[:, a, c, :], bT_lo[:, a, c, :],
                                               wb_hi[:, a, c, e:e + CH], wb_lo[:, a, c, e:e + CH], c == 0, c == G4 - 1)
                    last.then_inc(g1_done, 1)
                    if has(t + 1):
                        transpose_branches(t + 1, 1 - s)
                    if has(t - 1):
                        out_product(t - 1)
                    pe.wait_ge(mixed, L + t + 1)
                    if has(t + 1):
                        pe.wait_ge(lo1_done, L + t + 2)
                    for c in range(KC):
                        last = nc.tensor.transpose(p_t[:, c // 4, (c % 4) * P:(c % 4 + 1) * P],
                                                   gates[:, s, 2 * CH + c * P:2 * CH + (c + 1) * P], ident[:, :])
                    last.then_inc(t2_done, 1)
                    if isinstance(t, int) and t == TILES - 1:
                        out_product(t)

                def out_product(t):
                    pe.wait_ge(lo2_done, L + t + 1)
                    pe.wait_ge(y_done, L + t)
                    for e in range(0, D, CH):
                        for c in range(KC):
                            last = product(p_z[:, e:e + CH], mT_hi[:, c, :], mT_lo[:, c, :],
                                           wo_hi[:, c, e:e + CH], wo_lo[:, c, e:e + CH], c == 0, c == KC - 1)
                    last.then_inc(g2_done, 1)

                step(0, 0)
                with pe.Fori(0, (TILES - 3) // 2) as i:
                    step(2 * i + 1, 1)
                    step(2 * i + 2, 0)
                step(TILES - 2, 1)
                step(TILES - 1, 0)

            @block.scalar
            def _(act):
                for s in (sig_done, wexp_done, groot_done, hi1_done, hi2_done, sq_done, froot_done):
                    act.sem_inc(s, L)
                act.sem_inc(stored, 16)
                for n in range(len(pieces)):
                    raw, hi, _, _, _ = piece(n)
                    if pieces[n][:2] == ("b", 1):
                        act.wait_ge(gw_done, n - 1)
                    else:
                        act.wait_ge(raw_in[n % 2], 16 * (n // 2) + 16)
                    nc.scalar.copy(hi, raw).then_inc(w_hi_done, 1)

                def prepare(t, s):
                    act.wait_ge(gates_in[s], 8 * (t - s) + 16)
                    act.wait_ge(branches, L + t)
                    nc.scalar.activation(sg[:, :], gates[:, s, 0:2 * CH], ACT.Sigmoid)
                    nc.scalar.activation(gates[:, s, 2 * CH:], gates[:, s, 2 * CH:], ACT.Sigmoid).then_inc(sig_done, 1)
                    act.wait_ge(diff_done, L + t + 1)
                    nc.scalar.activation(wg[:, :, :], wd[:, :, :], ACT.Exp).then_inc(wexp_done, 1)
                    act.wait_ge(gms_done, L + t + 1)
                    nc.scalar.activation(gn[:, 2, :], gn[:, 1, :], ACT.Sqrt).then_inc(groot_done, 1)

                def split_hi1(t):
                    act.wait_ge(t1_done, L + t + 1)
                    nc.scalar.copy(bT_hi[:, :, :, :], p_t[:, :, :]).then_inc(hi1_done, 1)

                def final(t, s):
                    act.wait_ge(y_done, L + t + 1)
                    nc.scalar.activation(x[:, s, :], y[:, :], ACT.Square, accum_out=fn[:, 0:1]).then_inc(sq_done, 1)
                    act.wait_ge(fms_done, L + t + 1)
                    nc.scalar.activation(fn[:, 2:3], fn[:, 1:2], ACT.Sqrt).then_inc(froot_done, 1)
                    act.wait_ge(y_ready, L + t + 1)
                    if isinstance(t, int) and t == NT:
                        act.dma_start(O["y_sample"].rearrange("b t d -> (b t) d"), y[NS:P, :]).then_inc(stored, 16)
                    else:
                        act.dma_start(O["y_prompt"][0, rows(t), :], y[:, :]).then_inc(stored, 16)

                def step(t, s):
                    if isinstance(t, int) and t == 0:
                        prepare(0, 0)
                        split_hi1(0)
                        prepare(1, 1)
                    if has(t + 1):
                        split_hi1(t + 1)
                    if has(t - 1):
                        final(t - 1, 1 - s)
                    act.wait_ge(t2_done, L + t + 1)
                    nc.scalar.copy(mT_hi[:, :, :], p_t[:, :, :]).then_inc(hi2_done, 1)
                    if has(t + 2):
                        prepare(t + 2, s)
                    if isinstance(t, int) and t == TILES - 1:
                        final(t, s)

                step(0, 0)
                with act.Fori(0, (TILES - 5) // 2) as i:
                    step(2 * i + 1, 1)
                    step(2 * i + 2, 0)
                for t in range(TILES - 4, TILES):
                    step(t, t % 2)

            @block.vector
            def _(dve):
                for s in (diff_done, gms_done, branches, lo1_done, mixed, lo2_done, y_done, fms_done, y_ready):
                    dve.sem_inc(s, L)
                dve.wait_ge(const_in, 32)
                for n in range(len(pieces)):
                    raw, hi, lo, _, _ = piece(n)
                    if pieces[n][:2] == ("b", 1):
                        dve.wait_ge(raw_in[n % 2], 16 * (n // 2) + 16)
                        nc.vector.tensor_scalar(raw, raw, gw[:, 0:1], None, ALU.mult).then_inc(gw_done, 1)
                    dve.wait_ge(w_hi_done, n + 1)
                    nc.vector.tensor_tensor(lo, raw, hi.bitcast(F32), ALU.subtract).then_inc(w_lo_done, 1)
                V = nc.vector

                def prepare(t, s):
                    link = Chain(dve, prep, PREP * t)
                    dve.wait_ge(og_in, 16 * t + 16)
                    nm, dn = og[:, :, CH:CH + NH], og[:, :, CH + NH:]
                    link(V.tensor_tensor(low[:, :], nm[:, 0, :], nm[:, 1, :], ALU.min))
                    link(V.tensor_tensor(low[:, :], low[:, :], nm[:, 2, :], ALU.min))
                    V.tensor_tensor(wd[:, :, :], low[:, :].unsqueeze(1).to_broadcast([P, 3, NH]), nm,
                                    ALU.subtract).then_inc(diff_done, 1)
                    dve.wait_ge(ol_in, 16 * t + 16)
                    for h in range(GH):
                        cols = slice(h * GV_W, (h + 1) * GV_W)
                        dve.sem_inc(turns, 1)
                        last = V.tensor_tensor_reduce(out=junk[:, :], in0=ol[:, cols], in1=ol[:, cols], scale=1.0,
                                                      scalar=0.0, op0=ALU.mult, op1=ALU.add, accum_out=gn[:, 0, h:h + 1])
                        link(last)
                    V.tensor_scalar(gn[:, 1, :], gn[:, 0, :], 1.0 / GV_W, EPS, ALU.mult, ALU.add).then_inc(gms_done, 1)
                    dve.wait_ge(wexp_done, L + t + 1)
                    link(V.tensor_tensor(wd[:, :, :], wg[:, :, :], dn, ALU.mult))
                    link(V.tensor_tensor(den[:, 0, :], wd[:, 0, :], wd[:, 1, :], ALU.add))
                    link(V.tensor_tensor(den[:, 0, :], den[:, 0, :], wd[:, 2, :], ALU.add))
                    link(V.reciprocal(den[:, 1, :], den[:, 0, :]))
                    link(V.tensor_tensor(wg[:, :, :], wg[:, :, :], den[:, 1:2, :].to_broadcast([P, 3, NH]), ALU.mult))
                    sums = og[:, :, 0:CH].rearrange("p g (h e) -> p g h e", h=NH)
                    link(V.tensor_tensor(sums, sums, wg[:, :, :].unsqueeze(3).to_broadcast([P, 3, NH, HD]), ALU.mult))
                    V.tensor_tensor(og[:, 0, 0:CH], og[:, 0, 0:CH], og[:, 1, 0:CH], ALU.add)
                    dve.wait_ge(groot_done, L + t + 1)
                    link(V.reciprocal(gn[:, 3, :], gn[:, 2, :]))
                    V.tensor_tensor(og[:, 0, 0:CH], og[:, 0, 0:CH], og[:, 2, 0:CH], ALU.add)
                    link(V.tensor_tensor(gn[:, 4, :], gn[:, 3, :], gn[:, 3, :], ALU.mult))
                    link(V.tensor_tensor(gn[:, 4, :], gn[:, 4, :], gn[:, 1, :], ALU.mult))
                    link(V.tensor_scalar(gn[:, 4, :], gn[:, 4, :], -0.5, 1.5, ALU.mult, ALU.add))
                    link(V.tensor_tensor(gn[:, 5, :], gn[:, 3, :], gn[:, 4, :], ALU.mult))
                    heads = ol[:, :].rearrange("p (h e) -> p h e", h=GH)
                    V.tensor_tensor(heads, heads, gn[:, 5, :].unsqueeze(2).to_broadcast([P, GH, GV_W]), ALU.mult)
                    dve.wait_ge(sig_done, L + t + 1)
                    link2 = V.tensor_tensor(gates[:, s, 0:2 * CH], gates[:, s, 0:2 * CH], sg[:, :], ALU.mult)
                    link2.then_inc(silu_done, 1)
                    dve.wait_ge(silu_done, t + 1)
                    V.tensor_tensor(gates[:, s, 0:CH], gates[:, s, 0:CH], og[:, 0, 0:CH], ALU.mult)
                    V.tensor_tensor(gates[:, s, CH:2 * CH], gates[:, s, CH:2 * CH], ol[:, :],
                                    ALU.mult).then_inc(branches, 1)
                    assert link.links == PREP, link.links

                def split_lo1(t):
                    dve.wait_ge(hi1_done, L + t + 1)
                    V.tensor_tensor(bT_lo[:, :, :, :], p_t[:, :, :].rearrange("p a (c t) -> p a c t", c=G4),
                                    bT_hi[:, :, :, :].bitcast(F32), ALU.subtract).then_inc(lo1_done, 1)

                def mix(t, s):
                    dve.wait_ge(g1_done, L + t + 1)
                    m = gates[:, s, 2 * CH:].rearrange("p (a e) -> p a e", a=2)
                    V.tensor_tensor(m, m, p_b[:, :, :], ALU.mult).then_inc(mixing, 1)
                    dve.wait_ge(mixing, t + 1)
                    V.tensor_tensor(m[:, 0, :], m[:, 0, :], m[:, 1, :], ALU.add).then_inc(mixed, 1)

                def final(t, s):
                    link = Chain(dve, fin, FIN * t)
                    dve.wait_ge(g2_done, L + t + 1)
                    dve.wait_ge(x_in[s], 8 * (t - s) + (32 if isinstance(t, int) and t == NT else 16))
                    dve.wait_ge(stored, 16 * t + 16)
                    V.tensor_tensor(y[:, :], x[:, s, :], p_z[:, :], ALU.add).then_inc(y_done, 1)
                    dve.wait_ge(sq_done, L + t + 1)
                    m = [fn[:, j:j + 1] for j in range(6)]
                    V.tensor_scalar(m[1], m[0], 1.0 / D, EPS, ALU.mult, ALU.add).then_inc(fms_done, 1)
                    dve.wait_ge(froot_done, L + t + 1)
                    rsqrt_steps(nc, dve, fin, FIN * t, m)
                    V.scalar_tensor_tensor(out=y[:, :], in0=y[:, :], scalar=m[2], in1=fw[:, :], op0=ALU.mult,
                                           op1=ALU.mult).then_inc(y_ready, 1)

                def step(t, s):
                    if isinstance(t, int) and t == 0:
                        prepare(0, 0)
                        split_lo1(0)
                        prepare(1, 1)
                    mix(t, s)
                    if has(t + 1):
                        split_lo1(t + 1)
                    if has(t - 1):
                        final(t - 1, 1 - s)
                    dve.wait_ge(hi2_done, L + t + 1)
                    V.tensor_tensor(mT_lo[:, :, :], p_t[:, :, :].rearrange("p a (c t) -> p (a c) t", c=4),
                                    mT_hi[:, :, :].bitcast(F32), ALU.subtract).then_inc(lo2_done, 1)
                    if has(t + 2):
                        prepare(t + 2, s)
                    if isinstance(t, int) and t == TILES - 1:
                        final(t, s)

                step(0, 0)
                with dve.Fori(0, (TILES - 5) // 2) as i:
                    step(2 * i + 1, 1)
                    step(2 * i + 2, 0)
                for t in range(TILES - 4, TILES):
                    step(t, t % 2)


ROWS = 2 * T * NH
UNITS = (1, 4, 8)
UNIT0 = (0, 1, 5)
NU = 13


def attend_sample(nc, A, S, ident):
    TMs, OG, OA = S["tm"], S["og"], S["oa"]
    TS = TMs[SEQ:TOK, :]
    caches = (A["cache_kv_w128"], A["cache_kv_w512"], A["cache_kv_w2048"])
    NB = DB // 2
    st, sb, pb, sem = scope(nc)
    with st:
        kc = sb("e_kc", [P, 2, NU, CH])
        vc = sb("e_vc", [P, 2, NU, CH])
        vn = sb("e_vn", [2 * T, 3, CH])
        kn = sb("e_kn", [NS, 3, CH])
        qb = sb("e_qb", [P, 2, T, CH])
        sT = sb("e_sT", [P, 3, ROWS])
        sn = sb("e_sn", [NS, 3, 2, T * NH])
        snT = sb("e_snT", [P, 3, NS])
        sn2 = sb("e_sn2", [P, 3, T])
        s = sb("e_s", [P, 3, P + T])
        mask = sb("e_mask", [P, 3, P + T])
        diag = sb("e_diag", [P, CH])
        mx = sb("e_mx", [P, 2, 3])
        nm = sb("e_nm", [P, 3])
        dn = sb("e_dn", [P, 3])
        lw = sb("e_lw", [P, 1])
        wg = sb("e_wg", [P, 3])
        wd = sb("e_wd", [P, 3])
        ds_ = sb("e_ds", [P, 2])
        pn = sb("e_pn", [P, 3, 2 * T])
        pnT = sb("e_pnT", [2 * T, 3, P])
        pm0 = sb("e_pm0", [P, ROWS])
        pm1 = sb("e_pm1", [P, 2, 4 * 72])
        pm2 = sb("e_pm2", [P, 2, 8 * 72])
        po = sb("e_po", [P, 3, CH])
        oa = sb("e_oa", [P, 2, HD])
        fill = sb("e_fill", [NS, 3, OG_W])
        p_s = pb("e_p_s", [P, 3, P])
        p_sn = pb("e_p_sn", [P, 3, NS])
        p_p = pb("e_p_p", [P, 3, P])
        p_pn = pb("e_p_pn", [2 * T, 3, P])
        p_o = pb("e_p_o", [P, 3, CH])

        const_in = sem("e_const_in")
        kn_in = sem("e_kn_in")
        qn_in = [sem("e_qn_in0"), sem("e_qn_in1")]
        qb_in = [sem("e_qb_in0"), sem("e_qb_in1")]
        k_in = [sem("e_k_in0"), sem("e_k_in1")]
        v_in = sem("e_v_in")
        stored = sem("e_stored")
        filled = sem("e_filled")
        cleared = sem("e_cleared")
        turns = sem("e_turns")
        chain = sem("e_chain")
        sn_done = sem("e_sn_done")
        snT_done = sem("e_snT_done")
        scored = sem("e_scored")
        sT_done = sem("e_sT_done")
        maxed = sem("e_maxed")
        exp_done = sem("e_exp_done")
        wexp_done = sem("e_wexp_done")
        p_ready = sem("e_p_ready")
        pT_done = sem("e_pT_done")
        pm_done = sem("e_pm_done")
        pv_done = sem("e_pv_done")
        lowest = sem("e_lowest")
        out_ready = sem("e_out_ready")
        L = LEAD
        LINKS = 18

        def cached(g, b, kv):
            dil, _ = GROUPS[g]
            src = caches[g][0, ds(b, 1), :, kv, :, :].rearrange("b (l r) h e -> l (b r) (h e)", r=dil)
            return src[:, 0:UNITS[g], :]

        with nc.Block() as block:

            @block.sync
            def _(sp):
                sp.dma_start(mask[:, :, :], A["dec_mask"]).then_inc(const_in, 16)
                sp.dma_start(diag[:, :], A["dec_diag"]).then_inc(const_in, 16)
                sp.dma_start(kn[:, :, :], TS[:, 3 * CH:6 * CH]).then_inc(kn_in, 16)
                for g in range(3):
                    if g == 2:
                        sp.wait_ge(sn_done, 1)
                    for b in range(DB):
                        src = TS[T * b:T * b + T, g * CH:(g + 1) * CH]
                        sp.dma_start(qb[T * b:T * b + T, g % 2, :, :], src.unsqueeze(0).to_broadcast([T, T, CH])
                                     ).then_inc(qn_in[g % 2], 16)
                sp.wait_ge(cleared, 6)
                sp.dma_start(OG[SEQ:TOK, :, :], fill[:, :, :]).then_inc(filled, 16)
                with sp.Fori(0, NB) as i:
                    for b in range(2):
                        for g in range(3):
                            k = 3 * b + g
                            sp.wait_ge(scored, L + 6 * i + k - 1)
                            if k < 2:
                                sp.wait_ge(sn_done, 3)
                            src = TS[ds((2 * i + b) * T, T), g * CH:(g + 1) * CH]
                            sp.dma_start(qb[:, k % 2, :, :], src.unsqueeze(0).to_broadcast([P, T, CH])
                                         ).then_inc(qb_in[k % 2], 16)
                            if g == 0:
                                sp.wait_ge(scored, L + 6 * i - 6 + 3 * b + 3)
                                for gg in range(3):
                                    sp.dma_start(kc[:, b, UNIT0[gg]:UNIT0[gg] + UNITS[gg], :],
                                                 cached(gg, 2 * i + b, 0)).then_inc(k_in[b], 16)
                    sp.wait_ge(pv_done, L + i)
                    for b in range(2):
                        for g in range(3):
                            sp.dma_start(vc[:, b, UNIT0[g]:UNIT0[g] + UNITS[g], :],
                                         cached(g, 2 * i + b, 1)).then_inc(v_in, 16)
                    sp.dma_start(vn[:, :, :], TS[ds(2 * i * T, 2 * T), 6 * CH:9 * CH]).then_inc(v_in, 16)
                sp.wait_ge(filled, 16)
                sp.wait_ge(stored, 16 + 16 * NB)
                sp.dma_start(OG[SEQ:TOK, 0, 0:CH], OA.rearrange("(t h) e -> t (h e)", h=NH)).then_inc(filled, 16)
                sp.wait_ge(filled, 32)

            @block.gpsimd
            def _(pool):
                nc.gpsimd.memset(pm1[:, :, :], 0.0).then_inc(cleared, 1)
                nc.gpsimd.memset(pm2[:, :, :], 0.0).then_inc(cleared, 1)
                nc.gpsimd.memset(pn[:, :, :], 0.0).then_inc(cleared, 1)
                nc.gpsimd.memset(fill[:, :, :], 0.0).then_inc(cleared, 1)
                pool.wait_ge(cleared, 4)
                nc.gpsimd.memset(fill[:, 0, CH + NH:], 1.0).then_inc(cleared, 1)
                pool.sem_inc(cleared, 1)
                pool.wait_ge(cleared, 6)

            @block.tensor
            def _(pe):
                for x in (sT_done, pT_done, pv_done):
                    pe.sem_inc(x, L)
                pe.wait_ge(sn_done, 3)
                for g in range(3):
                    last = nc.tensor.transpose(p_sn[:, g, :], sn[:, g, :, :], ident[0:NS, 0:NS])
                last.then_inc(snT_done, 1)
                with pe.Fori(0, NB) as i:
                    pe.wait_ge(scored, L + 6 * i + 6)
                    for g in range(3):
                        last = nc.tensor.transpose(p_s[:, g, :], sT[:, g, :], ident[:, :])
                    last.then_inc(sT_done, 1)
                    pe.wait_ge(p_ready, L + i + 1)
                    for g in range(3):
                        nc.tensor.transpose(p_p[:, g, :], s[:, g, 0:P], ident[:, :])
                        last = nc.tensor.transpose(p_pn[:, g, :], pn[:, g, :], ident[:, :])
                    last.then_inc(pT_done, 1)
                    pe.wait_ge(pm_done, L + i + 1)
                    pe.wait_ge(v_in, 112 * i + 112)
                    pe.wait_ge(out_ready, L + i)
                    for g in range(3):
                        nc.tensor.matmul(p_o[:, g, :], pnT[:, g, :], vn[:, g, :], start=True, stop=False)
                        for b in range(2):
                            for c in range(UNITS[g]):
                                if g == 0:
                                    stat = pm0[:, 64 * b:64 * b + 64]
                                else:
                                    stat = (pm1, pm2)[g - 1][:, b, 64 * c:64 * c + 64]
                                last = nc.tensor.matmul(p_o[64 * b:64 * b + 64, g, :], stat, vc[:, b, UNIT0[g] + c, :],
                                                        start=False, stop=(c == UNITS[g] - 1))
                    last.then_inc(pv_done, 1)

            @block.scalar
            def _(act):
                for x in (exp_done, wexp_done, pm_done):
                    act.sem_inc(x, L)
                act.sem_inc(stored, 16)
                act.wait_ge(cleared, 6)
                with act.Fori(0, NB) as i:
                    act.wait_ge(maxed, L + i + 1)
                    for g in range(3):
                        last = nc.scalar.activation(s[:, g, :], s[:, g, :], ACT.Exp, bias=nm[:, g:g + 1],
                                                    accum_out=dn[:, g:g + 1])
                    last.then_inc(exp_done, 1)
                    act.wait_ge(lowest, L + i + 1)
                    nc.scalar.activation(wg[:, :], wd[:, :], ACT.Exp).then_inc(wexp_done, 1)
                    act.wait_ge(pT_done, L + i + 1)
                    act.wait_ge(pv_done, L + i)
                    nc.scalar.copy(pnT[:, :, :], p_pn[:, :, :])
                    nc.scalar.copy(pm0[:, :], p_p[:, 0, :])
                    d1 = pm1[:, :, :].rearrange("p b (c x) -> p b c x", x=72)
                    s1 = p_p[:, 1, :].rearrange("p (b a c h) -> p b a c h", b=2, a=2, c=4)
                    for a in range(2):
                        nc.scalar.copy(d1[:, :, :, 32 * a:32 * a + NH], s1[:, :, a, :, :])
                    d2 = pm2[:, :, :].rearrange("p b (c x) -> p b c x", x=72)
                    nc.scalar.copy(d2[:, :, :, 0:NH], p_p[:, 2, :].rearrange("p (b c h) -> p b c h", b=2, c=8)
                                   ).then_inc(pm_done, 1)
                    act.wait_ge(out_ready, L + i + 1)
                    act.dma_start(OA[ds(i * ROWS, ROWS), :], oa[:, 0, :]).then_inc(stored, 16)

            @block.vector
            def _(dve):
                V = nc.vector
                for x in (scored, maxed, p_ready, lowest, out_ready):
                    dve.sem_inc(x, L)
                dve.wait_ge(const_in, 32)
                dve.wait_ge(kn_in, 16)
                for g in range(3):
                    dve.wait_ge(qn_in[g % 2], 128 * (g // 2) + 128)
                    q = qb[0:NS, g % 2, :, :]
                    V.tensor_tensor(q, q, kn[:, g:g + 1, :].to_broadcast([NS, T, CH]), ALU.mult).then_inc(chain, 1)
                    dve.wait_ge(chain, 3 * g + 1)
                    prod = q.rearrange("p t (h e) -> p (t h) e", h=NH)
                    V.tensor_reduce(sn[:, g, 0, :], prod, AX_X, ALU.add).then_inc(chain, 1)
                    dve.wait_ge(chain, 3 * g + 2)
                    V.tensor_copy(sn[:, g, 1, :], sn[:, g, 0, :]).then_inc(chain, 1)
                    dve.wait_ge(chain, 3 * g + 3)
                    dve.sem_inc(sn_done, 1)
                dve.wait_ge(snT_done, 1)
                V.tensor_copy(snT[:, :, :], p_sn[:, :, :]).then_inc(chain, 1)
                dve.wait_ge(chain, 10)
                dve.wait_ge(cleared, 6)
                with dve.Fori(0, NB) as i:
                    link = Chain(dve, chain, 10 + LINKS * i)
                    for b in range(2):
                        for g in range(3):
                            k = 3 * b + g
                            dve.wait_ge(qb_in[k % 2], 48 * i + 16 * (k // 2) + 16)
                            if g == 0:
                                dve.wait_ge(k_in[b], 48 * i + 48)
                            q = qb[:, k % 2, :, :]
                            keys = kc[:, b, UNIT0[g]:UNIT0[g] + UNITS[g], :]
                            if g == 1:
                                q = q.rearrange("p (a c) e -> p a c e", a=2)
                                keys = keys.unsqueeze(1).to_broadcast([P, 2, 4, CH])
                            elif g == 0:
                                keys = keys.to_broadcast([P, T, CH])
                            link(V.tensor_tensor(q, q, keys, ALU.mult))
                            if k == 0:
                                dve.wait_ge(sT_done, L + i)
                            prod = qb[:, k % 2, :, :].rearrange("p t (h e) -> p (t h) e", h=NH)
                            V.tensor_reduce(sT[:, g, 64 * b:64 * b + 64], prod, AX_X, ALU.add).then_inc(scored, 1)
                    for b in range(2):
                        last = V.tensor_copy(sn2[64 * b:64 * b + 64, :, :],
                                             snT[64 * b:64 * b + 64, :, ds((2 * i + b) * T, T)])
                    link(last)
                    dve.wait_ge(pT_done, L + i)
                    dve.wait_ge(sT_done, L + i + 1)
                    for g in range(3):
                        dve.sem_inc(turns, 1)
                        V.tensor_tensor_reduce(out=s[:, g, 0:P], in0=p_s[:, g, :], in1=mask[:, g, 0:P],
                                               scale=HD ** -0.5, scalar=LOWEST, op0=ALU.add, op1=ALU.max,
                                               accum_out=mx[:, 0, g:g + 1])
                        last = V.tensor_tensor_reduce(out=s[:, g, P:], in0=sn2[:, g, :], in1=mask[:, g, P:],
                                                      scale=HD ** -0.5, scalar=LOWEST, op0=ALU.add, op1=ALU.max,
                                                      accum_out=mx[:, 1, g:g + 1])
                    link(last)
                    link(V.tensor_tensor(nm[:, :], mx[:, 0, :], mx[:, 1, :], ALU.max))
                    link(V.tensor_scalar(nm[:, :], nm[:, :], -1.0, None, ALU.mult))
                    dve.sem_inc(maxed, 1)
                    link(V.tensor_reduce(lw[:, :], nm[:, :], AX_X, ALU.min))
                    link(V.tensor_scalar(wd[:, :], nm[:, :], -1.0, lw[:, 0:1], ALU.mult, ALU.add))
                    dve.sem_inc(lowest, 1)
                    dve.wait_ge(exp_done, L + i + 1)
                    for b in range(2):
                        last = V.tensor_copy(pn[64 * b:64 * b + 64, :, T * b:T * b + T], s[64 * b:64 * b + 64, :, P:])
                    last.then_inc(p_ready, 1)
                    dve.wait_ge(wexp_done, L + i + 1)
                    link(V.tensor_tensor(wd[:, :], wg[:, :], dn[:, :], ALU.mult))
                    link(V.tensor_reduce(ds_[:, 0:1], wd[:, :], AX_X, ALU.add))
                    link(V.reciprocal(ds_[:, 1:2], ds_[:, 0:1]))
                    link(V.tensor_scalar(wg[:, :], wg[:, :], ds_[:, 1:2], None, ALU.mult))
                    dve.wait_ge(pv_done, L + i + 1)
                    for g in range(3):
                        last = V.scalar_tensor_tensor(out=po[:, g, :], in0=p_o[:, g, :], scalar=wg[:, g:g + 1],
                                                      in1=diag[:, :], op0=ALU.mult, op1=ALU.mult)
                    link(last)
                    link(V.tensor_reduce(oa[:, 1, :], po[:, :, :].rearrange("p g (h e) -> p e (g h)", h=NH), AX_X,
                                         ALU.add))
                    dve.wait_ge(stored, 16 * i + 16)
                    V.tensor_copy(oa[:, 0, :], oa[:, 1, :]).then_inc(out_ready, 1)
                    assert link.links == LINKS, link.links


def gla_sample(nc, A, S, O, ident):
    TMs, TSs, OL = S["tm"], S["ts"], S["ol"]
    NP = GH // 2
    st, sb, pb, sem = scope(nc)
    with st:
        wa = sb("g_wa", [RANK, GH * GK])
        ba = sb("g_ba", [P, NP])
        raw = sb("g_raw", [NS, TS_W])
        v = sb("g_v", [NS, GH * GV_W])
        state = sb("g_state", [P, DB, NP, 2 * GV_W])
        new = sb("g_new", [P, DB, NP, GV_W])
        f = sb("g_f", [P, 4, NS])
        fr = sb("g_fr", [RANK, NS])
        z = sb("g_z", [P, NP, NS])
        e = sb("g_e", [P, NP, NS])
        keep = sb("g_keep", [P, NP, NS])
        b = sb("g_b", [P, NP, NS])
        eb = sb("g_eb", [P, 3, NP, NS])
        decay = sb("g_decay", [P, NP, DB])
        qe = sb("g_qe", [P, NP, NS])
        ke = sb("g_ke", [P, NP, NS])
        kd = sb("g_kd", [P, NP, NS])
        qm = sb("g_qm", [P, NP, DB * 72])
        km = sb("g_km", [NS, NP, DB, P])
        att = sb("g_att", [NS, 2, NP, NS])
        cmask = sb("g_cmask", [NS, NS], U32)
        bmask = sb("g_bmask", [NS, DB])
        out = sb("g_out", [NS, GH * GV_W])
        p_f = pb("g_p_f", [P, 4, NS])
        p_r = pb("g_p_r", [RANK, NS])
        p_g = pb("g_p_g", [P, NP, NS])
        p_att = pb("g_p_att", [NS, 2, CH])
        p_o = pb("g_p_o", [NS, GH * GV_W])
        p_u = pb("g_p_u", [P, 2, CH])
        in_ = sem("g_in")
        st_in = sem("g_st_in")
        cleared = sem("g_cleared")
        t_done = sem("g_t_done")
        t_evacd = sem("g_t_evacd")
        g_done = sem("g_g_done")
        z_done = sem("g_z_done")
        gate = sem("g_gate")
        d = sem("g_d")
        e_ready = sem("g_e_ready")
        kd_ready = sem("g_kd_ready")
        kdT_done = sem("g_kdT_done")
        km_done = sem("g_km_done")
        att_done = sem("g_att_done")
        att_masked = sem("g_att_masked")
        o_done = sem("g_o_done")
        o_evacd = sem("g_o_evacd")
        u_done = sem("g_u_done")
        u_read = sem("g_u_read")
        stored = sem("g_stored")
        with nc.Block() as block:

            @block.sync
            def _(sp):
                for dst, src in ((raw[:, :], TSs), (v[:, :], TMs[SEQ:TOK, TM_GV * CH:(TM_GV + 1) * CH]),
                                 (wa[:, :], A["w_gla_a2"].rearrange("a r k -> (a r) k")), (ba[:, :], A["b_gla_a"]),
                                 (cmask[:, :], A["sample_mask"]), (bmask[:, :], A["batch_mask"])):
                    sp.dma_start(dst, src).then_inc(in_, 16)
                sp.wait_ge(cleared, 1)
                for h in range(GH):
                    r, c = slice(GK * (h % 2), GK * (h % 2) + GK), slice(GV_W * (h % 2), GV_W * (h % 2) + GV_W)
                    sp.dma_start(state[r, :, h // 2, c], A["state_gla"][0, :, h, :, :].rearrange("b k v -> k b v")
                                 ).then_inc(st_in, 16)
                sp.wait_ge(o_evacd, 1)
                sp.dma_start(OL[SEQ:TOK, :], out[:, :]).then_inc(stored, 16)
                sp.wait_ge(u_read, DB * NP)
                for h in range(GH):
                    r = slice(GK * (h % 2), GK * (h % 2) + GK)
                    sp.dma_start(O["gla_sample"][0, :, h, :, :].rearrange("b k v -> k b v"), new[r, :, h // 2, :]
                                 ).then_inc(stored, 16)
                sp.wait_ge(stored, 16 + 16 * GH)

            @block.gpsimd
            def _(pool):
                nc.gpsimd.memset(state[:, :, :, :], 0.0).then_inc(cleared, 1)
                nc.gpsimd.memset(keep[:, :, :], 1.0).then_inc(cleared, 1)
                nc.gpsimd.memset(qm[:, :, :], 0.0).then_inc(cleared, 1)
                nc.gpsimd.memset(att[:, :, :, :], 0.0).then_inc(cleared, 1)
                pool.wait_ge(cleared, 4)
                nc.gpsimd.memset(keep[:, :, :].rearrange("p a (c t) -> p (a c) t", t=T)[:, :, 0:1], 0.0
                                 ).then_inc(cleared, 1)

            @block.tensor
            def _(pe):
                pe.wait_ge(in_, 96)
                for c in range(4):
                    nc.tensor.transpose(p_f[:, c, :], raw[:, c * P:(c + 1) * P], ident[0:NS, 0:NS])
                nc.tensor.transpose(p_r[:, :], raw[:, 4 * P:4 * P + RANK], ident[0:NS, 0:NS]).then_inc(t_done, 1)
                pe.wait_ge(t_evacd, 2)
                for a in range(NP):
                    last = nc.tensor.matmul(p_g[:, a, :], wa[:, a * P:(a + 1) * P], fr[:, :], start=True, stop=True)
                last.then_inc(g_done, 1)
                pe.wait_ge(kd_ready, 1)
                for a in range(NP):
                    last = nc.tensor.transpose(p_f[0:NS, 2 * a:2 * a + 2, :], kd[:, a, :], ident[:, :])
                last.then_inc(kdT_done, 1)
                for a in range(NP):
                    for h in range(2):
                        r = slice(GK * h, GK * h + GK)
                        last = nc.tensor.matmul(p_att[:, h, a * NS:(a + 1) * NS], ke[r, a, :], qe[r, a, :],
                                                start=True, stop=True)
                last.then_inc(att_done, 1)
                pe.wait_ge(st_in, 16 * GH)
                pe.wait_ge(km_done, NP)
                for a in range(NP):
                    for j in range(DB):
                        nc.tensor.matmul(p_o[:, 2 * GV_W * a:2 * GV_W * (a + 1)], qm[:, a, NS * j:NS * j + NS],
                                         state[:, j, a, :], start=(a == 0 and j == 0), stop=False)
                pe.wait_ge(att_masked, 1)
                for h in range(GH):
                    cols = slice(GV_W * h, GV_W * (h + 1))
                    last = nc.tensor.matmul(p_o[:, cols], att[:, h % 2, h // 2, :], v[:, cols], start=False,
                                            stop=(h == GH - 1))
                last.then_inc(o_done, 1)
                for j in range(DB):
                    for a in range(NP):
                        n = NP * j + a
                        if n >= 2:
                            pe.wait_ge(u_read, n - 1)
                        nc.tensor.matmul(p_u[:, n % 2, 0:2 * GV_W], km[:, a, j, :], v[:, 2 * GV_W * a:2 * GV_W * (a + 1)],
                                         start=True, stop=True).then_inc(u_done, 1)

            @block.scalar
            def _(act):
                act.wait_ge(t_done, 1)
                nc.scalar.copy(f[:, :, :], p_f[:, :, :]).then_inc(t_evacd, 1)
                nc.scalar.copy(fr[:, :], p_r[:, :]).then_inc(t_evacd, 1)
                log_gates(nc, act, None, z[:, :, :], e[:, :, :], gate, None)
                act.wait_ge(d, 1)
                nc.scalar.activation(eb[:, 0, :, :], b[:, :, :], ACT.Exp, scale=1.0 / TAU).then_inc(e_ready, 1)
                nc.scalar.activation(eb[:, 1, :, :], b[:, :, :], ACT.Exp, scale=-1.0 / TAU).then_inc(e_ready, 1)
                ends = b[:, :, :].rearrange("p a (c t) -> p a c t", t=T)[:, :, :, T - 1]
                nc.scalar.activation(decay[:, :, :], ends, ACT.Exp, scale=1.0 / TAU).then_inc(e_ready, 1)
                act.wait_ge(d, 2)
                nc.scalar.activation(eb[:, 2, :, :], e[:, :, :], ACT.Exp, scale=-1.0 / TAU).then_inc(e_ready, 1)
                act.wait_ge(o_done, 1)
                nc.scalar.copy(out[:, :], p_o[:, :]).then_inc(o_evacd, 1)

            @block.vector
            def _(dve):
                V = nc.vector
                dve.wait_ge(in_, 96)
                dve.wait_ge(cleared, 5)
                dve.wait_ge(g_done, 1)
                for a in range(NP):
                    last = V.tensor_scalar(z[:, a, :], p_g[:, a, :], ba[:, a:a + 1], None, ALU.add)
                last.then_inc(z_done, 1)
                dve.wait_ge(z_done, 1)
                log_gates(nc, None, dve, z[:, :, :], e[:, :, :], gate, None)
                flat = lambda x: x[:, :, :].rearrange("p a t -> p (a t)")
                V.tensor_tensor_scan(flat(b), flat(keep), flat(z), 0.0, ALU.mult, ALU.add).then_inc(d, 1)
                dve.wait_ge(d, 1)
                chunks = lambda x: x[:, :, :].rearrange("p a (c t) -> p (a c) t", t=T)
                V.tensor_tensor(chunks(e), chunks(b), chunks(b)[:, :, T - 1:T].to_broadcast([P, NP * DB, T]),
                                ALU.subtract).then_inc(d, 1)
                dve.wait_ge(e_ready, 4)
                dve.wait_ge(t_evacd, 2)
                V.scalar_tensor_tensor(out=qe[:, :, :], in0=f[:, 0:2, :], scalar=GK ** -0.5, in1=eb[:, 0, :, :],
                                       op0=ALU.mult, op1=ALU.mult)
                V.tensor_tensor(ke[:, :, :], f[:, 2:4, :], eb[:, 1, :, :], ALU.mult)
                V.tensor_tensor(kd[:, :, :], f[:, 2:4, :], eb[:, 2, :, :], ALU.mult).then_inc(kd_ready, 1)
                dve.wait_ge(kd_ready, 1)
                V.tensor_copy(qm[:, :, :].rearrange("p a (j x) -> p a j x", x=72)[:, :, :, 0:T],
                              qe[:, :, :].rearrange("p a (j t) -> p a j t", t=T))
                dve.wait_ge(kdT_done, 1)
                for a in range(NP):
                    V.tensor_tensor(km[:, a, :, :],
                                    p_f[0:NS, 2 * a:2 * a + 2, :].rearrange("p x t -> p (x t)").unsqueeze(1)
                                    .to_broadcast([NS, DB, P]),
                                    bmask[:, :].unsqueeze(2).to_broadcast([NS, DB, P]), ALU.mult).then_inc(km_done, 1)
                dve.wait_ge(att_done, 1)
                for h in range(2):
                    last = V.copy_predicated(att[:, h, :, :], cmask[:, :].unsqueeze(1).to_broadcast([NS, NP, NS]),
                                             p_att[:, h, 0:NP * NS].rearrange("p (a t) -> p a t", a=NP))
                last.then_inc(att_masked, 1)
                dve.wait_ge(st_in, 16 * GH)
                for j in range(DB):
                    for a in range(NP):
                        n = NP * j + a
                        dve.wait_ge(u_done, n + 1)
                        for h in range(2):
                            r, c = slice(GK * h, GK * h + GK), slice(GV_W * h, GV_W * h + GV_W)
                            last = V.scalar_tensor_tensor(out=new[r, j, a, :], in0=state[r, j, a, c],
                                                          scalar=decay[r, a, j:j + 1], in1=p_u[r, n % 2, c],
                                                          op0=ALU.mult, op1=ALU.add)
                        last.then_inc(u_read, 1)


def store_windows(pool, S, O, done):
    TMs = S["tm"]
    for g, win in enumerate(WINDOWS):
        rows = min(win, SEQ)
        for kv in range(2):
            cols = slice((3 + 3 * kv + g) * CH, (4 + 3 * kv + g) * CH)
            pool.dma_start(O[f"kv_w{win}_prompt"][0, 0, :, kv, :, :].rearrange("s h e -> s (h e)"),
                           TMs[SEQ - rows:SEQ, cols]).then_inc(done, 16)
            pool.dma_start(O[f"kv_w{win}_sample"][0, :, :, kv, :, :].rearrange("b t h e -> (b t) (h e)"),
                           TMs[SEQ:TOK, cols]).then_inc(done, 16)


def decoder_step(nc, A, O):
    S = {name: nc.dram_tensor(name, shape, F32, kind="Internal").ap()
         for name, shape in (("tm", (TOK, TM_W)), ("ts", (NS, TS_W)), ("fm", (CH, SEQ)), ("gl", (RANK, SEQ)),
                             ("og", (TOK, 3, OG_W)), ("ol", (TOK, GH * GV_W)), ("oa", (NS * NH, HD)))}
    st, sb, _, sem = scope(nc)
    with st:
        ident = sb("ident", [P, P])
        ident_in = sem("ident_in")
        with nc.Block() as block:
            @block.sync
            def _(sp):
                sp.dma_start(ident[:, :], A["ident"]).then_inc(ident_in, 16)
                sp.wait_ge(ident_in, 16)

        h_st, h_sb, _, _ = scope(nc)
        with h_st:
            hT_hi = h_sb("hT_hi", [P, KC, TOK], F32R)
            hT_lo = h_sb("hT_lo", [P, KC, TOK], F32R)
            norm_and_transpose(nc, A, hT_hi, hT_lo, ident)
            project(nc, A, S, hT_hi, hT_lo)
        attend_prompt(nc, A, S, O, ident)
        attend_sample(nc, A, S, ident)
        gla_prompt(nc, A, S, O, ident)
        gla_sample(nc, A, S, O, ident)
        merge(nc, A, S, O, ident)


_OUTS = [("y_prompt", (1, SEQ, D)), ("y_sample", (DB, T, D))] + \
        [(f"kv_w{w}_prompt", (1, 1, min(w, SEQ), 2, NH, HD)) for w in (128, 512, 2048)] + \
        [("gla_prompt", (1, 1, GH, GK, GV_W))] + \
        [(f"kv_w{w}_sample", (1, DB, T, 2, NH, HD)) for w in (128, 512, 2048)] + \
        [("gla_sample", (1, DB, GH, GK, GV_W))]


_INS = ["x_prompt", "x_sample", "cache_kv_w128", "cache_kv_w512", "cache_kv_w2048", "state_gla", "ln_w", "w_in",
        "w_gla_a2", "b_gla_a", "gla_norm_w", "w_attn_out", "w_gla_out", "w_out", "final_norm_w"]


def _constants():
    import numpy as np

    half = HALF
    inv = (1.0 / (np.float32(500000.0) ** (np.arange(half, dtype=np.float32) * np.float32(2.0 / 16)))).astype(np.float32)
    pos = np.concatenate([np.arange(SEQ), np.arange(SEQ - NS, SEQ), SEQ + np.arange(NS) % T]).astype(np.float32)
    ang = pos[:, None] * inv[None, :]
    rope = np.concatenate([np.cos(ang), np.sin(ang)], axis=1).astype(np.float32)
    q, k = np.arange(P)[:, None], np.arange(P)[None, :]
    own = np.where(k <= q, 0.0, NEG)
    masks = np.stack([np.concatenate([np.full((P, P), NEG), own], 1),
                      np.concatenate([np.where(k >= q, 0.0, NEG), own], 1)], axis=1).astype(np.float32)
    chunk_mask = ((k >= q) & (k // CHUNK == q // CHUNK)).astype(np.uint32)
    tok = (np.arange(ROWS) // NH % T)[:, None]
    j = np.arange(T)[None, :]
    seen = np.stack([np.concatenate([k >= tok, j <= tok], 1),
                     np.concatenate([k >= tok // 4, (j == tok) | (j == tok - 4)], 1),
                     np.concatenate([k >= 0 * tok, j == tok], 1)], axis=1)
    dec_mask = np.where(seen, 0.0, NEG).astype(np.float32)
    dec_diag = (np.arange(CH)[None, :] // HD == np.arange(ROWS)[:, None] % NH).astype(np.float32)
    n = np.arange(NS)
    sample_mask = ((n[None, :] >= n[:, None]) & (n[None, :] // T == n[:, None] // T)).astype(np.uint32)
    batch_mask = (n[:, None] // T == np.arange(DB)[None, :]).astype(np.float32)
    return {"rope": rope, "ident": np.eye(P, dtype=np.float32), "masks": masks, "chunk_mask": chunk_mask,
            "dec_mask": dec_mask, "dec_diag": dec_diag, "sample_mask": sample_mask, "batch_mask": batch_mask}


def kernel(**inputs):
    import numpy as np
    import concourse.bacc as bacc
    from concourse.bass_utils import run_bass_kernel_spmd as run

    nc = bacc.Bacc("TRN2", target_bir_lowering=False, num_devices=1)
    arrays, A = {}, {}
    inputs = dict(inputs)
    inputs["ln_w"] = np.asarray(inputs["ln_w"]).reshape(KC, P).T
    inputs["b_gla_a"] = np.asarray(inputs["b_gla_a"]).reshape(GH // 2, P).T
    for name, a in [(n, inputs[n]) for n in _INS] + sorted(_constants().items()):
        a = np.ascontiguousarray(a)
        arrays["in_" + name] = a
        A[name] = nc.dram_tensor("in_" + name, a.shape, mybir.dt.from_np(a.dtype), kind="ExternalInput").ap()
    O = {name: nc.dram_tensor("out_" + name, shape, F32, kind="ExternalOutput").ap() for name, shape in _OUTS}
    decoder_step(nc, A, O)
    r = run(nc, [arrays], core_ids=[0]).results[0]
    return tuple(r["out_" + name] for name, _ in _OUTS)
```

```python
from contextlib import ExitStack

import concourse.bass as bass
from concourse import mybir

F32 = mybir.dt.float32
F32R = mybir.dt.float32r
U32 = mybir.dt.uint32
ALU = mybir.AluOpType
ACT = mybir.ActivationFunctionType
AX_X = mybir.AxisListType.X
ds = bass.ds

D = 1024
SEQ = 2048
DB, T = 8, 8
NS = DB * T
TOK = SEQ + NS
P = 128
KC = D // P
NT = SEQ // P
CH = 512
HD = 64
NH = 8
HALF = 8
EPS = 1e-6

COL_AZ, COL_GQK, COL_GV, COL_GZ, COL_GLR, COL_MGA = 4608, 5120, 5632, 6144, 6656, 6672
RANK = 16
IN_W = 8720

N_ROPED, N_TM = 6, 16
TM_GV, TM_AZ, TM_GZ, TM_MG = 9, 10, 11, 12
TM_W = N_TM * CH
N_CHUNK = N_TM + 1
FM_GQ, FM_GK = 0, 256
LEAD = 8
WINDOWS = (128, 512, 2048)
GROUPS = ((1, 16), (4, 4), (16, 1))
UNITS = (1, 4, 8)
UNIT0 = (0, 1, 5)
NU = 13
TS_W = CH + RANK


def scope(nc):
    st = ExitStack()
    sems = []

    def sb(name, shape, dt=F32):
        return st.enter_context(nc.sbuf_tensor(name, shape, dt))

    def pb(name, shape, dt=F32):
        return st.enter_context(nc.psum_tensor(name, shape, dt))

    def sem(name):
        sems.append(nc.alloc_semaphore(name))
        return sems[-1]

    def clear():
        if sems:
            nc.clear_and_free_semaphores(sems)
            nc.all_engine_barrier()

    st.callback(clear)
    return st, sb, pb, sem


def rsqrt_steps(nc, dve, done, before, m):
    nc.vector.reciprocal(m[3], m[2]).then_inc(done, 1)
    dve.wait_ge(done, before + 1)
    nc.vector.tensor_scalar(m[4], m[1], m[3], m[3], ALU.mult, ALU.mult).then_inc(done, 1)
    dve.wait_ge(done, before + 2)
    nc.vector.tensor_scalar(m[5], m[4], -0.5, 1.5, ALU.mult, ALU.add).then_inc(done, 1)
    dve.wait_ge(done, before + 3)
    nc.vector.tensor_tensor(m[2], m[3], m[5], ALU.mult).then_inc(done, 1)
    dve.wait_ge(done, before + 4)


def norm_and_transpose(nc, A, hT_hi, hT_lo, ident):
    st, sb, pb, sem = scope(nc)
    with st:
        xs = sb("a_x", [P, 2, D])
        junk = sb("a_junk", [P, D])
        hf = sb("a_hf", [P, 2, KC, P])
        lnw = sb("a_lnw", [P, KC])
        ms = sb("a_ms", [P, 2, 6])
        pt = pb("a_pt", [P, 2, 2, 4, P])
        x_in = [sem("a_x_in0"), sem("a_x_in1")]
        w_in = sem("a_w_in")
        x_free = sem("a_x_free")
        sq_done = sem("a_sq_done")
        stat = sem("a_stat")
        rooted = sem("a_rooted")
        scaled = sem("a_scaled")
        tr_done = sem("a_tr_done")
        weighted = sem("a_weighted")
        hi_done = sem("a_hi_done")
        lo_done = sem("a_lo_done")
        xp = A["x_prompt"].rearrange("a s d -> (a s) d")
        xq = A["x_sample"].rearrange("a s d -> (a s) d")
        with nc.Block() as block:

            @block.sync
            def _(sp):
                sp.dma_start(lnw[:, :], A["ln_w"]).then_inc(w_in, 16)
                sp.sem_inc(x_free, 2)
                with sp.Fori(0, NT // 2) as i:
                    for s in range(2):
                        sp.wait_ge(x_free, 2 * i + s + 1)
                        sp.dma_start(xs[:, s, :], xp[ds((2 * i + s) * P, P), :]).then_inc(x_in[s], 16)
                sp.wait_ge(x_free, NT + 1)
                sp.dma_start(xs[0:NS, 0, :], xq).then_inc(x_in[0], 16)

            @block.scalar
            def _(act):
                def square(i, s, n, rows):
                    act.wait_ge(x_in[s], 16 * i + 16)
                    nc.scalar.activation(junk[0:rows, :], xs[0:rows, s, :], ACT.Square,
                                         accum_out=ms[0:rows, s, 0:1]).then_inc(sq_done, 1)

                def root(n, s, rows):
                    act.wait_ge(stat, 5 * n + 1)
                    nc.scalar.activation(ms[0:rows, s, 2:3], ms[0:rows, s, 1:2], ACT.Sqrt).then_inc(rooted, 1)

                def round_hi(n, s, off, cols):
                    act.wait_ge(weighted, 2 * n + 2)
                    nc.scalar.copy(hT_hi[:, :, ds(off, cols)], hf[:, s, :, 0:cols]).then_inc(hi_done, 1)

                with act.Fori(0, NT // 2) as i:
                    for s in range(2):
                        square(i, s, 2 * i + s, P)
                        root(2 * i + s, s, P)
                        round_hi(2 * i + s, s, (2 * i + s) * P, P)
                square(NT // 2, 0, NT, NS)
                root(NT, 0, NS)
                round_hi(NT, 0, SEQ, NS)

            @block.vector
            def _(dve):
                dve.wait_ge(w_in, 16)
                dve.sem_inc(lo_done, 1)

                def tile(n, s, off, rows):
                    dve.wait_ge(sq_done, n + 1)
                    m = [ms[0:rows, s, j:j + 1] for j in range(6)]
                    nc.vector.tensor_scalar(m[1], m[0], 1.0 / D, EPS, ALU.mult, ALU.add).then_inc(stat, 1)
                    dve.wait_ge(rooted, n + 1)
                    rsqrt_steps(nc, dve, stat, 5 * n + 1, m)
                    nc.vector.tensor_scalar(xs[0:rows, s, :], xs[0:rows, s, :], ms[0:rows, s, 2:3], None,
                                            ALU.mult).then_inc(scaled, 1)
                    for h in range(2):
                        dve.wait_ge(tr_done, 2 * n + h + 1)
                        nc.vector.tensor_tensor(
                            hf[:, s, 4 * h:4 * h + 4, 0:rows], pt[:, s, h, :, 0:rows],
                            lnw[:, 4 * h:4 * h + 4].unsqueeze(2).to_broadcast([P, 4, rows]),
                            ALU.mult).then_inc(weighted, 1)
                    dve.wait_ge(hi_done, n + 1)
                    nc.vector.tensor_tensor(hT_lo[:, :, ds(off, rows)], hf[:, s, :, 0:rows],
                                            hT_hi[:, :, ds(off, rows)].bitcast(F32),
                                            ALU.subtract).then_inc(lo_done, 1)

                with dve.Fori(0, NT // 2) as i:
                    for s in range(2):
                        tile(2 * i + s, s, (2 * i + s) * P, P)
                tile(NT, 0, SEQ, NS)
                dve.wait_ge(lo_done, NT + 2)

            @block.tensor
            def _(pe):
                def tile(n, s, rows):
                    pe.wait_ge(scaled, n + 1)
                    for h in range(2):
                        for c in range(4):
                            k = 4 * h + c
                            last = nc.tensor.transpose(pt[:, s, h, c, 0:rows], xs[0:rows, s, k * P:(k + 1) * P],
                                                       ident[0:rows, 0:rows])
                        last.then_inc(tr_done, 1)
                    pe.wait_ge(tr_done, 2 * n + 2)
                    pe.sem_inc(x_free, 1)

                with pe.Fori(0, NT // 2) as i:
                    for s in range(2):
                        tile(2 * i + s, s, P)
                tile(NT, 0, NS)


def cached(A, g, b, kv):
    dil, _ = GROUPS[g]
    cache = A[f"cache_kv_w{WINDOWS[g]}"]
    src = cache[0, ds(b, 1), :, kv, :, :].rearrange("b (l r) h e -> l (b r) (h e)", r=dil)
    return src[:, 0:UNITS[g], :]


def project(nc, A, S, hT_hi, hT_lo, sT):
    TMs, TSs, FMs, GLs = S["tm"], S["ts"], S["fm"], S["gl"]
    TILES = NT + 1
    LASTS = TOK - P
    st, sb, pb, sem = scope(nc)
    with st:
        raw = sb("b_raw", [P, KC, CH])
        whi = sb("b_whi", [P, KC, CH], F32R)
        wlo = sb("b_wlo", [P, KC, CH], F32R)
        stage = sb("b_stage", [P, 5, CH])
        cs = sb("b_cs", [P, TILES, 2, HALF])
        rc = sb("b_rc", [P, NH, 2, HALF])
        rs = sb("b_rs", [P, NH, 2, HALF])
        ck = sb("b_ck", [P, 2, CH])
        cq = sb("b_cq", [P, 2, CH])
        acc = pb("b_acc", [P, 5, CH])
        cs_in = sem("b_cs_in")
        w_in = [sem("b_w_in0"), sem("b_w_in1")]
        hi_done = sem("b_hi_done")
        lo_done = sem("b_lo_done")
        w_used = sem("b_w_used")
        mm_done = sem("b_mm_done")
        evacd = sem("b_evacd")
        roped = sem("b_roped")
        rmul = sem("b_rmul")
        stored = [sem(f"b_stored{k}") for k in range(5)]
        ck_in = [sem("b_ck_in0"), sem("b_ck_in1")]
        cq_in = [sem("b_cq_in0"), sem("b_cq_in1")]
        multiplied = sem("b_multiplied")
        scored = sem("b_scored")
        items = [(g, c, t) for g in range(3) for c in range(UNITS[g]) for t in range(c if g else 0, T, UNITS[g])]
        NI = len(items)
        unit = lambda m: UNIT0[items[m][0]] + items[m][1]
        unit_end = [max(m for m in range(NI) if unit(m) == u) + 1 for u in range(NU)]
        FIRST = N_CHUNK - 1 - DB
        W = A["w_in"].rearrange("a (c p) e -> p (a c) e", p=P)
        slot = lambda t: t % 4 if t < NT else 4
        EV0 = 4
        N_ALL = N_CHUNK * TILES

        with nc.Block() as block:

            @block.sync
            def _(sp):
                sp.dma_start(cs[:, :, :, :], A["rope"].rearrange("(t p) (a f) -> p t a f", p=P, a=2)).then_inc(cs_in, 16)
                for k in range(5):
                    sp.sem_inc(stored[k], 16)

                def load(i, col, width=CH):
                    for h in range(2):
                        if not (isinstance(i, int) and i == 0):
                            sp.wait_ge(lo_done, 8 * i - 4 + 4 * h)
                        sp.dma_start(raw[:, 4 * h:4 * h + 4, 0:width],
                                     W[:, 4 * h:4 * h + 4, ds(col, width)]).then_inc(w_in[h], 16)

                def store(i, t, dst, src):
                    sp.dma_start(dst, src).then_inc(stored[slot(t)], 16)

                def tm_chunk(i, ready):
                    for t in range(TILES):
                        ready(TILES * i + t)
                        if t < NT:
                            store(i, t, TMs[t * P:(t + 1) * P, ds(i * CH, CH)], stage[:, slot(t), :])
                        else:
                            store(i, t, TMs[SEQ:TOK, ds(i * CH, CH)], stage[NS:P, 4, :])

                rotated = lambda n: sp.wait_ge(roped, n + 2)
                copied = lambda n: sp.wait_ge(evacd, EV0 + n + 1)
                load(0, 0)
                with sp.Fori(0, N_ROPED) as i:
                    load(i + 1, (i + 1) * CH)
                    tm_chunk(i, rotated)
                with sp.Fori(N_ROPED, TM_GV - 1) as i:
                    load(i + 1, (i + 1) * CH)
                    tm_chunk(i, copied)
                for i, col in ((TM_GV - 1, COL_GV), (TM_GV, COL_AZ), (TM_AZ, COL_GZ)):
                    load(i + 1, col)
                    tm_chunk(i, copied)
                with sp.Fori(TM_GZ, N_TM - 1) as i:
                    load(i + 1, COL_MGA + CH * (i - TM_GZ))
                    tm_chunk(i, copied)
                load(N_TM, COL_GQK)
                tm_chunk(N_TM - 1, copied)
                load(N_CHUNK, COL_GLR, P)
                for t in range(NT):
                    copied(TILES * N_TM + t)
                    store(N_TM, t, FMs[(t // 4) * P:(t // 4 + 1) * P, (t % 4) * CH:(t % 4 + 1) * CH], stage[:, slot(t), :])
                copied(TILES * N_TM + NT)
                store(N_TM, NT, TSs[:, 0:CH], stage[NS:P, 4, :])
                for tb in range(4):
                    copied(N_ALL + tb)
                    store(N_CHUNK, tb, GLs[:, tb * CH:(tb + 1) * CH], stage[0:RANK, tb, :])
                copied(N_ALL + 4)
                store(N_CHUNK, NT, TSs[:, CH:TS_W], stage[NS:P, 4, 0:RANK])
                for k in range(4):
                    sp.wait_ge(stored[k], 16 + 16 * (4 * N_CHUNK + 1))
                sp.wait_ge(stored[4], 16 + 16 * (N_CHUNK + 1))

            @block.gpsimd
            def _(pool):
                pool.wait_ge(stored[4], 16 + 16 * 3)
                with pool.Fori(0, DB) as b:
                    for m, (g, c, t) in enumerate(items):
                        u = unit(m)
                        if m == 0 or unit(m - 1) != u:
                            last = unit_end[u - 2] if u >= 2 else (0, unit_end[NU - 2] - NI)[u]
                            pool.wait_ge(scored, LEAD + NI * b + last)
                            pool.dma_start(ck[:, u % 2, :], cached(A, g, b, 0)[:, c, :]).then_inc(ck_in[u % 2], 16)
                        pool.wait_ge(scored, LEAD + NI * b + m - 1)
                        pool.dma_start(cq[:, m % 2, :], TMs[ds(SEQ + T * b + t, 1), g * CH:(g + 1) * CH]
                                       .to_broadcast([P, CH])).then_inc(cq_in[m % 2], 16)

            @block.scalar
            def _(act):
                def split_hi(i, width=CH):
                    for k in range(KC):
                        if k % 4 == 0:
                            act.wait_ge(w_in[k // 4], 16 * i + 16)
                        if not (isinstance(i, int) and i == 0):
                            act.wait_ge(w_used, 8 * i - 8 + k + 1)
                        nc.scalar.copy(whi[:, k, 0:width], raw[:, k, 0:width]).then_inc(hi_done, 1)

                def evac(i, t, width=CH):
                    act.wait_ge(mm_done, TILES * i + t + 1)
                    uses = 4 * i + t // 4 if t < NT else i
                    act.wait_ge(stored[slot(t)], 16 * uses + 16)
                    nc.scalar.copy(stage[:, slot(t), 0:width], acc[:, slot(t), 0:width]).then_inc(evacd, 1)

                act.sem_inc(evacd, EV0)
                split_hi(0)
                with act.Fori(0, N_CHUNK - 1) as i:
                    for t in range(NT):
                        evac(i, t)
                    split_hi(i + 1)
                    evac(i, NT)
                i = N_CHUNK - 1
                for t in range(NT):
                    evac(i, t)
                split_hi(N_CHUNK, P)
                evac(i, NT)
                for tb in range(4):
                    act.wait_ge(mm_done, N_ALL + tb + 1)
                    act.wait_ge(stored[tb], 16 + 16 * 4 * N_CHUNK)
                    nc.scalar.copy(stage[:, tb, :], acc[:, tb, :]).then_inc(evacd, 1)
                act.wait_ge(mm_done, N_ALL + 5)
                act.wait_ge(stored[4], 16 + 16 * N_CHUNK)
                nc.scalar.copy(stage[:, 4, 0:RANK], acc[:, 4, 0:RANK]).then_inc(evacd, 1)

            @block.vector
            def _(dve):
                def split_lo(i, width=CH):
                    for k in range(KC):
                        dve.wait_ge(hi_done, 8 * i + k + 1)
                        nc.vector.tensor_tensor(wlo[:, k, 0:width], raw[:, k, 0:width],
                                                whi[:, k, 0:width].bitcast(F32), ALU.subtract).then_inc(lo_done, 1)

                def rope(i, t):
                    n = TILES * i + t
                    dve.wait_ge(evacd, EV0 + n + 1)
                    dve.wait_ge(roped, n + 1)
                    x = stage[:, slot(t), :].rearrange("p (h e) -> p h e", h=NH)[:, :, 0:2 * HALF].rearrange(
                        "p h (a f) -> p h a f", a=2)
                    full = [P, NH, 2, HALF]
                    cos = cs[:, t, 0:1, :].unsqueeze(1).to_broadcast(full)
                    sin = cs[:, t, 1:2, :].unsqueeze(1).to_broadcast(full)
                    nc.vector.tensor_tensor(rc[:, :, :, :], x, cos, ALU.mult).then_inc(rmul, 1)
                    nc.vector.tensor_tensor(rs[:, :, :, :], x, sin, ALU.mult).then_inc(rmul, 1)
                    dve.wait_ge(rmul, 2 * n + 2)
                    nc.vector.tensor_tensor(x[:, :, 0, :], rc[:, :, 0, :], rs[:, :, 1, :], ALU.subtract)
                    nc.vector.tensor_tensor(x[:, :, 1, :], rc[:, :, 1, :], rs[:, :, 0, :], ALU.add).then_inc(roped, 1)

                dve.wait_ge(cs_in, 16)
                dve.sem_inc(roped, 1)
                dve.sem_inc(scored, LEAD)
                split_lo(0)
                with dve.Fori(0, N_ROPED) as i:
                    for t in range(NT):
                        rope(i, t)
                    split_lo(i + 1)
                    rope(i, NT)
                with dve.Fori(N_ROPED, FIRST) as i:
                    split_lo(i + 1)
                with dve.Fori(0, DB) as b:
                    for m, (g, c, t) in enumerate(items):
                        u = unit(m)
                        dve.wait_ge(cq_in[m % 2], 16 * (NI // 2) * b + 16 * (m // 2) + 16)
                        if m == 0 or unit(m - 1) != u:
                            dve.wait_ge(ck_in[u % 2], 16 * ((NU + 1 - u % 2) // 2) * b + 16 * (u // 2) + 16)
                        q = cq[:, m % 2, :]
                        nc.vector.tensor_tensor(q, q, ck[:, u % 2, :], ALU.mult).then_inc(multiplied, 1)
                        dve.wait_ge(multiplied, NI * b + m + 1)
                        nc.vector.tensor_reduce(sT[:, g, ds((T * b + t) * NH, NH)],
                                                q.rearrange("p (h e) -> p h e", h=NH), AX_X, ALU.add
                                                ).then_inc(scored, 1)
                    split_lo(b + FIRST + 1)
                dve.wait_ge(scored, LEAD + NI * DB)
                split_lo(N_CHUNK, P)

            @block.tensor
            def _(pe):
                def product(out, k, stat_hi, stat_lo, mov_hi, mov_lo):
                    nc.tensor.matmul(out, stat_hi, mov_hi, start=(k == 0), stop=False)
                    nc.tensor.matmul(out, stat_hi, mov_lo, start=False, stop=False)
                    return nc.tensor.matmul(out, stat_lo, mov_hi, start=False, stop=(k == KC - 1))

                def tile(i, t, out, stat, mov):
                    pe.wait_ge(evacd, TILES * i + t + 1)
                    for k in range(KC):
                        if t == 0:
                            pe.wait_ge(lo_done, 8 * i + k + 1)
                        last = product(out, k, *stat(k), *mov(k))
                        if t == NT and k < KC - 1:
                            last.then_inc(w_used, 1)
                    last.then_inc(mm_done, 1)
                    if t == NT:
                        pe.wait_ge(mm_done, TILES * i + t + 1)
                        pe.sem_inc(w_used, 1)

                def tokens(off, width):
                    return lambda k: (hT_hi[:, k, off:off + width], hT_lo[:, k, off:off + width])

                def weights(off, width):
                    return lambda k: (whi[:, k, off:off + width], wlo[:, k, off:off + width])

                with pe.Fori(0, N_TM) as i:
                    for t in range(TILES):
                        tile(i, t, acc[:, slot(t), :], tokens(t * P if t < NT else LASTS, P), weights(0, CH))
                for t in range(NT):
                    tile(N_TM, t, acc[:, slot(t), :], weights((t // 4) * P, P), tokens((t % 4) * CH, CH))
                tile(N_TM, NT, acc[:, 4, :], tokens(LASTS, P), weights(0, CH))
                for tb in range(4):
                    tile(N_CHUNK, tb, acc[:, tb, :], weights(0, P), tokens(tb * CH, CH))
                pe.wait_ge(evacd, N_ALL + 5)
                for k in range(KC):
                    last = product(acc[:, 4, 0:RANK], k, *tokens(LASTS, P)(k), *weights(0, RANK)(k))
                last.then_inc(mm_done, 1)


NEG = -3.0e38
LOWEST = -3.4e38
OG_W = CH + 2 * NH


def attend_prompt(nc, A, S, O, ident, E):
    TMs, OG = S["tm"], S["og"]
    UNROLL = 4
    st, sb, pb, sem = scope(nc)
    with st:
        qk = sb("c_qk", [P, 2, 2, CH])
        v = sb("c_v", [P, UNROLL, CH])
        qT = sb("c_qT", [P, 2, 4, P])
        kT = sb("c_kT", [P, 4, UNROLL + 1, P])
        sm = sb("c_sm", [P, 2, 2, 2 * P])
        p = sb("c_p", [P, 2, 2, 2 * P])
        pT = sb("c_pT", [P, 2, 4, P])
        mx = sb("c_mx", [P, 2, 2])
        og = sb("c_og", [P, UNROLL, OG_W])
        mask = sb("c_mask", [P, 2, 2 * P])
        first = sb("c_first", [P, 2 * P])
        kn = sb("c_kn", [NS, 3, CH])
        qn = sb("c_qn", [NS, T, CH])
        p_qk = pb("c_p_qk", [P, CH])
        p_s = pb("c_p_s", [P, 2, 2, CH])
        p_t = pb("c_p_t", [P, 2, 4, P])
        p_o = pb("c_p_o", [P, NH, HD])

        mask_in = sem("c_mask_in")
        qk_in = [sem("c_qk_in0"), sem("c_qk_in1")]
        v_in = [sem(f"c_v_in{j}") for j in range(UNROLL)]
        stored = [sem(f"c_stored{j}") for j in range(UNROLL)]
        zeroed = sem("c_zeroed")
        windows_out = sem("c_windows_out")
        first_set = sem("c_first_set")
        tqk_done = sem("c_tqk_done")
        q_evacd = sem("c_q_evacd")
        k_evacd = sem("c_k_evacd")
        o_evacd = sem("c_o_evacd")
        qk_done = sem("c_qk_done")
        turns = sem("c_turns")
        masked = sem("c_masked")
        maxed = sem("c_maxed")
        exp_done = sem("c_exp_done")
        pt_done = sem("c_pt_done")
        pt_evacd_act = sem("c_pt_evacd_act")
        pt_evacd_dve = sem("c_pt_evacd_dve")
        pv_done = sem("c_pv_done")

        def loops(eng, body):
            for nth, g in enumerate((1, 0, 2)):
                with eng.Fori(0, NT // UNROLL) as i:
                    body(g, NT * nth + UNROLL * i, i)

        with nc.Block() as block:
            def evac_of(n0, w):
                return (pt_evacd_dve if w % 2 else pt_evacd_act), LEAD + 2 * n0 + w // 2 + 1

            def evac(eng, copy, n0, w, done, near):
                eng.wait_ge(pt_done, LEAD + 4 * n0 + w + 1)
                eng.wait_ge(pv_done, LEAD + 4 * n0 + w - 1)
                if near:
                    copy(pT[:, w % 2, 1::2, :], p_t[:, w % 2, 1::2, :]).then_inc(done, 1)
                else:
                    copy(pT[:, w % 2, :, :], p_t[:, w % 2, :, :]).then_inc(done, 1)


            @block.sync
            def _(sp):
                sp.dma_start(mask[:, :, :], A["masks"]).then_inc(mask_in, 16)

                def body(g, n0, i):
                    dil, nblk = GROUPS[g]
                    for j in range(UNROLL):
                        n = n0 + j
                        if g == 0:
                            rows = TMs[ds((UNROLL * i + j) * P, P), :]
                        elif g == 1:
                            rows = TMs[0:SEQ, :].rearrange("(a r) e -> r a e", r=dil)[ds(i, 1), j * P:(j + 1) * P, :]
                            rows = rows.rearrange("r a e -> (r a) e")
                        else:
                            rows = TMs[0:SEQ, :].rearrange("(a r) e -> r a e", r=dil)[ds(UNROLL * i + j, 1), :, :]
                            rows = rows.rearrange("r a e -> (r a) e")
                        sp.wait_ge(tqk_done, LEAD + 2 * (n - 2) + 2)
                        for a in range(2):
                            sp.dma_start(qk[:, j % 2, a, :], rows[:, (3 * a + g) * CH:(3 * a + g + 1) * CH]
                                         ).then_inc(qk_in[j % 2], 16)
                        sp.wait_ge(pv_done, LEAD + 4 * (n - 3) + 4)
                        if j == UNROLL - 1:
                            sp.wait_ge(zeroed, 2)
                        sp.dma_start(v[:, j, :], rows[:, (6 + g) * CH:(7 + g) * CH]).then_inc(v_in[j], 16)

                for j in range(UNROLL):
                    sp.sem_inc(stored[j], 16)
                loops(sp, body)
                for j in range(UNROLL):
                    sp.wait_ge(stored[j], 16 + 16 * 3 * NT // UNROLL)

            @block.gpsimd
            def _(pool):
                nc.gpsimd.memset(kT[:, :, 0, :], 0.0).then_inc(zeroed, 1)
                nc.gpsimd.memset(v[:, UNROLL - 1, :], 0.0).then_inc(zeroed, 1)
                E.new_key_scores(nc, pool, A, S, kn, qn)
                store_windows(pool, S, O, windows_out)
                pool.wait_ge(windows_out, 12 * 16)

            @block.tensor
            def _(pe):
                for s in (tqk_done, qk_done, pt_done, pv_done):
                    pe.sem_inc(s, LEAD)
                pe.wait_ge(zeroed, 2)

                def transposes(n, j, a):
                    if a == 0:
                        pe.wait_ge(qk_in[j % 2], 16 * (n - j) + 32 * (j // 2) + 32)
                        pe.wait_ge(k_evacd, LEAD + n)
                    else:
                        pe.wait_ge(q_evacd, LEAD + n + 1)
                    for c in range(4):
                        last = nc.tensor.transpose(p_qk[:, c * P:(c + 1) * P],
                                                   qk[:, j % 2, a, c * P:(c + 1) * P], ident[:, :])
                    last.then_inc(tqk_done, 1)

                def body(g, n0, i):
                    near = g == 2

                    def scores(w):
                        j, c = divmod(w, 4)
                        if c == 0:
                            pe.wait_ge(q_evacd, LEAD + n0 + j + 1)
                            pe.wait_ge(k_evacd, LEAD + n0 + j + 1)
                        pe.wait_ge(masked, LEAD + 4 * n0 + w - 1)
                        for h in range(2):
                            rows = slice(HD * h, HD * h + HD)
                            keys = kT[rows, c, j + 1:j + 2, :] if near else kT[rows, c, j:j + 2, :]
                            out = p_s[:, h, w % 2, P if near else 0:2 * P]
                            last = nc.tensor.matmul(out, qT[rows, j % 2, c, :], keys, start=True, stop=True)
                        last.then_inc(qk_done, 1)

                    def transpose_p(w):
                        pe.wait_ge(exp_done, LEAD + 4 * n0 + w + 1)
                        pe.wait_ge(*evac_of(n0, w - 2))
                        for h in range(2):
                            for b in ((1,) if near else (0, 1)):
                                last = nc.tensor.transpose(p_t[:, w % 2, 2 * h + b, :],
                                                           p[:, w % 2, h, b * P:(b + 1) * P], ident[:, :])
                        last.then_inc(pt_done, 1)

                    def sums(w):
                        j, c = divmod(w, 4)
                        pe.wait_ge(*evac_of(n0, w))
                        if c == 0:
                            pe.wait_ge(v_in[j], 4 * n0 + 16)
                            pe.wait_ge(o_evacd, LEAD + n0 + j)
                        for h in range(2):
                            cols = slice((2 * c + h) * HD, (2 * c + h + 1) * HD)
                            for b in ((1,) if near else (0, 1)):
                                vb = v[:, j if b else (j - 1) % UNROLL, cols]
                                last = nc.tensor.matmul(p_o[:, 2 * c + h, :], pT[:, w % 2, 2 * h + b, :], vb,
                                                        start=(b == 1 if near else b == 0), stop=(b == 1))
                        last.then_inc(pv_done, 1)

                    transposes(n0, 0, 0)
                    transposes(n0, 0, 1)
                    N = 4 * UNROLL
                    for w in range(N + 2):
                        if w < N:
                            scores(w)
                        if w % 4 in (1, 2) and w // 4 + 1 < UNROLL:
                            transposes(n0 + w // 4 + 1, w // 4 + 1, w % 4 - 1)
                        if 1 <= w <= N:
                            transpose_p(w - 1)
                        if w >= 2:
                            sums(w - 2)

                loops(pe, body)

            @block.scalar
            def _(act):
                for s in (q_evacd, o_evacd, exp_done, pt_evacd_act):
                    act.sem_inc(s, LEAD)

                def store(g, n, i, j):
                    dil, _ = GROUPS[g]
                    act.wait_ge(o_evacd, LEAD + n + 1)
                    out = OG[0:SEQ, g, :]
                    if g == 0:
                        out = out[ds((UNROLL * i + j) * P, P), :]
                    else:
                        out = out.rearrange("(a r) e -> r a e", r=dil)
                        out = out[ds(i, 1), j * P:(j + 1) * P, :] if g == 1 else out[ds(UNROLL * i + j, 1), :, :]
                        out = out.rearrange("r a e -> (r a) e")
                    act.dma_start(out, og[:, j, :]).then_inc(stored[j], 16)

                def body(g, n0, i):
                    near = g == 2

                    def q_evac(n, j):
                        act.wait_ge(tqk_done, LEAD + 2 * n + 1)
                        act.wait_ge(qk_done, LEAD + 4 * (n - 1))
                        nc.scalar.copy(qT[:, j % 2, :, :], p_qk[:, :]).then_inc(q_evacd, 1)

                    def exps(w):
                        j, c = divmod(w, 4)
                        act.wait_ge(maxed, LEAD + 4 * n0 + w + 1)
                        act.wait_ge(pt_done, LEAD + 4 * n0 + w - 1)
                        lo = P if near else 0
                        for h in range(2):
                            hh = 2 * c + h
                            last = nc.scalar.activation(p[:, w % 2, h, lo:], sm[:, w % 2, h, lo:], ACT.Exp,
                                                        bias=og[:, j, CH + hh:CH + hh + 1],
                                                        accum_out=og[:, j, CH + NH + hh:CH + NH + hh + 1])
                        last.then_inc(exp_done, 1)

                    def o_evac(j):
                        act.wait_ge(pv_done, LEAD + 4 * (n0 + j) + 4)
                        nc.scalar.copy(og[:, j, 0:CH], p_o[:, :, :]).then_inc(o_evacd, 1)

                    q_evac(n0, 0)
                    N = 4 * UNROLL
                    for w in range(N + 2):
                        if w < N:
                            exps(w)
                        if w % 4 == 1 and w // 4 + 1 < UNROLL:
                            q_evac(n0 + w // 4 + 1, w // 4 + 1)
                        if 1 <= w <= N and (w - 1) % 2 == 0:
                            evac(act, nc.scalar.copy, n0, w - 1, pt_evacd_act, near)
                        if w >= 2 and (w - 2) % 4 == 3:
                            o_evac((w - 2) // 4)
                            store(g, n0 + (w - 2) // 4, i, (w - 2) // 4)

                loops(act, body)

            @block.vector
            def _(dve):
                for s in (k_evacd, masked, maxed, pt_evacd_dve):
                    dve.sem_inc(s, LEAD)
                dve.wait_ge(mask_in, 16)
                dve.wait_ge(zeroed, 2)
                nc.vector.tensor_copy(first[:, :], mask[:, 0, :]).then_inc(first_set, 1)
                dve.wait_ge(first_set, 1)

                def body(g, n0, i):
                    near = g == 2

                    def k_evac(n, j):
                        dve.wait_ge(tqk_done, LEAD + 2 * n + 2)
                        dve.wait_ge(qk_done, LEAD + 4 * n - 4 * (UNROLL - 2))
                        src = p_qk[:, :].rearrange("p (c k) -> p c k", c=4)
                        last = nc.vector.tensor_copy(kT[:, :, j + 1, :], src)
                        if j == UNROLL - 1:
                            last = nc.vector.tensor_copy(kT[:, :, 0, :], src)
                        last.then_inc(k_evacd, 1)

                    def mask_and_max(w):
                        j, c = divmod(w, 4)
                        dve.wait_ge(qk_done, LEAD + 4 * n0 + w + 1)
                        dve.wait_ge(exp_done, LEAD + 4 * n0 + w - 1)
                        if c == 0:
                            dve.wait_ge(stored[j], 4 * n0 + 16)
                        dve.sem_inc(turns, 1)
                        lo = P if near else 0
                        m = first[:, lo:] if j == 0 else mask[:, 1, lo:]
                        for h in range(2):
                            last = nc.vector.tensor_tensor_reduce(
                                out=sm[:, w % 2, h, lo:], in0=p_s[:, h, w % 2, lo:2 * P], in1=m, scale=HD ** -0.5,
                                scalar=LOWEST, op0=ALU.add, op1=ALU.max, accum_out=mx[:, w % 2, h:h + 1])
                        last.then_inc(masked, 1)
                        dve.wait_ge(masked, LEAD + 4 * n0 + w + 1)
                        nc.vector.tensor_scalar(og[:, j, CH + 2 * c:CH + 2 * c + 2], mx[:, w % 2, :], -1.0, None,
                                                ALU.mult).then_inc(maxed, 1)

                    k_evac(n0, 0)
                    N = 4 * UNROLL
                    for w in range(N + 2):
                        if w < N:
                            mask_and_max(w)
                        if w % 4 == 2 and w // 4 + 1 < UNROLL:
                            k_evac(n0 + w // 4 + 1, w // 4 + 1)
                        if 1 <= w <= N and (w - 1) % 2 == 1:
                            evac(dve, nc.vector.tensor_copy, n0, w - 1, pt_evacd_dve, near)
                        if w == 4 and g == 0:
                            nc.vector.tensor_copy(first[:, :], mask[:, 1, :])

                loops(dve, body)


GH, GK, GV_W = 4, 64, 128
CHUNK = 64
TAU = 16.0


def log_gates(nc, act, dve, z, e, done, z_ready, base=0):
    if dve is not None:
        nc.vector.scalar_tensor_tensor(out=e, in0=z, scalar=-1.0, in1=z, op0=ALU.mult, op1=ALU.min
                                       ).then_inc(done, 1)
        dve.wait_ge(done, base + 3)
        nc.vector.scalar_tensor_tensor(out=z, in0=z, scalar=0.0, in1=e, op0=ALU.min,
                                       op1=ALU.subtract).then_inc(done, 1)
        dve.wait_ge(done, base + 4)
    if act is not None:
        act.wait_ge(done, base + 1)
        nc.scalar.activation(e, e, ACT.Exp).then_inc(done, 1)
        act.wait_ge(done, base + 2)
        nc.scalar.activation(e, e, ACT.Ln, bias=1.0).then_inc(done, 1)


def gla_prompt(nc, A, S, O, ident):
    TMs, FMs, GLs, OL = S["tm"], S["fm"], S["gl"], S["ol"]
    NP = GH // 2
    st, sb, pb, sem = scope(nc)
    with st:
        wa = sb("d_wa", [RANK, GH * GK])
        ba = sb("d_ba", [P, NP])
        glr = sb("d_glr", [RANK, SEQ])
        z = sb("d_z", [P, NP, SEQ])
        e = sb("d_e", [P, NP, SEQ])
        keep = sb("d_keep", [P, NP, SEQ])
        b = sb("d_b", [P, NP, SEQ])
        eb = sb("d_eb", [P, NP, SEQ])
        enb = sb("d_enb", [P, NP, SEQ])
        ed = sb("d_ed", [P, NP, SEQ])
        decay = sb("d_decay", [P, NP, SEQ // CHUNK])
        qk = sb("d_qk", [P, 2, 2, NP, P])
        v = sb("d_v", [P, 2, GH * GV_W])
        qe = sb("d_qe", [P, 2, NP, P])
        ke = sb("d_ke", [P, 2, NP, P])
        kd = sb("d_kd", [P, 2, NP, P])
        kdT = sb("d_kdT", [P, 2, NP, P])
        att = sb("d_att", [P, 2, 2, NP, P])
        state = sb("d_state", [P, NP, 2 * GV_W])
        out = sb("d_out", [P, 2, GH * GV_W])
        cmask = sb("d_cmask", [P, P], U32)
        p_kd = pb("d_p_kd", [P, NP, P])
        p_att = pb("d_p_att", [P, 2, CH])
        p_o = pb("d_p_o", [P, 2, GH * GV_W])
        p_u = pb("d_p_u", [P, NP, 2 * GV_W])
        const_in = sem("d_const_in")
        qk_in = [sem("d_qk_in0"), sem("d_qk_in1")]
        v_in = [sem("d_v_in0"), sem("d_v_in1")]
        stored = [sem("d_stored0"), sem("d_stored1")]
        state_out = sem("d_state_out")
        cleared = sem("d_cleared")
        gate_mm = sem("d_gate_mm")
        gate_z = sem("d_gate_z")
        gate = sem("d_gate")
        summed = sem("d_summed")
        e_ready = sem("d_e_ready")
        scaled = sem("d_scaled")
        turns = sem("d_turns")
        kd_done = sem("d_kd_done")
        kd_evacd = sem("d_kd_evacd")
        att_done = sem("d_att_done")
        att_masked = sem("d_att_masked")
        o_done = sem("d_o_done")
        o_evacd = sem("d_o_evacd")
        u_done = sem("d_u_done")
        st_done = sem("d_st_done")

        with nc.Block() as block:

            @block.sync
            def _(sp):
                for dst, src in ((glr, GLs), (wa, A["w_gla_a2"].rearrange("a r k -> (a r) k")), (ba, A["b_gla_a"]),
                                 (cmask, A["chunk_mask"])):
                    sp.dma_start(dst[:, :], src).then_inc(const_in, 16)
                for s in range(2):
                    sp.sem_inc(stored[s], 16)
                with sp.Fori(0, NT // 2) as i:
                    for s in range(2):
                        n = 2 * i + s
                        sp.wait_ge(scaled, LEAD + n - 1)
                        for a, row in ((0, FM_GQ), (1, FM_GK)):
                            sp.dma_start(qk[:, s, a, :, :], FMs[row:row + NP * P, :].rearrange(
                                "(a p) t -> p a t", p=P)[:, :, ds(n * P, P)]).then_inc(qk_in[s], 16)
                        sp.wait_ge(o_done, LEAD + n - 1)
                        sp.dma_start(v[:, s, :], TMs[ds(n * P, P), TM_GV * CH:(TM_GV + 1) * CH]).then_inc(v_in[s], 16)
                sp.wait_ge(st_done, LEAD + 2 * NT)
                for h in range(GH):
                    r = slice(GK * (h % 2), GK * (h % 2) + GK)
                    sp.dma_start(O["gla_prompt"][0, 0, h], state[r, h // 2, GV_W * (h % 2):GV_W * (h % 2) + GV_W]
                                 ).then_inc(state_out, 16)
                sp.wait_ge(state_out, 16 * GH)
                for s in range(2):
                    sp.wait_ge(stored[s], 16 + 16 * NT // 2)

            @block.gpsimd
            def _(pool):
                nc.gpsimd.memset(keep[:, :, :], 1.0).then_inc(cleared, 1)
                pool.wait_ge(cleared, 1)
                nc.gpsimd.memset(keep[:, :, :].rearrange("p a (c t) -> p (a c) t", t=CHUNK)[:, :, 0:1], 0.0
                                 ).then_inc(cleared, 1)
                nc.gpsimd.memset(att[:, :, :, :, :], 0.0).then_inc(cleared, 1)
                nc.gpsimd.memset(state[:, :, :], 0.0).then_inc(cleared, 1)

            @block.tensor
            def _(pe):
                for s in (kd_done, att_done, o_done, u_done):
                    pe.sem_inc(s, LEAD)
                pe.wait_ge(const_in, 64)
                for a in range(NP):
                    for c in range(SEQ // CH):
                        k = (SEQ // CH) * a + c
                        if k >= 2:
                            pe.wait_ge(gate_z, k - 1)
                        nc.tensor.matmul(p_o[:, k % 2, :], wa[:, a * P:(a + 1) * P], glr[:, c * CH:(c + 1) * CH],
                                         start=True, stop=True).then_inc(gate_mm, 1)
                pe.wait_ge(gate_z, NP * SEQ // CH)
                pe.wait_ge(cleared, 4)
                with pe.Fori(0, NT // 2) as i:
                    for s in range(2):
                        n = 2 * i + s
                        pe.wait_ge(scaled, LEAD + n + 1)
                        pe.wait_ge(kd_evacd, LEAD + n)
                        for a in range(NP):
                            last = nc.tensor.transpose(p_kd[:, a, :], kd[:, s, a, :], ident[:, :])
                        last.then_inc(kd_done, 1)
                        pe.wait_ge(att_masked, LEAD + n)
                        for a in range(NP):
                            for h in range(2):
                                r = slice(GK * h, GK * h + GK)
                                last = nc.tensor.matmul(p_att[:, h, a * P:(a + 1) * P], ke[r, s, a, :], qe[r, s, a, :],
                                                        start=True, stop=True)
                        last.then_inc(att_done, 1)
                        pe.wait_ge(v_in[s], 16 * i + 16)
                        pe.wait_ge(o_evacd, LEAD + n - 1)
                        pe.wait_ge(kd_evacd, LEAD + n + 1)
                        for c in range(2):
                            t = slice(CHUNK * c, CHUNK * c + CHUNK)
                            pe.wait_ge(st_done, LEAD + 2 * n + c)
                            for a in range(NP):
                                cols = slice(2 * GV_W * a, 2 * GV_W * (a + 1))
                                nc.tensor.matmul(p_o[t, s, cols], qe[:, s, a, t], state[:, a, :], start=(a == 0),
                                                 stop=False)
                            for a in range(NP):
                                cols = slice(2 * GV_W * a, 2 * GV_W * (a + 1))
                                last = nc.tensor.matmul(p_u[:, a, :], kdT[t, s, a, :], v[t, s, cols], start=True,
                                                        stop=True)
                            last.then_inc(u_done, 1)
                        pe.wait_ge(att_masked, LEAD + n + 1)
                        for h in range(GH):
                            cols = slice(GV_W * h, GV_W * (h + 1))
                            last = nc.tensor.matmul(p_o[:, s, cols], att[:, s, h % 2, h // 2, :], v[:, s, cols],
                                                    start=False, stop=(h == GH - 1))
                        last.then_inc(o_done, 1)

            @block.scalar
            def _(act):
                for s in (kd_evacd, o_evacd):
                    act.sem_inc(s, LEAD)
                log_gates(nc, act, None, z[:, :, :], e[:, :, :], gate, None)
                act.wait_ge(summed, 1)
                nc.scalar.activation(eb[:, :, :], b[:, :, :], ACT.Exp, scale=1.0 / TAU).then_inc(e_ready, 1)
                nc.scalar.activation(enb[:, :, :], b[:, :, :], ACT.Exp, scale=-1.0 / TAU).then_inc(e_ready, 1)
                ends = b[:, :, :].rearrange("p a (c t) -> p a c t", t=CHUNK)[:, :, :, CHUNK - 1]
                nc.scalar.activation(decay[:, :, :], ends, ACT.Exp, scale=1.0 / TAU).then_inc(e_ready, 1)
                act.wait_ge(summed, 2)
                nc.scalar.activation(ed[:, :, :], e[:, :, :], ACT.Exp, scale=-1.0 / TAU).then_inc(e_ready, 1)

                with act.Fori(0, NT // 2) as i:
                    for s in range(2):
                        n = 2 * i + s
                        act.wait_ge(kd_done, LEAD + n + 1)
                        act.wait_ge(u_done, LEAD + 2 * (n - 1))
                        nc.scalar.copy(kdT[:, s, :, :], p_kd[:, :, :]).then_inc(kd_evacd, 1)
                        act.wait_ge(o_done, LEAD + n + 1)
                        act.wait_ge(stored[s], 16 * i + 16)
                        nc.scalar.copy(out[:, s, :], p_o[:, s, :]).then_inc(o_evacd, 1)
                        act.wait_ge(o_evacd, LEAD + n + 1)
                        act.dma_start(OL[ds(n * P, P), :], out[:, s, :]).then_inc(stored[s], 16)

            @block.vector
            def _(dve):
                for s in (scaled, att_masked, st_done):
                    dve.sem_inc(s, LEAD)
                for k in range(NP * SEQ // CH):
                    a, c = divmod(k, SEQ // CH)
                    dve.wait_ge(gate_mm, k + 1)
                    nc.vector.tensor_scalar(z[:, a, c * CH:(c + 1) * CH], p_o[:, k % 2, :], ba[:, a:a + 1], None,
                                            ALU.add).then_inc(gate_z, 1)
                dve.wait_ge(gate_z, NP * SEQ // CH)
                log_gates(nc, None, dve, z[:, :, :], e[:, :, :], gate, None)
                dve.wait_ge(cleared, 4)
                flat = lambda x: x[:, :, :].rearrange("p a t -> p (a t)")
                nc.vector.tensor_tensor_scan(flat(b), flat(keep), flat(z), 0.0, ALU.mult, ALU.add).then_inc(summed, 1)
                dve.wait_ge(summed, 1)
                chunks = lambda x: x[:, :, :].rearrange("p a (c t) -> p (a c) t", t=CHUNK)
                nc.vector.tensor_tensor(chunks(e), chunks(b), chunks(b)[:, :, CHUNK - 1:CHUNK].to_broadcast(
                    [P, NP * SEQ // CHUNK, CHUNK]), ALU.subtract).then_inc(summed, 1)
                dve.wait_ge(e_ready, 4)
                with dve.Fori(0, NT // 2) as i:
                    for s in range(2):
                        n = 2 * i + s
                        dve.wait_ge(qk_in[s], 32 * i + 32)
                        dve.wait_ge(o_done, LEAD + n - 1)
                        t = ds(n * P, P)
                        nc.vector.scalar_tensor_tensor(out=qe[:, s, :, :], in0=qk[:, s, 0, :, :], scalar=GK ** -0.5,
                                                       in1=eb[:, :, t], op0=ALU.mult, op1=ALU.mult)
                        nc.vector.tensor_tensor(ke[:, s, :, :], qk[:, s, 1, :, :], enb[:, :, t], ALU.mult)
                        nc.vector.tensor_tensor(kd[:, s, :, :], qk[:, s, 1, :, :], ed[:, :, t],
                                                ALU.mult).then_inc(scaled, 1)
                        dve.wait_ge(att_done, LEAD + n + 1)
                        dve.sem_inc(turns, 1)
                        for h in range(2):
                            last = nc.vector.copy_predicated(
                                att[:, s, h, :, :], cmask[:, :].unsqueeze(1).to_broadcast([P, NP, P]),
                                p_att[:, h, 0:NP * P].rearrange("p (a t) -> p a t", a=NP))
                        last.then_inc(att_masked, 1)
                        for c in range(2):
                            dve.wait_ge(u_done, LEAD + 2 * n + c + 1)
                            for h in range(GH):
                                a, r = h // 2, slice(GK * (h % 2), GK * (h % 2) + GK)
                                cols = slice(GV_W * (h % 2), GV_W * (h % 2) + GV_W)
                                last = nc.vector.scalar_tensor_tensor(
                                    out=state[r, a, cols], in0=state[r, a, cols], scalar=decay[r, a, ds(2 * n + c, 1)],
                                    in1=p_u[r, a, cols], op0=ALU.mult, op1=ALU.add)
                            last.then_inc(st_done, 1)
                            dve.wait_ge(st_done, LEAD + 2 * n + c + 1)


class Chain:

    def __init__(self, eng, done, at):
        self.eng, self.done, self.at, self.links = eng, done, at, 0

    def __call__(self, instruction):
        instruction.then_inc(self.done, 1)
        self.links += 1
        self.eng.wait_ge(self.done, self.at + self.links)


def merge(nc, A, S, O, ident):
    TMs, OG, OL = S["tm"], S["og"], S["ol"]
    TILES = NT + 1
    G4 = D // 2 // P
    st, sb, pb, sem = scope(nc)
    with st:
        wb_hi = sb("f_wb_hi", [P, 2, G4, D], F32R)
        wb_lo = sb("f_wb_lo", [P, 2, G4, D], F32R)
        wo_hi = sb("f_wo_hi", [P, KC, D], F32R)
        wo_lo = sb("f_wo_lo", [P, KC, D], F32R)
        gates = sb("f_gates", [P, 2, 6 * CH])
        og = sb("f_og", [P, 3, OG_W])
        ol = sb("f_ol", [P, CH])
        x = sb("f_x", [P, 2, D])
        sg = sb("f_sg", [P, 2 * CH])
        bT_hi = sb("f_bT_hi", [P, 2, G4, P], F32R)
        bT_lo = sb("f_bT_lo", [P, 2, G4, P], F32R)
        mT_hi = sb("f_mT_hi", [P, KC, P], F32R)
        mT_lo = sb("f_mT_lo", [P, KC, P], F32R)
        y = sb("f_y", [P, D])
        fw = sb("f_fw", [P, D])
        gw = sb("f_gw", [P, 1])
        junk = sb("f_junk", [P, GV_W])
        low = sb("f_low", [P, NH])
        wg = sb("f_wg", [P, 3, NH])
        wd = sb("f_wd", [P, 3, NH])
        den = sb("f_den", [P, 2, NH])
        gn = sb("f_gn", [P, 6, GH])
        fn = sb("f_fn", [P, 6])
        p_t = pb("f_p_t", [P, 2, CH])
        p_b = pb("f_p_b", [P, 2, D])
        p_z = pb("f_p_z", [P, D])

        const_in = sem("f_const_in")
        raw_in = [sem("f_raw_in0"), sem("f_raw_in1")]
        w_hi_done = sem("f_w_hi_done")
        w_lo_done = sem("f_w_lo_done")
        gw_done = sem("f_gw_done")
        gates_in = [sem("f_gates_in0"), sem("f_gates_in1")]
        x_in = [sem("f_x_in0"), sem("f_x_in1")]
        og_in = sem("f_og_in")
        ol_in = sem("f_ol_in")
        stored = sem("f_stored")
        sig_done = sem("f_sig_done")
        diff_done = sem("f_diff_done")
        wexp_done = sem("f_wexp_done")
        gms_done = sem("f_gms_done")
        groot_done = sem("f_groot_done")
        branches = sem("f_branches")
        prep = sem("f_prep")
        t1_done = sem("f_t1_done")
        hi1_done = sem("f_hi1_done")
        lo1_done = sem("f_lo1_done")
        g1_done = sem("f_g1_done")
        mixing = sem("f_mixing")
        silu_done = sem("f_silu_done")
        turns = sem("f_turns")
        mixed = sem("f_mixed")
        t2_done = sem("f_t2_done")
        hi2_done = sem("f_hi2_done")
        lo2_done = sem("f_lo2_done")
        g2_done = sem("f_g2_done")
        y_done = sem("f_y_done")
        sq_done = sem("f_sq_done")
        fms_done = sem("f_fms_done")
        froot_done = sem("f_froot_done")
        fin = sem("f_fin")
        y_ready = sem("f_y_ready")
        L = LEAD
        PREP, FIN = 17, 4

        def rows(t):
            return slice(SEQ - NS, TOK) if isinstance(t, int) and t == NT else ds(t * P, P)

        def has(t):
            return not isinstance(t, int) or 0 <= t < TILES

        pieces = [("b", a, c) for a in range(2) for c in range(0, G4, 2)] + [("o", 0, c) for c in range(0, KC, 2)]

        def piece(n):
            kind, a, c = pieces[n]
            raw = gates[:, n % 2, 0:2 * D].rearrange("p (c e) -> p c e", c=2)
            if kind == "b":
                return raw, wb_hi[:, a, c:c + 2, :], wb_lo[:, a, c:c + 2, :], \
                    A["w_attn_out" if a == 0 else "w_gla_out"], c
            return raw, wo_hi[:, c:c + 2, :], wo_lo[:, c:c + 2, :], A["w_out"], c

        with nc.Block() as block:

            @block.sync
            def _(sp):
                sp.dma_start(fw[:, :], A["final_norm_w"].rearrange("(a d) -> a d", a=1).to_broadcast([P, D])
                             ).then_inc(const_in, 16)
                sp.dma_start(gw[:, :], A["gla_norm_w"].rearrange("a (p b) -> p (a b)", b=1)).then_inc(const_in, 16)
                for n in range(len(pieces)):
                    raw, _, _, src, c = piece(n)
                    if n >= 2:
                        sp.wait_ge(w_lo_done, n - 1)
                    sp.dma_start(raw, src.rearrange("a (c p) e -> p (a c) e", p=P)[:, c:c + 2, :]
                                 ).then_inc(raw_in[n % 2], 16)

                def load(t, s):
                    sp.wait_ge(t2_done, L + t - 1)
                    sp.dma_start(gates[:, s, :], TMs[rows(t), TM_AZ * CH:]).then_inc(gates_in[s], 16)
                    sp.wait_ge(branches, L + t)
                    sp.dma_start(og[:, :, :], OG[rows(t), :, :]).then_inc(og_in, 16)
                    sp.dma_start(ol[:, :], OL[rows(t), :]).then_inc(ol_in, 16)

                def load_x(t, s):
                    sp.wait_ge(sq_done, L + t - 1)
                    if isinstance(t, int) and t == NT:
                        sp.dma_start(x[0:NS, s, :], A["x_prompt"][0, SEQ - NS:SEQ, :]).then_inc(x_in[s], 16)
                        sp.dma_start(x[NS:P, s, :], A["x_sample"].rearrange("b t d -> (b t) d")).then_inc(x_in[s], 16)
                    else:
                        sp.dma_start(x[:, s, :], A["x_prompt"][0, rows(t), :]).then_inc(x_in[s], 16)

                sp.wait_ge(w_lo_done, len(pieces))
                load(0, 0)
                load(1, 1)
                load_x(0, 0)

                def step(t, s):
                    if has(t + 2):
                        load(t + 2, s)
                    if has(t + 1):
                        load_x(t + 1, 1 - s)

                step(0, 0)
                with sp.Fori(0, (TILES - 5) // 2) as i:
                    step(2 * i + 1, 1)
                    step(2 * i + 2, 0)
                for t in range(TILES - 4, TILES):
                    step(t, t % 2)
                sp.wait_ge(stored, 16 + 16 * TILES)

            @block.tensor
            def _(pe):
                for s in (t1_done, g1_done, t2_done, g2_done):
                    pe.sem_inc(s, L)

                def transpose_branches(t, s):
                    pe.wait_ge(branches, L + t + 1)
                    for a in range(2):
                        if a == 0:
                            pe.wait_ge(lo2_done, L + t - 1)
                        for c in range(G4):
                            last = nc.tensor.transpose(p_t[:, a, c * P:(c + 1) * P],
                                                       gates[:, s, (G4 * a + c) * P:(G4 * a + c + 1) * P], ident[:, :])
                    last.then_inc(t1_done, 1)

                def product(out, stat_hi, stat_lo, mov_hi, mov_lo, first, last):
                    nc.tensor.matmul(out, stat_hi, mov_hi, start=first, stop=False)
                    nc.tensor.matmul(out, stat_hi, mov_lo, start=False, stop=False)
                    return nc.tensor.matmul(out, stat_lo, mov_hi, start=False, stop=last)

                def step(t, s):
                    if isinstance(t, int) and t == 0:
                        pe.wait_ge(w_lo_done, len(pieces))
                        transpose_branches(0, 0)
                    pe.wait_ge(lo1_done, L + t + 1)
                    pe.wait_ge(mixed, L + t)
                    for a in range(2):
                        for e in range(0, D, CH):
                            for c in range(G4):
                                last = product(p_b[:, a, e:e + CH], bT_hi[:, a, c, :], bT_lo[:, a, c, :],
                                               wb_hi[:, a, c, e:e + CH], wb_lo[:, a, c, e:e + CH], c == 0, c == G4 - 1)
                    last.then_inc(g1_done, 1)
                    if has(t + 1):
                        transpose_branches(t + 1, 1 - s)
                    if has(t - 1):
                        out_product(t - 1)
                    pe.wait_ge(mixed, L + t + 1)
                    if has(t + 1):
                        pe.wait_ge(lo1_done, L + t + 2)
                    for c in range(KC):
                        last = nc.tensor.transpose(p_t[:, c // 4, (c % 4) * P:(c % 4 + 1) * P],
                                                   gates[:, s, 2 * CH + c * P:2 * CH + (c + 1) * P], ident[:, :])
                    last.then_inc(t2_done, 1)
                    if isinstance(t, int) and t == TILES - 1:
                        out_product(t)

                def out_product(t):
                    pe.wait_ge(lo2_done, L + t + 1)
                    pe.wait_ge(y_done, L + t)
                    for e in range(0, D, CH):
                        for c in range(KC):
                            last = product(p_z[:, e:e + CH], mT_hi[:, c, :], mT_lo[:, c, :],
                                           wo_hi[:, c, e:e + CH], wo_lo[:, c, e:e + CH], c == 0, c == KC - 1)
                    last.then_inc(g2_done, 1)

                step(0, 0)
                with pe.Fori(0, (TILES - 3) // 2) as i:
                    step(2 * i + 1, 1)
                    step(2 * i + 2, 0)
                step(TILES - 2, 1)
                step(TILES - 1, 0)

            @block.scalar
            def _(act):
                for s in (sig_done, wexp_done, groot_done, hi1_done, hi2_done, sq_done, froot_done):
                    act.sem_inc(s, L)
                act.sem_inc(stored, 16)
                for n in range(len(pieces)):
                    raw, hi, _, _, _ = piece(n)
                    if pieces[n][:2] == ("b", 1):
                        act.wait_ge(gw_done, n - 1)
                    else:
                        act.wait_ge(raw_in[n % 2], 16 * (n // 2) + 16)
                    nc.scalar.copy(hi, raw).then_inc(w_hi_done, 1)

                def prepare(t, s):
                    act.wait_ge(gates_in[s], 8 * (t - s) + 16)
                    act.wait_ge(branches, L + t)
                    nc.scalar.activation(sg[:, :], gates[:, s, 0:2 * CH], ACT.Sigmoid)
                    nc.scalar.activation(gates[:, s, 2 * CH:], gates[:, s, 2 * CH:], ACT.Sigmoid).then_inc(sig_done, 1)
                    act.wait_ge(diff_done, L + t + 1)
                    nc.scalar.activation(wg[:, :, :], wd[:, :, :], ACT.Exp).then_inc(wexp_done, 1)
                    act.wait_ge(gms_done, L + t + 1)
                    nc.scalar.activation(gn[:, 2, :], gn[:, 1, :], ACT.Sqrt).then_inc(groot_done, 1)

                def split_hi1(t):
                    act.wait_ge(t1_done, L + t + 1)
                    nc.scalar.copy(bT_hi[:, :, :, :], p_t[:, :, :]).then_inc(hi1_done, 1)

                def final(t, s):
                    act.wait_ge(y_done, L + t + 1)
                    nc.scalar.activation(x[:, s, :], y[:, :], ACT.Square, accum_out=fn[:, 0:1]).then_inc(sq_done, 1)
                    act.wait_ge(fms_done, L + t + 1)
                    nc.scalar.activation(fn[:, 2:3], fn[:, 1:2], ACT.Sqrt).then_inc(froot_done, 1)
                    act.wait_ge(y_ready, L + t + 1)
                    if isinstance(t, int) and t == NT:
                        act.dma_start(O["y_sample"].rearrange("b t d -> (b t) d"), y[NS:P, :]).then_inc(stored, 16)
                    else:
                        act.dma_start(O["y_prompt"][0, rows(t), :], y[:, :]).then_inc(stored, 16)

                def step(t, s):
                    if isinstance(t, int) and t == 0:
                        prepare(0, 0)
                        split_hi1(0)
                        prepare(1, 1)
                    if has(t + 1):
                        split_hi1(t + 1)
                    if has(t - 1):
                        final(t - 1, 1 - s)
                    act.wait_ge(t2_done, L + t + 1)
                    nc.scalar.copy(mT_hi[:, :, :], p_t[:, :, :]).then_inc(hi2_done, 1)
                    if has(t + 2):
                        prepare(t + 2, s)
                    if isinstance(t, int) and t == TILES - 1:
                        final(t, s)

                step(0, 0)
                with act.Fori(0, (TILES - 5) // 2) as i:
                    step(2 * i + 1, 1)
                    step(2 * i + 2, 0)
                for t in range(TILES - 4, TILES):
                    step(t, t % 2)

            @block.vector
            def _(dve):
                for s in (diff_done, gms_done, branches, lo1_done, mixed, lo2_done, y_done, fms_done, y_ready):
                    dve.sem_inc(s, L)
                dve.wait_ge(const_in, 32)
                for n in range(len(pieces)):
                    raw, hi, lo, _, _ = piece(n)
                    if pieces[n][:2] == ("b", 1):
                        dve.wait_ge(raw_in[n % 2], 16 * (n // 2) + 16)
                        nc.vector.tensor_scalar(raw, raw, gw[:, 0:1], None, ALU.mult).then_inc(gw_done, 1)
                    dve.wait_ge(w_hi_done, n + 1)
                    nc.vector.tensor_tensor(lo, raw, hi.bitcast(F32), ALU.subtract).then_inc(w_lo_done, 1)
                V = nc.vector

                def prepare(t, s):
                    link = Chain(dve, prep, PREP * t)
                    dve.wait_ge(og_in, 16 * t + 16)
                    nm, dn = og[:, :, CH:CH + NH], og[:, :, CH + NH:]
                    link(V.tensor_tensor(low[:, :], nm[:, 0, :], nm[:, 1, :], ALU.min))
                    link(V.tensor_tensor(low[:, :], low[:, :], nm[:, 2, :], ALU.min))
                    V.tensor_tensor(wd[:, :, :], low[:, :].unsqueeze(1).to_broadcast([P, 3, NH]), nm,
                                    ALU.subtract).then_inc(diff_done, 1)
                    dve.wait_ge(ol_in, 16 * t + 16)
                    for h in range(GH):
                        cols = slice(h * GV_W, (h + 1) * GV_W)
                        dve.sem_inc(turns, 1)
                        last = V.tensor_tensor_reduce(out=junk[:, :], in0=ol[:, cols], in1=ol[:, cols], scale=1.0,
                                                      scalar=0.0, op0=ALU.mult, op1=ALU.add, accum_out=gn[:, 0, h:h + 1])
                        link(last)
                    V.tensor_scalar(gn[:, 1, :], gn[:, 0, :], 1.0 / GV_W, EPS, ALU.mult, ALU.add).then_inc(gms_done, 1)
                    dve.wait_ge(wexp_done, L + t + 1)
                    link(V.tensor_tensor(wd[:, :, :], wg[:, :, :], dn, ALU.mult))
                    link(V.tensor_tensor(den[:, 0, :], wd[:, 0, :], wd[:, 1, :], ALU.add))
                    link(V.tensor_tensor(den[:, 0, :], den[:, 0, :], wd[:, 2, :], ALU.add))
                    link(V.reciprocal(den[:, 1, :], den[:, 0, :]))
                    link(V.tensor_tensor(wg[:, :, :], wg[:, :, :], den[:, 1:2, :].to_broadcast([P, 3, NH]), ALU.mult))
                    sums = og[:, :, 0:CH].rearrange("p g (h e) -> p g h e", h=NH)
                    link(V.tensor_tensor(sums, sums, wg[:, :, :].unsqueeze(3).to_broadcast([P, 3, NH, HD]), ALU.mult))
                    V.tensor_tensor(og[:, 0, 0:CH], og[:, 0, 0:CH], og[:, 1, 0:CH], ALU.add)
                    dve.wait_ge(groot_done, L + t + 1)
                    link(V.reciprocal(gn[:, 3, :], gn[:, 2, :]))
                    V.tensor_tensor(og[:, 0, 0:CH], og[:, 0, 0:CH], og[:, 2, 0:CH], ALU.add)
                    link(V.tensor_tensor(gn[:, 4, :], gn[:, 3, :], gn[:, 3, :], ALU.mult))
                    link(V.tensor_tensor(gn[:, 4, :], gn[:, 4, :], gn[:, 1, :], ALU.mult))
                    link(V.tensor_scalar(gn[:, 4, :], gn[:, 4, :], -0.5, 1.5, ALU.mult, ALU.add))
                    link(V.tensor_tensor(gn[:, 5, :], gn[:, 3, :], gn[:, 4, :], ALU.mult))
                    heads = ol[:, :].rearrange("p (h e) -> p h e", h=GH)
                    V.tensor_tensor(heads, heads, gn[:, 5, :].unsqueeze(2).to_broadcast([P, GH, GV_W]), ALU.mult)
                    dve.wait_ge(sig_done, L + t + 1)
                    link2 = V.tensor_tensor(gates[:, s, 0:2 * CH], gates[:, s, 0:2 * CH], sg[:, :], ALU.mult)
                    link2.then_inc(silu_done, 1)
                    dve.wait_ge(silu_done, t + 1)
                    V.tensor_tensor(gates[:, s, 0:CH], gates[:, s, 0:CH], og[:, 0, 0:CH], ALU.mult)
                    V.tensor_tensor(gates[:, s, CH:2 * CH], gates[:, s, CH:2 * CH], ol[:, :],
                                    ALU.mult).then_inc(branches, 1)
                    assert link.links == PREP, link.links

                def split_lo1(t):
                    dve.wait_ge(hi1_done, L + t + 1)
                    V.tensor_tensor(bT_lo[:, :, :, :], p_t[:, :, :].rearrange("p a (c t) -> p a c t", c=G4),
                                    bT_hi[:, :, :, :].bitcast(F32), ALU.subtract).then_inc(lo1_done, 1)

                def mix(t, s):
                    dve.wait_ge(g1_done, L + t + 1)
                    m = gates[:, s, 2 * CH:].rearrange("p (a e) -> p a e", a=2)
                    V.tensor_tensor(m, m, p_b[:, :, :], ALU.mult).then_inc(mixing, 1)
                    dve.wait_ge(mixing, t + 1)
                    V.tensor_tensor(m[:, 0, :], m[:, 0, :], m[:, 1, :], ALU.add).then_inc(mixed, 1)

                def final(t, s):
                    link = Chain(dve, fin, FIN * t)
                    dve.wait_ge(g2_done, L + t + 1)
                    dve.wait_ge(x_in[s], 8 * (t - s) + (32 if isinstance(t, int) and t == NT else 16))
                    dve.wait_ge(stored, 16 * t + 16)
                    V.tensor_tensor(y[:, :], x[:, s, :], p_z[:, :], ALU.add).then_inc(y_done, 1)
                    dve.wait_ge(sq_done, L + t + 1)
                    m = [fn[:, j:j + 1] for j in range(6)]
                    V.tensor_scalar(m[1], m[0], 1.0 / D, EPS, ALU.mult, ALU.add).then_inc(fms_done, 1)
                    dve.wait_ge(froot_done, L + t + 1)
                    rsqrt_steps(nc, dve, fin, FIN * t, m)
                    V.scalar_tensor_tensor(out=y[:, :], in0=y[:, :], scalar=m[2], in1=fw[:, :], op0=ALU.mult,
                                           op1=ALU.mult).then_inc(y_ready, 1)

                def step(t, s):
                    if isinstance(t, int) and t == 0:
                        prepare(0, 0)
                        split_lo1(0)
                        prepare(1, 1)
                    mix(t, s)
                    if has(t + 1):
                        split_lo1(t + 1)
                    if has(t - 1):
                        final(t - 1, 1 - s)
                    dve.wait_ge(hi2_done, L + t + 1)
                    V.tensor_tensor(mT_lo[:, :, :], p_t[:, :, :].rearrange("p a (c t) -> p (a c) t", c=4),
                                    mT_hi[:, :, :].bitcast(F32), ALU.subtract).then_inc(lo2_done, 1)
                    if has(t + 2):
                        prepare(t + 2, s)
                    if isinstance(t, int) and t == TILES - 1:
                        final(t, s)

                step(0, 0)
                with dve.Fori(0, (TILES - 5) // 2) as i:
                    step(2 * i + 1, 1)
                    step(2 * i + 2, 0)
                for t in range(TILES - 4, TILES):
                    step(t, t % 2)


ROWS = 2 * T * NH


class SampleBuffers:

    def __init__(self, sb, sem):
        self.vc = sb("e_vc", [P, 2, 2, NU, CH])
        self.vn = sb("e_vn", [2 * T, 2, 3, CH])
        self.sn = sb("e_sn", [NS, 3, 2, T * NH])
        self.mask = sb("e_mask", [P, 3, P + T])
        self.diag = sb("e_diag", [P, CH])
        self.const_in = sem("e_const_in")
        self.kn_in = sem("e_kn_in")
        self.qn_in = sem("e_qn_in")
        self.v_in = [sem("e_v_in0"), sem("e_v_in1")]
        self.link = sem("e_link")

    V_IN = 16 * (2 * 3 + 1)

    def load_v(self, eng, A, S, i, s):
        for b in range(2):
            for g in range(3):
                eng.dma_start(self.vc[:, s, b, UNIT0[g]:UNIT0[g] + UNITS[g], :], cached(A, g, 2 * i + b, 1)
                              ).then_inc(self.v_in[s], 16)
        eng.dma_start(self.vn[:, s, :, :], S["tm"][ds(SEQ + 2 * i * T, 2 * T), 6 * CH:9 * CH]
                      ).then_inc(self.v_in[s], 16)

    def new_key_scores(self, nc, pool, A, S, kn, qn):
        TS = S["tm"][SEQ:TOK, :]
        pool.dma_start(self.mask[:, :, :], A["dec_mask"]).then_inc(self.const_in, 16)
        pool.dma_start(self.diag[:, :], A["dec_diag"]).then_inc(self.const_in, 16)
        pool.dma_start(kn[:, :, :], TS[:, 3 * CH:6 * CH]).then_inc(self.kn_in, 16)
        for s in range(2):
            self.load_v(pool, A, S, s, s)
        pool.wait_ge(self.kn_in, 16)
        link = Chain(pool, self.link, 0)
        for g in range(3):
            for b in range(DB):
                src = TS[T * b:T * b + T, g * CH:(g + 1) * CH]
                pool.dma_start(qn[T * b:T * b + T, :, :], src.unsqueeze(0).to_broadcast([T, T, CH])
                               ).then_inc(self.qn_in, 16)
            pool.wait_ge(self.qn_in, 16 * DB * (g + 1))
            link(nc.gpsimd.tensor_tensor(qn[:, :, :], qn[:, :, :], kn[:, g:g + 1, :].to_broadcast([NS, T, CH]),
                                         ALU.mult))
            prod = qn[:, :, :].rearrange("p t (h e) -> p (t h) e", h=NH)
            half = HD // 2
            while half:
                if half > 1:
                    link(nc.gpsimd.tensor_tensor(prod[:, :, 0:half], prod[:, :, 0:half], prod[:, :, half:2 * half],
                                                 ALU.add))
                else:
                    for twice in range(2):
                        last = nc.gpsimd.tensor_tensor(self.sn[:, g, twice, :].unsqueeze(2), prod[:, :, 0:1],
                                                       prod[:, :, 1:2], ALU.add)
                    link(last)
                half //= 2


def attend_sample(nc, A, S, ident, sT, E):
    OG, OA = S["og"], S["oa"]
    NB = DB // 2
    vc, vn, sn, mask, diag = E.vc, E.vn, E.sn, E.mask, E.diag
    st, sb, pb, sem = scope(nc)
    with st:
        sp_ = sb("e_sp", [P, 2, 3, ROWS])
        snT = sb("e_snT", [P, 3, NS])
        sn2 = sb("e_sn2", [P, 2, 3, T])
        s = sb("e_s", [P, 2, 3, P + T])
        mx = sb("e_mx", [P, 2, 2, 3])
        nm = sb("e_nm", [P, 2, 3])
        dn = sb("e_dn", [P, 2, 3])
        lw = sb("e_lw", [P, 2, 1])
        wg = sb("e_wg", [P, 2, 3])
        wd = sb("e_wd", [P, 2, 3])
        ds_ = sb("e_ds", [P, 2])
        pn = sb("e_pn", [P, 2, 3, 2 * T])
        pnT = sb("e_pnT", [2 * T, 2, 3, P])
        pm0 = sb("e_pm0", [P, 2, ROWS])
        pm1 = sb("e_pm1", [P, 2, 2, 4 * 72])
        pm2 = sb("e_pm2", [P, 2, 2, 8 * 72])
        po = sb("e_po", [P, 3, CH])
        oa = sb("e_oa", [P, 2, HD])
        fill = sb("e_fill", [NS, 3, OG_W])
        p_s = pb("e_p_s", [P, 2, 4, P])
        p_sn = pb("e_p_sn", [P, 3, NS])
        p_p = pb("e_p_p", [P, 3, P])
        p_pn = pb("e_p_pn", [2 * T, 3, P])
        p_o = pb("e_p_o", [P, 3, CH])

        stored = [sem("e_stored0"), sem("e_stored1")]
        filled = sem("e_filled")
        cleared = sem("e_cleared")
        turns = sem("e_turns")
        chain = sem("e_chain")
        snT_done = sem("e_snT_done")
        picked = sem("e_picked")
        sT_done = sem("e_sT_done")
        maxed = sem("e_maxed")
        exp_done = sem("e_exp_done")
        wexp_done = sem("e_wexp_done")
        p_ready = sem("e_p_ready")
        pT_done = sem("e_pT_done")
        pm_done = sem("e_pm_done")
        pv_done = sem("e_pv_done")
        lowest = sem("e_lowest")
        out_ready = sem("e_out_ready")
        L = LEAD
        LINKS = 12

        with nc.Block() as block:

            @block.sync
            def _(sp):
                sp.wait_ge(cleared, 6)
                sp.dma_start(OG[SEQ:TOK, :, :], fill[:, :, :]).then_inc(filled, 16)
                sp.wait_ge(filled, 16)
                for k in range(2):
                    sp.wait_ge(stored[k], 16 + 16 * NB // 2)
                sp.dma_start(OG[SEQ:TOK, 0, 0:CH], OA.rearrange("(t h) e -> t (h e)", h=NH)).then_inc(filled, 16)
                sp.wait_ge(filled, 32)

            @block.gpsimd
            def _(pool):
                nc.gpsimd.memset(pn[:, :, :, :], 0.0).then_inc(cleared, 1)
                nc.gpsimd.memset(pm1[:, :, :, :], 0.0).then_inc(cleared, 1)
                nc.gpsimd.memset(pm2[:, :, :, :], 0.0).then_inc(cleared, 1)
                nc.gpsimd.memset(fill[:, :, :], 0.0).then_inc(cleared, 1)
                pool.wait_ge(cleared, 4)
                nc.gpsimd.memset(fill[:, 0, CH + NH:], 1.0).then_inc(cleared, 1)
                pool.sem_inc(cleared, 1)
                pool.wait_ge(cleared, 6)
                for n in range(2, NB):
                    pool.wait_ge(pv_done, L + n - 1)
                    E.load_v(pool, A, S, n, n % 2)

            @block.tensor
            def _(pe):
                for x in (sT_done, pT_done, pv_done):
                    pe.sem_inc(x, L)
                for g in range(3):
                    last = nc.tensor.transpose(p_sn[:, g, :], sn[:, g, :, :], ident[0:NS, 0:NS])
                last.then_inc(snT_done, 1)
                with pe.Fori(0, NB // 2) as i:
                    for k in range(2):
                        n = 2 * i + k
                        pe.wait_ge(picked, L + n + 1)
                        pe.wait_ge(maxed, L + n - 1)
                        for g in range(3):
                            last = nc.tensor.transpose(p_s[:, k, g, :], sp_[:, k, g, :], ident[:, :])
                        last.then_inc(sT_done, 1)
                    for k in range(2):
                        n = 2 * i + k
                        pe.wait_ge(p_ready, L + n + 1)
                        pe.wait_ge(pm_done, L + n)
                        for g in range(3):
                            nc.tensor.transpose(p_p[:, g, :], s[:, k, g, 0:P], ident[:, :])
                            last = nc.tensor.transpose(p_pn[:, g, :], pn[:, k, g, :], ident[:, :])
                        last.then_inc(pT_done, 1)
                        pe.wait_ge(pm_done, L + n + 1)
                        pe.wait_ge(E.v_in[k], E.V_IN * i + E.V_IN)
                        pe.wait_ge(out_ready, L + n)
                        for g in range(3):
                            nc.tensor.matmul(p_o[:, g, :], pnT[:, k, g, :], vn[:, k, g, :], start=True, stop=False)
                            for b in range(2):
                                for c in range(UNITS[g]):
                                    if g == 0:
                                        stat = pm0[:, k, 64 * b:64 * b + 64]
                                    else:
                                        stat = (pm1, pm2)[g - 1][:, k, b, 64 * c:64 * c + 64]
                                    last = nc.tensor.matmul(p_o[64 * b:64 * b + 64, g, :], stat,
                                                            vc[:, k, b, UNIT0[g] + c, :], start=False,
                                                            stop=(c == UNITS[g] - 1))
                        last.then_inc(pv_done, 1)

            @block.scalar
            def _(act):
                for x in (picked, exp_done, wexp_done, pm_done):
                    act.sem_inc(x, L)
                for k in range(2):
                    act.sem_inc(stored[k], 16)
                act.wait_ge(cleared, 6)
                with act.Fori(0, NB // 2) as i:
                    for k in range(2):
                        n = 2 * i + k
                        act.wait_ge(sT_done, L + n - 1)
                        nc.scalar.copy(sp_[:, k, :, :], sT[:, :, ds(n * ROWS, ROWS)]).then_inc(picked, 1)
                    for k in range(2):
                        n = 2 * i + k
                        act.wait_ge(maxed, L + n + 1)
                        for g in range(3):
                            last = nc.scalar.activation(s[:, k, g, :], s[:, k, g, :], ACT.Exp, bias=nm[:, k, g:g + 1],
                                                        accum_out=dn[:, k, g:g + 1])
                        last.then_inc(exp_done, 1)
                        act.wait_ge(lowest, L + n + 1)
                        nc.scalar.activation(wg[:, k, :], wd[:, k, :], ACT.Exp).then_inc(wexp_done, 1)
                    for k in range(2):
                        n = 2 * i + k
                        act.wait_ge(pT_done, L + n + 1)
                        act.wait_ge(pv_done, L + n - 1)
                        nc.scalar.copy(pnT[:, k, :, :], p_pn[:, :, :])
                        nc.scalar.copy(pm0[:, k, :], p_p[:, 0, :])
                        d1 = pm1[:, k, :, :].rearrange("p b (c x) -> p b c x", x=72)
                        s1 = p_p[:, 1, :].rearrange("p (b a c h) -> p b a c h", b=2, a=2, c=4)
                        for a in range(2):
                            nc.scalar.copy(d1[:, :, :, 32 * a:32 * a + NH], s1[:, :, a, :, :])
                        d2 = pm2[:, k, :, :].rearrange("p b (c x) -> p b c x", x=72)
                        nc.scalar.copy(d2[:, :, :, 0:NH], p_p[:, 2, :].rearrange("p (b c h) -> p b c h", b=2, c=8)
                                       ).then_inc(pm_done, 1)
                    for k in range(2):
                        n = 2 * i + k
                        act.wait_ge(out_ready, L + n + 1)
                        act.dma_start(OA[ds(n * ROWS, ROWS), :], oa[:, k, :]).then_inc(stored[k], 16)

            @block.vector
            def _(dve):
                V = nc.vector
                for x in (maxed, p_ready, lowest, out_ready):
                    dve.sem_inc(x, L)
                dve.wait_ge(E.const_in, 32)
                dve.wait_ge(snT_done, 1)
                V.tensor_copy(snT[:, :, :], p_sn[:, :, :]).then_inc(chain, 1)
                dve.wait_ge(chain, 1)
                dve.wait_ge(cleared, 6)
                with dve.Fori(0, NB // 2) as i:
                    link = Chain(dve, chain, 1 + (2 * LINKS) * i)

                    def softmax(n, k):
                        for b in range(2):
                            last = V.tensor_copy(sn2[64 * b:64 * b + 64, k, :, :],
                                                 snT[64 * b:64 * b + 64, :, ds((2 * n + b) * T, T)])
                        link(last)
                        dve.wait_ge(pT_done, L + n - 1)
                        dve.wait_ge(sT_done, L + n + 1)
                        for g in range(3):
                            dve.sem_inc(turns, 1)
                            V.tensor_tensor_reduce(out=s[:, k, g, 0:P], in0=p_s[:, k, g, :], in1=mask[:, g, 0:P],
                                                   scale=HD ** -0.5, scalar=LOWEST, op0=ALU.add, op1=ALU.max,
                                                   accum_out=mx[:, k, 0, g:g + 1])
                            last = V.tensor_tensor_reduce(out=s[:, k, g, P:], in0=sn2[:, k, g, :], in1=mask[:, g, P:],
                                                          scale=HD ** -0.5, scalar=LOWEST, op0=ALU.add, op1=ALU.max,
                                                          accum_out=mx[:, k, 1, g:g + 1])
                        link(last)
                        link(V.tensor_tensor(nm[:, k, :], mx[:, k, 0, :], mx[:, k, 1, :], ALU.max))
                        link(V.tensor_scalar(nm[:, k, :], nm[:, k, :], -1.0, None, ALU.mult))
                        dve.sem_inc(maxed, 1)
                        link(V.tensor_reduce(lw[:, k, :], nm[:, k, :], AX_X, ALU.min))
                        link(V.tensor_scalar(wd[:, k, :], nm[:, k, :], -1.0, lw[:, k, 0:1], ALU.mult, ALU.add))
                        dve.sem_inc(lowest, 1)

                    def place(n, k):
                        dve.wait_ge(exp_done, L + n + 1)
                        for b in range(2):
                            last = V.tensor_copy(pn[64 * b:64 * b + 64, k, :, T * b:T * b + T],
                                                 s[64 * b:64 * b + 64, k, :, P:])
                        last.then_inc(p_ready, 1)

                    def weights(n, k):
                        dve.wait_ge(wexp_done, L + n + 1)
                        link(V.tensor_tensor(wd[:, k, :], wg[:, k, :], dn[:, k, :], ALU.mult))
                        link(V.tensor_reduce(ds_[:, 0:1], wd[:, k, :], AX_X, ALU.add))
                        link(V.reciprocal(ds_[:, 1:2], ds_[:, 0:1]))
                        link(V.tensor_scalar(wg[:, k, :], wg[:, k, :], ds_[:, 1:2], None, ALU.mult))

                    def output(n, k):
                        dve.wait_ge(pv_done, L + n + 1)
                        dve.wait_ge(stored[k], 16 * i + 16)
                        for g in range(3):
                            last = V.scalar_tensor_tensor(out=po[:, g, :], in0=p_o[:, g, :], scalar=wg[:, k, g:g + 1],
                                                          in1=diag[:, :], op0=ALU.mult, op1=ALU.mult)
                        link(last)
                        link(V.tensor_reduce(oa[:, k, :], po[:, :, :].rearrange("p g (h e) -> p e (g h)", h=NH), AX_X,
                                             ALU.add))
                        dve.sem_inc(out_ready, 1)

                    for k in range(2):
                        softmax(2 * i + k, k)
                    for k in range(2):
                        place(2 * i + k, k)
                    for k in range(2):
                        weights(2 * i + k, k)
                    for k in range(2):
                        output(2 * i + k, k)
                    assert link.links == 2 * LINKS, link.links


def gla_sample(nc, A, S, O, ident):
    TMs, TSs, OL = S["tm"], S["ts"], S["ol"]
    NP = GH // 2
    st, sb, pb, sem = scope(nc)
    with st:
        wa = sb("g_wa", [RANK, GH * GK])
        ba = sb("g_ba", [P, NP])
        raw = sb("g_raw", [NS, TS_W])
        v = sb("g_v", [NS, GH * GV_W])
        state = sb("g_state", [P, DB, NP, 2 * GV_W])
        new = sb("g_new", [P, DB, NP, GV_W])
        f = sb("g_f", [P, 4, NS])
        fr = sb("g_fr", [RANK, NS])
        z = sb("g_z", [P, NP, NS])
        e = sb("g_e", [P, NP, NS])
        keep = sb("g_keep", [P, NP, NS])
        b = sb("g_b", [P, NP, NS])
        eb = sb("g_eb", [P, 3, NP, NS])
        decay = sb("g_decay", [P, NP, DB])
        qe = sb("g_qe", [P, NP, NS])
        ke = sb("g_ke", [P, NP, NS])
        kd = sb("g_kd", [P, NP, NS])
        qm = sb("g_qm", [P, NP, DB * 72])
        km = sb("g_km", [NS, NP, DB, P])
        att = sb("g_att", [NS, 2, NP, NS])
        cmask = sb("g_cmask", [NS, NS], U32)
        bmask = sb("g_bmask", [NS, DB])
        out = sb("g_out", [NS, GH * GV_W])
        p_f = pb("g_p_f", [P, 4, NS])
        p_r = pb("g_p_r", [RANK, NS])
        p_g = pb("g_p_g", [P, NP, NS])
        p_att = pb("g_p_att", [NS, 2, CH])
        p_o = pb("g_p_o", [NS, GH * GV_W])
        p_u = pb("g_p_u", [P, 2, CH])
        in_ = sem("g_in")
        st_in = sem("g_st_in")
        cleared = sem("g_cleared")
        t_done = sem("g_t_done")
        t_evacd = sem("g_t_evacd")
        g_done = sem("g_g_done")
        z_done = sem("g_z_done")
        gate = sem("g_gate")
        d = sem("g_d")
        e_ready = sem("g_e_ready")
        kd_ready = sem("g_kd_ready")
        kdT_done = sem("g_kdT_done")
        km_done = sem("g_km_done")
        att_done = sem("g_att_done")
        att_masked = sem("g_att_masked")
        o_done = sem("g_o_done")
        o_evacd = sem("g_o_evacd")
        u_done = sem("g_u_done")
        u_read = sem("g_u_read")
        stored = sem("g_stored")
        with nc.Block() as block:

            @block.sync
            def _(sp):
                for dst, src in ((raw[:, :], TSs), (v[:, :], TMs[SEQ:TOK, TM_GV * CH:(TM_GV + 1) * CH]),
                                 (wa[:, :], A["w_gla_a2"].rearrange("a r k -> (a r) k")), (ba[:, :], A["b_gla_a"]),
                                 (cmask[:, :], A["sample_mask"]), (bmask[:, :], A["batch_mask"])):
                    sp.dma_start(dst, src).then_inc(in_, 16)
                sp.wait_ge(cleared, 1)
                for h in range(GH):
                    r, c = slice(GK * (h % 2), GK * (h % 2) + GK), slice(GV_W * (h % 2), GV_W * (h % 2) + GV_W)
                    sp.dma_start(state[r, :, h // 2, c], A["state_gla"][0, :, h, :, :].rearrange("b k v -> k b v")
                                 ).then_inc(st_in, 16)
                sp.wait_ge(o_evacd, 1)
                sp.dma_start(OL[SEQ:TOK, :], out[:, :]).then_inc(stored, 16)
                sp.wait_ge(u_read, DB * NP)
                for h in range(GH):
                    r = slice(GK * (h % 2), GK * (h % 2) + GK)
                    sp.dma_start(O["gla_sample"][0, :, h, :, :].rearrange("b k v -> k b v"), new[r, :, h // 2, :]
                                 ).then_inc(stored, 16)
                sp.wait_ge(stored, 16 + 16 * GH)

            @block.gpsimd
            def _(pool):
                nc.gpsimd.memset(state[:, :, :, :], 0.0).then_inc(cleared, 1)
                nc.gpsimd.memset(keep[:, :, :], 1.0).then_inc(cleared, 1)
                nc.gpsimd.memset(qm[:, :, :], 0.0).then_inc(cleared, 1)
                nc.gpsimd.memset(att[:, :, :, :], 0.0).then_inc(cleared, 1)
                pool.wait_ge(cleared, 4)
                nc.gpsimd.memset(keep[:, :, :].rearrange("p a (c t) -> p (a c) t", t=T)[:, :, 0:1], 0.0
                                 ).then_inc(cleared, 1)

            @block.tensor
            def _(pe):
                pe.wait_ge(in_, 96)
                for c in range(4):
                    nc.tensor.transpose(p_f[:, c, :], raw[:, c * P:(c + 1) * P], ident[0:NS, 0:NS])
                nc.tensor.transpose(p_r[:, :], raw[:, 4 * P:4 * P + RANK], ident[0:NS, 0:NS]).then_inc(t_done, 1)
                pe.wait_ge(t_evacd, 2)
                for a in range(NP):
                    last = nc.tensor.matmul(p_g[:, a, :], wa[:, a * P:(a + 1) * P], fr[:, :], start=True, stop=True)
                last.then_inc(g_done, 1)
                pe.wait_ge(kd_ready, 1)
                for a in range(NP):
                    last = nc.tensor.transpose(p_f[0:NS, 2 * a:2 * a + 2, :], kd[:, a, :], ident[:, :])
                last.then_inc(kdT_done, 1)
                for a in range(NP):
                    for h in range(2):
                        r = slice(GK * h, GK * h + GK)
                        last = nc.tensor.matmul(p_att[:, h, a * NS:(a + 1) * NS], ke[r, a, :], qe[r, a, :],
                                                start=True, stop=True)
                last.then_inc(att_done, 1)
                pe.wait_ge(st_in, 16 * GH)
                pe.wait_ge(km_done, NP)
                for a in range(NP):
                    for j in range(DB):
                        nc.tensor.matmul(p_o[:, 2 * GV_W * a:2 * GV_W * (a + 1)], qm[:, a, NS * j:NS * j + NS],
                                         state[:, j, a, :], start=(a == 0 and j == 0), stop=False)
                pe.wait_ge(att_masked, 1)
                for h in range(GH):
                    cols = slice(GV_W * h, GV_W * (h + 1))
                    last = nc.tensor.matmul(p_o[:, cols], att[:, h % 2, h // 2, :], v[:, cols], start=False,
                                            stop=(h == GH - 1))
                last.then_inc(o_done, 1)
                for j in range(DB):
                    for a in range(NP):
                        n = NP * j + a
                        if n >= 2:
                            pe.wait_ge(u_read, n - 1)
                        nc.tensor.matmul(p_u[:, n % 2, 0:2 * GV_W], km[:, a, j, :], v[:, 2 * GV_W * a:2 * GV_W * (a + 1)],
                                         start=True, stop=True).then_inc(u_done, 1)

            @block.scalar
            def _(act):
                act.wait_ge(t_done, 1)
                nc.scalar.copy(f[:, :, :], p_f[:, :, :]).then_inc(t_evacd, 1)
                nc.scalar.copy(fr[:, :], p_r[:, :]).then_inc(t_evacd, 1)
                log_gates(nc, act, None, z[:, :, :], e[:, :, :], gate, None)
                act.wait_ge(d, 1)
                nc.scalar.activation(eb[:, 0, :, :], b[:, :, :], ACT.Exp, scale=1.0 / TAU).then_inc(e_ready, 1)
                nc.scalar.activation(eb[:, 1, :, :], b[:, :, :], ACT.Exp, scale=-1.0 / TAU).then_inc(e_ready, 1)
                ends = b[:, :, :].rearrange("p a (c t) -> p a c t", t=T)[:, :, :, T - 1]
                nc.scalar.activation(decay[:, :, :], ends, ACT.Exp, scale=1.0 / TAU).then_inc(e_ready, 1)
                act.wait_ge(d, 2)
                nc.scalar.activation(eb[:, 2, :, :], e[:, :, :], ACT.Exp, scale=-1.0 / TAU).then_inc(e_ready, 1)
                act.wait_ge(o_done, 1)
                nc.scalar.copy(out[:, :], p_o[:, :]).then_inc(o_evacd, 1)

            @block.vector
            def _(dve):
                V = nc.vector
                dve.wait_ge(in_, 96)
                dve.wait_ge(cleared, 5)
                dve.wait_ge(g_done, 1)
                for a in range(NP):
                    last = V.tensor_scalar(z[:, a, :], p_g[:, a, :], ba[:, a:a + 1], None, ALU.add)
                last.then_inc(z_done, 1)
                dve.wait_ge(z_done, 1)
                log_gates(nc, None, dve, z[:, :, :], e[:, :, :], gate, None)
                flat = lambda x: x[:, :, :].rearrange("p a t -> p (a t)")
                V.tensor_tensor_scan(flat(b), flat(keep), flat(z), 0.0, ALU.mult, ALU.add).then_inc(d, 1)
                dve.wait_ge(d, 1)
                chunks = lambda x: x[:, :, :].rearrange("p a (c t) -> p (a c) t", t=T)
                V.tensor_tensor(chunks(e), chunks(b), chunks(b)[:, :, T - 1:T].to_broadcast([P, NP * DB, T]),
                                ALU.subtract).then_inc(d, 1)
                dve.wait_ge(e_ready, 4)
                dve.wait_ge(t_evacd, 2)
                V.scalar_tensor_tensor(out=qe[:, :, :], in0=f[:, 0:2, :], scalar=GK ** -0.5, in1=eb[:, 0, :, :],
                                       op0=ALU.mult, op1=ALU.mult)
                V.tensor_tensor(ke[:, :, :], f[:, 2:4, :], eb[:, 1, :, :], ALU.mult)
                V.tensor_tensor(kd[:, :, :], f[:, 2:4, :], eb[:, 2, :, :], ALU.mult).then_inc(kd_ready, 1)
                dve.wait_ge(kd_ready, 1)
                V.tensor_copy(qm[:, :, :].rearrange("p a (j x) -> p a j x", x=72)[:, :, :, 0:T],
                              qe[:, :, :].rearrange("p a (j t) -> p a j t", t=T))
                dve.wait_ge(kdT_done, 1)
                for a in range(NP):
                    V.tensor_tensor(km[:, a, :, :],
                                    p_f[0:NS, 2 * a:2 * a + 2, :].rearrange("p x t -> p (x t)").unsqueeze(1)
                                    .to_broadcast([NS, DB, P]),
                                    bmask[:, :].unsqueeze(2).to_broadcast([NS, DB, P]), ALU.mult).then_inc(km_done, 1)
                dve.wait_ge(att_done, 1)
                for h in range(2):
                    last = V.copy_predicated(att[:, h, :, :], cmask[:, :].unsqueeze(1).to_broadcast([NS, NP, NS]),
                                             p_att[:, h, 0:NP * NS].rearrange("p (a t) -> p a t", a=NP))
                last.then_inc(att_masked, 1)
                dve.wait_ge(st_in, 16 * GH)
                for j in range(DB):
                    for a in range(NP):
                        n = NP * j + a
                        dve.wait_ge(u_done, n + 1)
                        for h in range(2):
                            r, c = slice(GK * h, GK * h + GK), slice(GV_W * h, GV_W * h + GV_W)
                            last = V.scalar_tensor_tensor(out=new[r, j, a, :], in0=state[r, j, a, c],
                                                          scalar=decay[r, a, j:j + 1], in1=p_u[r, n % 2, c],
                                                          op0=ALU.mult, op1=ALU.add)
                        last.then_inc(u_read, 1)


def store_windows(pool, S, O, done):
    TMs = S["tm"]
    for g, win in enumerate(WINDOWS):
        rows = min(win, SEQ)
        for kv in range(2):
            cols = slice((3 + 3 * kv + g) * CH, (4 + 3 * kv + g) * CH)
            pool.dma_start(O[f"kv_w{win}_prompt"][0, 0, :, kv, :, :].rearrange("s h e -> s (h e)"),
                           TMs[SEQ - rows:SEQ, cols]).then_inc(done, 16)
            pool.dma_start(O[f"kv_w{win}_sample"][0, :, :, kv, :, :].rearrange("b t h e -> (b t) (h e)"),
                           TMs[SEQ:TOK, cols]).then_inc(done, 16)


def decoder_step(nc, A, O):
    S = {name: nc.dram_tensor(name, shape, F32, kind="Internal").ap()
         for name, shape in (("tm", (TOK, TM_W)), ("ts", (NS, TS_W)), ("fm", (CH, SEQ)), ("gl", (RANK, SEQ)),
                             ("og", (TOK, 3, OG_W)), ("ol", (TOK, GH * GV_W)), ("oa", (NS * NH, HD)))}
    st, sb, _, sem = scope(nc)
    with st:
        ident = sb("ident", [P, P])
        ident_in = sem("ident_in")
        with nc.Block() as block:
            @block.sync
            def _(sp):
                sp.dma_start(ident[:, :], A["ident"]).then_inc(ident_in, 16)
                sp.wait_ge(ident_in, 16)

        sT = sb("sT", [P, 3, NS * NH])
        h_st, h_sb, _, _ = scope(nc)
        with h_st:
            hT_hi = h_sb("hT_hi", [P, KC, TOK], F32R)
            hT_lo = h_sb("hT_lo", [P, KC, TOK], F32R)
            norm_and_transpose(nc, A, hT_hi, hT_lo, ident)
            project(nc, A, S, hT_hi, hT_lo, sT)
        e_st, e_sb, _, e_sem = scope(nc)
        with e_st:
            E = SampleBuffers(e_sb, e_sem)
            attend_prompt(nc, A, S, O, ident, E)
            attend_sample(nc, A, S, ident, sT, E)
        gla_prompt(nc, A, S, O, ident)
        gla_sample(nc, A, S, O, ident)
        merge(nc, A, S, O, ident)


_OUTS = [("y_prompt", (1, SEQ, D)), ("y_sample", (DB, T, D))] + \
        [(f"kv_w{w}_prompt", (1, 1, min(w, SEQ), 2, NH, HD)) for w in (128, 512, 2048)] + \
        [("gla_prompt", (1, 1, GH, GK, GV_W))] + \
        [(f"kv_w{w}_sample", (1, DB, T, 2, NH, HD)) for w in (128, 512, 2048)] + \
        [("gla_sample", (1, DB, GH, GK, GV_W))]


_INS = ["x_prompt", "x_sample", "cache_kv_w128", "cache_kv_w512", "cache_kv_w2048", "state_gla", "ln_w", "w_in",
        "w_gla_a2", "b_gla_a", "gla_norm_w", "w_attn_out", "w_gla_out", "w_out", "final_norm_w"]


def _constants():
    import numpy as np

    half = HALF
    inv = (1.0 / (np.float32(500000.0) ** (np.arange(half, dtype=np.float32) * np.float32(2.0 / 16)))).astype(np.float32)
    pos = np.concatenate([np.arange(SEQ), np.arange(SEQ - NS, SEQ), SEQ + np.arange(NS) % T]).astype(np.float32)
    ang = pos[:, None] * inv[None, :]
    rope = np.concatenate([np.cos(ang), np.sin(ang)], axis=1).astype(np.float32)
    q, k = np.arange(P)[:, None], np.arange(P)[None, :]
    own = np.where(k <= q, 0.0, NEG)
    masks = np.stack([np.concatenate([np.full((P, P), NEG), own], 1),
                      np.concatenate([np.where(k >= q, 0.0, NEG), own], 1)], axis=1).astype(np.float32)
    chunk_mask = ((k >= q) & (k // CHUNK == q // CHUNK)).astype(np.uint32)
    tok = (np.arange(ROWS) // NH % T)[:, None]
    j = np.arange(T)[None, :]
    seen = np.stack([np.concatenate([k >= tok, j <= tok], 1),
                     np.concatenate([k >= tok // 4, (j == tok) | (j == tok - 4)], 1),
                     np.concatenate([k >= 0 * tok, j == tok], 1)], axis=1)
    dec_mask = np.where(seen, 0.0, NEG).astype(np.float32)
    dec_diag = (np.arange(CH)[None, :] // HD == np.arange(ROWS)[:, None] % NH).astype(np.float32)
    n = np.arange(NS)
    sample_mask = ((n[None, :] >= n[:, None]) & (n[None, :] // T == n[:, None] // T)).astype(np.uint32)
    batch_mask = (n[:, None] // T == np.arange(DB)[None, :]).astype(np.float32)
    return {"rope": rope, "ident": np.eye(P, dtype=np.float32), "masks": masks, "chunk_mask": chunk_mask,
            "dec_mask": dec_mask, "dec_diag": dec_diag, "sample_mask": sample_mask, "batch_mask": batch_mask}


def kernel(**inputs):
    import numpy as np
    import concourse.bacc as bacc
    from concourse.bass_utils import run_bass_kernel_spmd as run

    nc = bacc.Bacc("TRN2", target_bir_lowering=False, num_devices=1)
    arrays, A = {}, {}
    inputs = dict(inputs)
    inputs["ln_w"] = np.asarray(inputs["ln_w"]).reshape(KC, P).T
    inputs["b_gla_a"] = np.asarray(inputs["b_gla_a"]).reshape(GH // 2, P).T
    for name, a in [(n, inputs[n]) for n in _INS] + sorted(_constants().items()):
        a = np.ascontiguousarray(a)
        arrays["in_" + name] = a
        A[name] = nc.dram_tensor("in_" + name, a.shape, mybir.dt.from_np(a.dtype), kind="ExternalInput").ap()
    O = {name: nc.dram_tensor("out_" + name, shape, F32, kind="ExternalOutput").ap() for name, shape in _OUTS}
    decoder_step(nc, A, O)
    r = run(nc, [arrays], core_ids=[0]).results[0]
    return tuple(r["out_" + name] for name, _ in _OUTS)
```

```python
from contextlib import ExitStack

import concourse.bass as bass
from concourse import mybir

F32 = mybir.dt.float32
F32R = mybir.dt.float32r
U32 = mybir.dt.uint32
ALU = mybir.AluOpType
ACT = mybir.ActivationFunctionType
AX_X = mybir.AxisListType.X
ds = bass.ds

D = 1024
SEQ = 2048
DB, T = 8, 8
NS = DB * T
TOK = SEQ + NS
P = 128
KC = D // P
NT = SEQ // P
CH = 512
HD = 64
NH = 8
HALF = 8
EPS = 1e-6

COL_AZ, COL_GQK, COL_GV, COL_GZ, COL_GLR, COL_MGA = 4608, 5120, 5632, 6144, 6656, 6672
RANK = 16
IN_W = 8720

N_ROPED, N_TM = 6, 16
TM_GV, TM_AZ, TM_GZ, TM_MG = 9, 10, 11, 12
TM_W = N_TM * CH
N_CHUNK = N_TM + 1
FM_GQ, FM_GK = 0, 256
LEAD = 8
WINDOWS = (128, 512, 2048)
GROUPS = ((1, 16), (4, 4), (16, 1))
UNITS = (1, 4, 8)
UNIT0 = (0, 1, 5)
NU = 13
TS_W = CH + RANK


def scope(nc):
    st = ExitStack()
    sems = []

    def sb(name, shape, dt=F32):
        return st.enter_context(nc.sbuf_tensor(name, shape, dt))

    def pb(name, shape, dt=F32):
        return st.enter_context(nc.psum_tensor(name, shape, dt))

    def sem(name):
        sems.append(nc.alloc_semaphore(name))
        return sems[-1]

    def clear():
        if sems:
            nc.clear_and_free_semaphores(sems)
            nc.all_engine_barrier()

    st.callback(clear)
    return st, sb, pb, sem


class Chain:

    def __init__(self, eng, done, at):
        self.eng, self.done, self.at, self.links = eng, done, at, 0

    def __call__(self, instruction):
        instruction.then_inc(self.done, 1)
        self.links += 1
        self.eng.wait_ge(self.done, self.at + self.links)


def rsqrt_steps(nc, dve, done, before, m):
    nc.vector.reciprocal(m[3], m[2]).then_inc(done, 1)
    dve.wait_ge(done, before + 1)
    nc.vector.tensor_scalar(m[4], m[1], m[3], m[3], ALU.mult, ALU.mult).then_inc(done, 1)
    dve.wait_ge(done, before + 2)
    nc.vector.tensor_scalar(m[5], m[4], -0.5, 1.5, ALU.mult, ALU.add).then_inc(done, 1)
    dve.wait_ge(done, before + 3)
    nc.vector.tensor_tensor(m[2], m[3], m[5], ALU.mult).then_inc(done, 1)
    dve.wait_ge(done, before + 4)


def load_weights(sp, A, raw, w_in, i, col, width, lo_done):
    W = A["w_in"].rearrange("a (c p) e -> p (a c) e", p=P)
    for h in range(2):
        if lo_done is not None:
            sp.wait_ge(lo_done, 8 * i - 4 + 4 * h)
        sp.dma_start(raw[:, 4 * h:4 * h + 4, 0:width], W[:, 4 * h:4 * h + 4, ds(col, width)]).then_inc(w_in[h], 16)


def norm_and_transpose(nc, A, hT_hi, hT_lo, ident, raw, w_in):
    TILES = NT + 1
    SLOTS = 4
    st, sb, pb, sem = scope(nc)
    with st:
        xs = sb("a_x", [P, SLOTS, D])
        xn = sb("a_xn", [P, 2, D])
        junk = sb("a_junk", [P, 2, D])
        hf = sb("a_hf", [P, 2, KC, P])
        lnw = sb("a_lnw", [P, KC])
        ms = sb("a_ms", [P, 4, TILES])
        pt = pb("a_pt", [P, 2, 2, 4, P])
        x_in = [sem(f"a_x_in{s}") for s in range(SLOTS)]
        lnw_in = sem("a_lnw_in")
        cleared = sem("a_cleared")
        sq_act = sem("a_sq_act")
        sq_dve = sem("a_sq_dve")
        stat = sem("a_stat")
        rooted = sem("a_rooted")
        scaled = sem("a_scaled")
        tr_done = sem("a_tr_done")
        weighted = sem("a_weighted")
        hi_done = sem("a_hi_done")
        lo_done = sem("a_lo_done")
        xp = A["x_prompt"].rearrange("a s d -> (a s) d")
        xq = A["x_sample"].rearrange("a s d -> (a s) d")
        rows_of = lambda n: NS if isinstance(n, int) and n == NT else P
        first_loads = [len(range(s, TILES, SLOTS)) for s in range(SLOTS)]
        with nc.Block() as block:

            @block.sync
            def _(sp):
                def load(n, s):
                    if rows_of(n) == P:
                        sp.dma_start(xs[:, s, :], xp[ds(n * P, P), :]).then_inc(x_in[s], 16)
                    else:
                        sp.dma_start(xs[0:NS, s, :], xq).then_inc(x_in[s], 16)

                def squared(n):
                    sp.wait_ge(sq_dve if n % 2 else sq_act, n // 2 + 1)

                sp.dma_start(lnw[:, :], A["ln_w"]).then_inc(lnw_in, 16)
                for n in range(TILES):
                    if n >= SLOTS:
                        squared(n - SLOTS)
                    load(n, n % SLOTS)
                for n in (1, 2, 3, 0):
                    squared(max(m for m in range(TILES) if m % SLOTS == n))
                    load(n, n)
                load_weights(sp, A, raw, w_in, 0, 0, CH, None)
                with sp.Fori(0, NT // SLOTS - 1) as i:
                    for s in range(SLOTS):
                        n = SLOTS * (i + 1) + s
                        sp.wait_ge(scaled, LEAD + n - SLOTS + 1)
                        load(n, s)
                sp.wait_ge(scaled, LEAD + NT - SLOTS + 1)
                load(NT, 0)

            @block.gpsimd
            def _(pool):
                nc.gpsimd.memset(ms[:, :, :], 1.0).then_inc(cleared, 1)

            def in_order(eng, step):
                step(0, 0, 0)
                with eng.Fori(0, NT // SLOTS - 1) as i:
                    for k in range(1, SLOTS + 1):
                        step(SLOTS * i + k, k % SLOTS, i + k // SLOTS)
                for n in range(NT - SLOTS + 1, TILES):
                    step(n, n % SLOTS, n // SLOTS)

            @block.scalar
            def _(act):
                act.sem_inc(scaled, LEAD)
                act.wait_ge(cleared, 1)
                for n in range(0, TILES, 2):
                    rows = rows_of(n)
                    act.wait_ge(x_in[n % SLOTS], 16 * (n // SLOTS) + 16)
                    if n >= 2:
                        act.wait_ge(sq_act, n // 2)
                    nc.scalar.activation(junk[0:rows, 0, :], xs[0:rows, n % SLOTS, :], ACT.Square,
                                         accum_out=ms[0:rows, 0, n:n + 1]).then_inc(sq_act, 1)
                act.wait_ge(stat, 1)
                nc.scalar.activation(ms[:, 2, :], ms[:, 1, :], ACT.Sqrt).then_inc(rooted, 1)
                act.wait_ge(stat, 6)

                def round_hi(n, s):
                    rows = rows_of(n)
                    act.wait_ge(weighted, LEAD + 2 * n + 2)
                    nc.scalar.copy(hT_hi[:, :, ds(n * P, rows)], hf[:, s % 2, :, 0:rows]).then_inc(hi_done, 1)

                def step(n, s, turn):
                    rows = rows_of(n)
                    act.wait_ge(x_in[s], 16 * first_loads[s] + 16 * turn + 16)
                    act.wait_ge(tr_done, LEAD + 2 * n - 2)
                    nc.scalar.activation(xn[0:rows, s % 2, :], xs[0:rows, s, :], ACT.Copy,
                                         scale=ms[0:rows, 2, ds(n, 1)]).then_inc(scaled, 1)
                    if not (isinstance(n, int) and n == 0):
                        round_hi(n - 1, (s - 1) % SLOTS)

                in_order(act, step)
                round_hi(NT, 0)

            @block.vector
            def _(dve):
                for x in (weighted, lo_done):
                    dve.sem_inc(x, LEAD)
                dve.wait_ge(lnw_in, 16)
                dve.wait_ge(cleared, 1)
                for n in range(1, TILES, 2):
                    dve.wait_ge(x_in[n % SLOTS], 16 * (n // SLOTS) + 16)
                    if n >= 3:
                        dve.wait_ge(sq_dve, n // 2)
                    nc.vector.tensor_tensor_reduce(out=junk[:, 1, :], in0=xs[:, n % SLOTS, :], in1=xs[:, n % SLOTS, :],
                                                   scale=1.0, scalar=0.0, op0=ALU.mult, op1=ALU.add,
                                                   accum_out=ms[:, 0, n:n + 1]).then_inc(sq_dve, 1)
                dve.wait_ge(sq_act, TILES - TILES // 2)
                dve.wait_ge(sq_dve, TILES // 2)
                V = nc.vector
                V.tensor_scalar(ms[:, 1, :], ms[:, 0, :], 1.0 / D, EPS, ALU.mult, ALU.add).then_inc(stat, 1)
                dve.wait_ge(rooted, 1)
                link = Chain(dve, stat, 1)
                link(V.reciprocal(ms[:, 0, :], ms[:, 2, :]))
                link(V.tensor_tensor(ms[:, 3, :], ms[:, 0, :], ms[:, 0, :], ALU.mult))
                link(V.tensor_tensor(ms[:, 3, :], ms[:, 3, :], ms[:, 1, :], ALU.mult))
                link(V.tensor_scalar(ms[:, 3, :], ms[:, 3, :], -0.5, 1.5, ALU.mult, ALU.add))
                link(V.tensor_tensor(ms[:, 2, :], ms[:, 0, :], ms[:, 3, :], ALU.mult))

                def subtract(n, s):
                    rows = rows_of(n)
                    dve.wait_ge(hi_done, n + 1)
                    V.tensor_tensor(hT_lo[:, :, ds(n * P, rows)], hf[:, s % 2, :, 0:rows],
                                    hT_hi[:, :, ds(n * P, rows)].bitcast(F32), ALU.subtract).then_inc(lo_done, 1)

                def step(n, s, turn):
                    rows = rows_of(n)
                    dve.wait_ge(lo_done, LEAD + n - 1)
                    for h in range(2):
                        dve.wait_ge(tr_done, LEAD + 2 * n + h + 1)
                        V.tensor_tensor(hf[:, s % 2, 4 * h:4 * h + 4, 0:rows], pt[:, s % 2, h, :, 0:rows],
                                        lnw[:, 4 * h:4 * h + 4].unsqueeze(2).to_broadcast([P, 4, rows]),
                                        ALU.mult).then_inc(weighted, 1)
                    if not (isinstance(n, int) and n == 0):
                        subtract(n - 1, (s - 1) % SLOTS)

                in_order(dve, step)
                subtract(NT, 0)
                dve.wait_ge(lo_done, LEAD + TILES)

            @block.tensor
            def _(pe):
                pe.sem_inc(tr_done, LEAD)

                def step(n, s, turn):
                    rows = rows_of(n)
                    pe.wait_ge(scaled, LEAD + n + 1)
                    pe.wait_ge(weighted, LEAD + 2 * n - 2)
                    for h in range(2):
                        for c in range(4):
                            k = 4 * h + c
                            last = nc.tensor.transpose(pt[:, s % 2, h, c, 0:rows],
                                                       xn[0:rows, s % 2, k * P:(k + 1) * P], ident[0:rows, 0:rows])
                        last.then_inc(tr_done, 1)

                in_order(pe, step)


def cached(A, g, b, kv):
    dil, _ = GROUPS[g]
    cache = A[f"cache_kv_w{WINDOWS[g]}"]
    src = cache[0, ds(b, 1), :, kv, :, :].rearrange("b (l r) h e -> l (b r) (h e)", r=dil)
    return src[:, 0:UNITS[g], :]


def project(nc, A, S, hT_hi, hT_lo, sT, raw, w_in):
    TMs, TSs, FMs, GLs = S["tm"], S["ts"], S["fm"], S["gl"]
    TILES = NT + 1
    LASTS = TOK - P
    st, sb, pb, sem = scope(nc)
    with st:
        whi = sb("b_whi", [P, KC, CH], F32R)
        wlo = sb("b_wlo", [P, KC, CH], F32R)
        stage = sb("b_stage", [P, 5, CH])
        cs = sb("b_cs", [P, TILES, 2, HALF])
        rc = sb("b_rc", [P, NH, 2, HALF])
        rs = sb("b_rs", [P, NH, 2, HALF])
        ck = sb("b_ck", [P, 2, CH])
        cq = sb("b_cq", [P, 2, CH])
        acc = pb("b_acc", [P, 5, CH])
        cs_in = sem("b_cs_in")
        hi_done = sem("b_hi_done")
        lo_done = sem("b_lo_done")
        w_used = sem("b_w_used")
        mm_done = sem("b_mm_done")
        evacd = sem("b_evacd")
        roped = sem("b_roped")
        rmul = sem("b_rmul")
        stored = [sem(f"b_stored{k}") for k in range(5)]
        ck_in = [sem("b_ck_in0"), sem("b_ck_in1")]
        cq_in = [sem("b_cq_in0"), sem("b_cq_in1")]
        multiplied = sem("b_multiplied")
        scored = sem("b_scored")
        items = [(g, c, t) for g in range(3) for c in range(UNITS[g]) for t in range(c if g else 0, T, UNITS[g])]
        NI = len(items)
        unit = lambda m: UNIT0[items[m][0]] + items[m][1]
        unit_end = [max(m for m in range(NI) if unit(m) == u) + 1 for u in range(NU)]
        FIRST = N_CHUNK - 1 - DB
        slot = lambda t: t % 4 if t < NT else 4
        EV0 = 4
        N_ALL = N_CHUNK * TILES

        with nc.Block() as block:

            @block.sync
            def _(sp):
                sp.dma_start(cs[:, :, :, :], A["rope"].rearrange("(t p) (a f) -> p t a f", p=P, a=2)).then_inc(cs_in, 16)
                for k in range(5):
                    sp.sem_inc(stored[k], 16)

                load = lambda i, col, width=CH: load_weights(sp, A, raw, w_in, i, col, width, lo_done)

                def store(i, t, dst, src):
                    sp.dma_start(dst, src).then_inc(stored[slot(t)], 16)

                def tm_chunk(i, ready):
                    for t in range(TILES):
                        ready(TILES * i + t)
                        if t < NT:
                            store(i, t, TMs[t * P:(t + 1) * P, ds(i * CH, CH)], stage[:, slot(t), :])
                        else:
                            store(i, t, TMs[SEQ:TOK, ds(i * CH, CH)], stage[NS:P, 4, :])

                rotated = lambda n: sp.wait_ge(roped, n + 2)
                copied = lambda n: sp.wait_ge(evacd, EV0 + n + 1)
                with sp.Fori(0, N_ROPED) as i:
                    load(i + 1, (i + 1) * CH)
                    tm_chunk(i, rotated)
                with sp.Fori(N_ROPED, TM_GV - 1) as i:
                    load(i + 1, (i + 1) * CH)
                    tm_chunk(i, copied)
                for i, col in ((TM_GV - 1, COL_GV), (TM_GV, COL_AZ), (TM_AZ, COL_GZ)):
                    load(i + 1, col)
                    tm_chunk(i, copied)
                with sp.Fori(TM_GZ, N_TM - 1) as i:
                    load(i + 1, COL_MGA + CH * (i - TM_GZ))
                    tm_chunk(i, copied)
                load(N_TM, COL_GQK)
                tm_chunk(N_TM - 1, copied)
                load(N_CHUNK, COL_GLR, P)
                for t in range(NT):
                    copied(TILES * N_TM + t)
                    store(N_TM, t, FMs[(t // 4) * P:(t // 4 + 1) * P, (t % 4) * CH:(t % 4 + 1) * CH], stage[:, slot(t), :])
                copied(TILES * N_TM + NT)
                store(N_TM, NT, TSs[:, 0:CH], stage[NS:P, 4, :])
                for tb in range(4):
                    copied(N_ALL + tb)
                    store(N_CHUNK, tb, GLs[:, tb * CH:(tb + 1) * CH], stage[0:RANK, tb, :])
                copied(N_ALL + 4)
                store(N_CHUNK, NT, TSs[:, CH:TS_W], stage[NS:P, 4, 0:RANK])
                for k in range(4):
                    sp.wait_ge(stored[k], 16 + 16 * (4 * N_CHUNK + 1))
                sp.wait_ge(stored[4], 16 + 16 * (N_CHUNK + 1))

            @block.gpsimd
            def _(pool):
                pool.wait_ge(stored[4], 16 + 16 * 3)
                with pool.Fori(0, DB) as b:
                    for m, (g, c, t) in enumerate(items):
                        u = unit(m)
                        if m == 0 or unit(m - 1) != u:
                            last = unit_end[u - 2] if u >= 2 else (0, unit_end[NU - 2] - NI)[u]
                            pool.wait_ge(scored, LEAD + NI * b + last)
                            pool.dma_start(ck[:, u % 2, :], cached(A, g, b, 0)[:, c, :]).then_inc(ck_in[u % 2], 16)
                        pool.wait_ge(scored, LEAD + NI * b + m - 1)
                        pool.dma_start(cq[:, m % 2, :], TMs[ds(SEQ + T * b + t, 1), g * CH:(g + 1) * CH]
                                       .to_broadcast([P, CH])).then_inc(cq_in[m % 2], 16)

            @block.scalar
            def _(act):
                def split_hi(i, width=CH):
                    for k in range(KC):
                        if k % 4 == 0:
                            act.wait_ge(w_in[k // 4], 16 * i + 16)
                        if not (isinstance(i, int) and i == 0):
                            act.wait_ge(w_used, 8 * i - 8 + k + 1)
                        nc.scalar.copy(whi[:, k, 0:width], raw[:, k, 0:width]).then_inc(hi_done, 1)

                def evac(i, t, width=CH):
                    act.wait_ge(mm_done, TILES * i + t + 1)
                    uses = 4 * i + t // 4 if t < NT else i
                    act.wait_ge(stored[slot(t)], 16 * uses + 16)
                    nc.scalar.copy(stage[:, slot(t), 0:width], acc[:, slot(t), 0:width]).then_inc(evacd, 1)

                act.sem_inc(evacd, EV0)
                split_hi(0)
                with act.Fori(0, N_CHUNK - 1) as i:
                    for t in range(NT):
                        evac(i, t)
                    split_hi(i + 1)
                    evac(i, NT)
                i = N_CHUNK - 1
                for t in range(NT):
                    evac(i, t)
                split_hi(N_CHUNK, P)
                evac(i, NT)
                for tb in range(4):
                    act.wait_ge(mm_done, N_ALL + tb + 1)
                    act.wait_ge(stored[tb], 16 + 16 * 4 * N_CHUNK)
                    nc.scalar.copy(stage[:, tb, :], acc[:, tb, :]).then_inc(evacd, 1)
                act.wait_ge(mm_done, N_ALL + 5)
                act.wait_ge(stored[4], 16 + 16 * N_CHUNK)
                nc.scalar.copy(stage[:, 4, 0:RANK], acc[:, 4, 0:RANK]).then_inc(evacd, 1)

            @block.vector
            def _(dve):
                def split_lo(i, width=CH):
                    for k in range(KC):
                        dve.wait_ge(hi_done, 8 * i + k + 1)
                        nc.vector.tensor_tensor(wlo[:, k, 0:width], raw[:, k, 0:width],
                                                whi[:, k, 0:width].bitcast(F32), ALU.subtract).then_inc(lo_done, 1)

                def rope(i, t):
                    n = TILES * i + t
                    dve.wait_ge(evacd, EV0 + n + 1)
                    dve.wait_ge(roped, n + 1)
                    x = stage[:, slot(t), :].rearrange("p (h e) -> p h e", h=NH)[:, :, 0:2 * HALF].rearrange(
                        "p h (a f) -> p h a f", a=2)
                    full = [P, NH, 2, HALF]
                    cos = cs[:, t, 0:1, :].unsqueeze(1).to_broadcast(full)
                    sin = cs[:, t, 1:2, :].unsqueeze(1).to_broadcast(full)
                    nc.vector.tensor_tensor(rc[:, :, :, :], x, cos, ALU.mult).then_inc(rmul, 1)
                    nc.vector.tensor_tensor(rs[:, :, :, :], x, sin, ALU.mult).then_inc(rmul, 1)
                    dve.wait_ge(rmul, 2 * n + 2)
                    nc.vector.tensor_tensor(x[:, :, 0, :], rc[:, :, 0, :], rs[:, :, 1, :], ALU.subtract)
                    nc.vector.tensor_tensor(x[:, :, 1, :], rc[:, :, 1, :], rs[:, :, 0, :], ALU.add).then_inc(roped, 1)

                dve.wait_ge(cs_in, 16)
                dve.sem_inc(roped, 1)
                dve.sem_inc(scored, LEAD)
                split_lo(0)
                with dve.Fori(0, N_ROPED) as i:
                    for t in range(NT):
                        rope(i, t)
                    split_lo(i + 1)
                    rope(i, NT)
                with dve.Fori(N_ROPED, FIRST) as i:
                    split_lo(i + 1)
                with dve.Fori(0, DB) as b:
                    for m, (g, c, t) in enumerate(items):
                        u = unit(m)
                        dve.wait_ge(cq_in[m % 2], 16 * (NI // 2) * b + 16 * (m // 2) + 16)
                        if m == 0 or unit(m - 1) != u:
                            dve.wait_ge(ck_in[u % 2], 16 * ((NU + 1 - u % 2) // 2) * b + 16 * (u // 2) + 16)
                        q = cq[:, m % 2, :]
                        nc.vector.tensor_tensor(q, q, ck[:, u % 2, :], ALU.mult).then_inc(multiplied, 1)
                        dve.wait_ge(multiplied, NI * b + m + 1)
                        nc.vector.tensor_reduce(sT[:, g, ds((T * b + t) * NH, NH)],
                                                q.rearrange("p (h e) -> p h e", h=NH), AX_X, ALU.add
                                                ).then_inc(scored, 1)
                    split_lo(b + FIRST + 1)
                dve.wait_ge(scored, LEAD + NI * DB)
                split_lo(N_CHUNK, P)

            @block.tensor
            def _(pe):
                def product(out, k, stat_hi, stat_lo, mov_hi, mov_lo):
                    nc.tensor.matmul(out, stat_hi, mov_hi, start=(k == 0), stop=False)
                    nc.tensor.matmul(out, stat_hi, mov_lo, start=False, stop=False)
                    return nc.tensor.matmul(out, stat_lo, mov_hi, start=False, stop=(k == KC - 1))

                def tile(i, t, out, stat, mov):
                    pe.wait_ge(evacd, TILES * i + t + 1)
                    for k in range(KC):
                        if t == 0:
                            pe.wait_ge(lo_done, 8 * i + k + 1)
                        last = product(out, k, *stat(k), *mov(k))
                        if t == NT and k < KC - 1:
                            last.then_inc(w_used, 1)
                    last.then_inc(mm_done, 1)
                    if t == NT:
                        pe.wait_ge(mm_done, TILES * i + t + 1)
                        pe.sem_inc(w_used, 1)

                def tokens(off, width):
                    return lambda k: (hT_hi[:, k, off:off + width], hT_lo[:, k, off:off + width])

                def weights(off, width):
                    return lambda k: (whi[:, k, off:off + width], wlo[:, k, off:off + width])

                with pe.Fori(0, N_TM) as i:
                    for t in range(TILES):
                        tile(i, t, acc[:, slot(t), :], tokens(t * P if t < NT else LASTS, P), weights(0, CH))
                for t in range(NT):
                    tile(N_TM, t, acc[:, slot(t), :], weights((t // 4) * P, P), tokens((t % 4) * CH, CH))
                tile(N_TM, NT, acc[:, 4, :], tokens(LASTS, P), weights(0, CH))
                for tb in range(4):
                    tile(N_CHUNK, tb, acc[:, tb, :], weights(0, P), tokens(tb * CH, CH))
                pe.wait_ge(evacd, N_ALL + 5)
                for k in range(KC):
                    last = product(acc[:, 4, 0:RANK], k, *tokens(LASTS, P)(k), *weights(0, RANK)(k))
                last.then_inc(mm_done, 1)


NEG = -3.0e38
LOWEST = -3.4e38
OG_W = CH + 2 * NH


def attend_prompt(nc, A, S, O, ident, E):
    TMs, OG = S["tm"], S["og"]
    UNROLL = 4
    st, sb, pb, sem = scope(nc)
    with st:
        qk = sb("c_qk", [P, 2, 2, CH])
        v = sb("c_v", [P, UNROLL, CH])
        qT = sb("c_qT", [P, 2, 4, P])
        kT = sb("c_kT", [P, 4, UNROLL + 1, P])
        sm = sb("c_sm", [P, 2, 2, 2 * P])
        p = sb("c_p", [P, 2, 2, 2 * P])
        pT = sb("c_pT", [P, 2, 4, P])
        mx = sb("c_mx", [P, 2, 2])
        og = sb("c_og", [P, UNROLL, OG_W])
        mask = sb("c_mask", [P, 2, 2 * P])
        kn = sb("c_kn", [NS, 3, CH])
        qn = sb("c_qn", [NS, T, CH])
        p_qk = pb("c_p_qk", [P, CH])
        p_s = pb("c_p_s", [P, 2, 2, CH])
        p_t = pb("c_p_t", [P, 2, 4, P])
        p_o = pb("c_p_o", [P, NH, HD])

        mask_in = sem("c_mask_in")
        qk_in = [sem("c_qk_in0"), sem("c_qk_in1")]
        v_in = [sem(f"c_v_in{j}") for j in range(UNROLL)]
        stored = [sem(f"c_stored{j}") for j in range(UNROLL)]
        zeroed = sem("c_zeroed")
        windows_out = sem("c_windows_out")
        tqk_done = sem("c_tqk_done")
        q_evacd = sem("c_q_evacd")
        k_evacd = sem("c_k_evacd")
        o_evacd = sem("c_o_evacd")
        qk_done = sem("c_qk_done")
        turns = sem("c_turns")
        masked = sem("c_masked")
        maxed = sem("c_maxed")
        exp_done = sem("c_exp_done")
        pt_done = sem("c_pt_done")
        pt_evacd_act = sem("c_pt_evacd_act")
        pt_evacd_dve = sem("c_pt_evacd_dve")
        pv_done = sem("c_pv_done")

        ORDER = (1, 0, 2)
        BODIES = NT // UNROLL
        N = 4 * UNROLL

        def loops(eng, body):
            before = None
            for nth, g in enumerate(ORDER):
                body(g, NT * nth, 0, before, True)
                until = BODIES - (nth == len(ORDER) - 1)
                with eng.Fori(1, until) as i:
                    body(g, NT * nth + UNROLL * i, i, (g, i - 1), True)
                before = (g, BODIES - 1)
            body(ORDER[-1], NT * 3 - UNROLL, BODIES - 1, (ORDER[-1], BODIES - 2), False)

        with nc.Block() as block:
            def evac_of(n0, w):
                return (pt_evacd_dve if w % 2 else pt_evacd_act), LEAD + 2 * n0 + w // 2 + 1

            def evac(eng, copy, n0, w, done, near):
                eng.wait_ge(pt_done, LEAD + 4 * n0 + w + 1)
                eng.wait_ge(pv_done, LEAD + 4 * n0 + w - 1)
                if near:
                    copy(pT[:, w % 2, 1::2, :], p_t[:, w % 2, 1::2, :]).then_inc(done, 1)
                else:
                    copy(pT[:, w % 2, :, :], p_t[:, w % 2, :, :]).then_inc(done, 1)


            @block.sync
            def _(sp):
                sp.dma_start(mask[:, :, :], A["masks"]).then_inc(mask_in, 16)

                def body(g, n0, i):
                    dil, nblk = GROUPS[g]
                    for j in range(UNROLL):
                        n = n0 + j
                        if g == 0:
                            rows = TMs[ds((UNROLL * i + j) * P, P), :]
                        elif g == 1:
                            rows = TMs[0:SEQ, :].rearrange("(a r) e -> r a e", r=dil)[ds(i, 1), j * P:(j + 1) * P, :]
                            rows = rows.rearrange("r a e -> (r a) e")
                        else:
                            rows = TMs[0:SEQ, :].rearrange("(a r) e -> r a e", r=dil)[ds(UNROLL * i + j, 1), :, :]
                            rows = rows.rearrange("r a e -> (r a) e")
                        sp.wait_ge(tqk_done, LEAD + 2 * (n - 2) + 2)
                        for a in range(2):
                            sp.dma_start(qk[:, j % 2, a, :], rows[:, (3 * a + g) * CH:(3 * a + g + 1) * CH]
                                         ).then_inc(qk_in[j % 2], 16)
                        sp.wait_ge(pv_done, LEAD + 4 * (n - 3) + 4)
                        if j == UNROLL - 1:
                            sp.wait_ge(zeroed, 2)
                        sp.dma_start(v[:, j, :], rows[:, (6 + g) * CH:(7 + g) * CH]).then_inc(v_in[j], 16)

                for j in range(UNROLL):
                    sp.sem_inc(stored[j], 16)
                for nth, g in enumerate(ORDER):
                    with sp.Fori(0, BODIES) as i:
                        body(g, NT * nth + UNROLL * i, i)
                for j in range(UNROLL):
                    sp.wait_ge(stored[j], 16 + 16 * 3 * NT // UNROLL)

            @block.gpsimd
            def _(pool):
                nc.gpsimd.memset(kT[:, :, 0, :], 0.0).then_inc(zeroed, 1)
                nc.gpsimd.memset(v[:, UNROLL - 1, :], 0.0).then_inc(zeroed, 1)
                E.new_key_scores(nc, pool, A, S, kn, qn)
                for k in range(2):
                    E.load_v(pool, A, S, k, k, lambda m: pool.wait_ge(pv_done, LEAD + 4 * (4 + 7 * k + m)))
                pieces = store_windows(pool, S, O, windows_out, lambda n: pool.wait_ge(pv_done, LEAD + 4 * (18 + n)))
                pool.wait_ge(windows_out, 16 * pieces)

            @block.tensor
            def _(pe):
                for s in (tqk_done, qk_done, pt_done, pv_done):
                    pe.sem_inc(s, LEAD)
                pe.wait_ge(zeroed, 2)

                def transposes(n, j, a):
                    if a == 0:
                        pe.wait_ge(qk_in[j % 2], 16 * (n - j) + 32 * (j // 2) + 32)
                        pe.wait_ge(k_evacd, LEAD + n)
                    else:
                        pe.wait_ge(q_evacd, LEAD + n + 1)
                    for c in range(4):
                        last = nc.tensor.transpose(p_qk[:, c * P:(c + 1) * P],
                                                   qk[:, j % 2, a, c * P:(c + 1) * P], ident[:, :])
                    last.then_inc(tqk_done, 1)

                def scores(g, n0, w):
                    near = g == 2
                    j, c = divmod(w, 4)
                    if c == 0:
                        pe.wait_ge(q_evacd, LEAD + n0 + j + 1)
                        pe.wait_ge(k_evacd, LEAD + n0 + j + 1)
                    pe.wait_ge(masked, LEAD + 4 * n0 + w - 1)
                    for h in range(2):
                        rows = slice(HD * h, HD * h + HD)
                        keys = kT[rows, c, j + 1:j + 2, :] if near else kT[rows, c, j:j + 2, :]
                        out = p_s[:, h, w % 2, P if near else 0:2 * P]
                        last = nc.tensor.matmul(out, qT[rows, j % 2, c, :], keys, start=True, stop=True)
                    last.then_inc(qk_done, 1)

                def transpose_p(g, n0, w):
                    pe.wait_ge(exp_done, LEAD + 4 * n0 + w + 1)
                    pe.wait_ge(*evac_of(n0, w - 2))
                    for h in range(2):
                        for b in ((1,) if g == 2 else (0, 1)):
                            last = nc.tensor.transpose(p_t[:, w % 2, 2 * h + b, :],
                                                       p[:, w % 2, h, b * P:(b + 1) * P], ident[:, :])
                    last.then_inc(pt_done, 1)

                def sums(g, n0, w):
                    near = g == 2
                    j, c = divmod(w, 4)
                    pe.wait_ge(*evac_of(n0, w))
                    if c == 0:
                        pe.wait_ge(v_in[j], 4 * n0 + 16)
                        pe.wait_ge(o_evacd, LEAD + n0 + j)
                    for h in range(2):
                        cols = slice((2 * c + h) * HD, (2 * c + h + 1) * HD)
                        for b in ((1,) if near else (0, 1)):
                            vb = v[:, j if b else (j - 1) % UNROLL, cols]
                            last = nc.tensor.matmul(p_o[:, 2 * c + h, :], pT[:, w % 2, 2 * h + b, :], vb,
                                                    start=(b == 1 if near else b == 0), stop=(b == 1))
                    last.then_inc(pv_done, 1)

                def body(g, n0, i, before, more):
                    for w in range(N):
                        scores(g, n0, w)
                        if w % 4 in (1, 2) and (w < N - 4 or more):
                            transposes(n0 + w // 4 + 1, (w // 4 + 1) % UNROLL, w % 4 - 1)
                        if w >= 1:
                            transpose_p(g, n0, w - 1)
                        elif before:
                            transpose_p(before[0], n0 - UNROLL, N - 1)
                        if w >= 2:
                            sums(g, n0, w - 2)
                        elif before:
                            sums(before[0], n0 - UNROLL, N - 2 + w)

                transposes(0, 0, 0)
                transposes(0, 0, 1)
                loops(pe, body)
                n0 = 3 * NT - UNROLL
                transpose_p(ORDER[-1], n0, N - 1)
                sums(ORDER[-1], n0, N - 2)
                sums(ORDER[-1], n0, N - 1)

            @block.scalar
            def _(act):
                for s in (q_evacd, o_evacd, exp_done, pt_evacd_act):
                    act.sem_inc(s, LEAD)

                def store(g, n, i, j):
                    dil, _ = GROUPS[g]
                    act.wait_ge(o_evacd, LEAD + n + 1)
                    out = OG[0:SEQ, g, :]
                    if g == 0:
                        out = out[ds((UNROLL * i + j) * P, P), :]
                    else:
                        out = out.rearrange("(a r) e -> r a e", r=dil)
                        out = out[ds(i, 1), j * P:(j + 1) * P, :] if g == 1 else out[ds(UNROLL * i + j, 1), :, :]
                        out = out.rearrange("r a e -> (r a) e")
                    act.dma_start(out, og[:, j, :]).then_inc(stored[j], 16)

                def q_evac(n, j):
                    act.wait_ge(tqk_done, LEAD + 2 * n + 1)
                    act.wait_ge(qk_done, LEAD + 4 * (n - 1))
                    nc.scalar.copy(qT[:, j % 2, :, :], p_qk[:, :]).then_inc(q_evacd, 1)

                def exps(g, n0, w):
                    j, c = divmod(w, 4)
                    act.wait_ge(maxed, LEAD + 4 * n0 + w + 1)
                    act.wait_ge(pt_done, LEAD + 4 * n0 + w - 1)
                    lo = P if g == 2 else 0
                    for h in range(2):
                        hh = 2 * c + h
                        last = nc.scalar.activation(p[:, w % 2, h, lo:], sm[:, w % 2, h, lo:], ACT.Exp,
                                                    bias=og[:, j, CH + hh:CH + hh + 1],
                                                    accum_out=og[:, j, CH + NH + hh:CH + NH + hh + 1])
                    last.then_inc(exp_done, 1)

                def o_evac(g, n0, i, j):
                    act.wait_ge(pv_done, LEAD + 4 * (n0 + j) + 4)
                    nc.scalar.copy(og[:, j, 0:CH], p_o[:, :, :]).then_inc(o_evacd, 1)
                    store(g, n0 + j, i, j)

                def body(g, n0, i, before, more):
                    for w in range(N):
                        exps(g, n0, w)
                        if w % 4 == 1 and (w < N - 4 or more):
                            q_evac(n0 + w // 4 + 1, (w // 4 + 1) % UNROLL)
                        if w >= 1 and (w - 1) % 2 == 0:
                            evac(act, nc.scalar.copy, n0, w - 1, pt_evacd_act, g == 2)
                        if w % 4 == 1:
                            if w >= 5:
                                o_evac(g, n0, i, w // 4 - 1)
                            elif before:
                                o_evac(before[0], n0 - UNROLL, before[1], UNROLL - 1)

                q_evac(0, 0)
                loops(act, body)
                o_evac(ORDER[-1], 3 * NT - UNROLL, BODIES - 1, UNROLL - 1)

            @block.vector
            def _(dve):
                for s in (k_evacd, masked, maxed, pt_evacd_dve):
                    dve.sem_inc(s, LEAD)
                dve.wait_ge(mask_in, 16)
                dve.wait_ge(zeroed, 2)

                def k_evac(n, j):
                    dve.wait_ge(tqk_done, LEAD + 2 * n + 2)
                    dve.wait_ge(qk_done, LEAD + 4 * n - 4 * (UNROLL - 2))
                    src = p_qk[:, :].rearrange("p (c k) -> p c k", c=4)
                    last = nc.vector.tensor_copy(kT[:, :, j + 1, :], src)
                    if j == UNROLL - 1:
                        last = nc.vector.tensor_copy(kT[:, :, 0, :], src)
                    last.then_inc(k_evacd, 1)

                def mask_and_max(g, n0, i, w):
                    j, c = divmod(w, 4)
                    dve.wait_ge(qk_done, LEAD + 4 * n0 + w + 1)
                    dve.wait_ge(exp_done, LEAD + 4 * n0 + w - 1)
                    if c == 0:
                        dve.wait_ge(stored[j], 4 * n0 + 16)
                    dve.sem_inc(turns, 1)
                    lo = P if g == 2 else 0
                    alone = j == 0 and (g == 1 or (g == 0 and isinstance(i, int)))
                    m = mask[:, 0 if alone else 1, lo:]
                    for h in range(2):
                        last = nc.vector.tensor_tensor_reduce(
                            out=sm[:, w % 2, h, lo:], in0=p_s[:, h, w % 2, lo:2 * P], in1=m, scale=HD ** -0.5,
                            scalar=LOWEST, op0=ALU.add, op1=ALU.max, accum_out=mx[:, w % 2, h:h + 1])
                    last.then_inc(masked, 1)
                    dve.wait_ge(masked, LEAD + 4 * n0 + w + 1)
                    nc.vector.tensor_scalar(og[:, j, CH + 2 * c:CH + 2 * c + 2], mx[:, w % 2, :], -1.0, None,
                                            ALU.mult).then_inc(maxed, 1)

                def body(g, n0, i, before, more):
                    for w in range(N):
                        mask_and_max(g, n0, i, w)
                        if w % 4 == 2 and (w < N - 4 or more):
                            k_evac(n0 + w // 4 + 1, (w // 4 + 1) % UNROLL)
                        if w >= 1 and (w - 1) % 2 == 1:
                            evac(dve, nc.vector.tensor_copy, n0, w - 1, pt_evacd_dve, g == 2)
                        elif w == 0 and before:
                            evac(dve, nc.vector.tensor_copy, n0 - UNROLL, N - 1, pt_evacd_dve, before[0] == 2)

                k_evac(0, 0)
                loops(dve, body)
                evac(dve, nc.vector.tensor_copy, 3 * NT - UNROLL, N - 1, pt_evacd_dve, True)


GH, GK, GV_W = 4, 64, 128
CHUNK = 64
TAU = 16.0


def log_gates(nc, act, dve, z, e, done, z_ready, base=0):
    if dve is not None:
        nc.vector.scalar_tensor_tensor(out=e, in0=z, scalar=-1.0, in1=z, op0=ALU.mult, op1=ALU.min
                                       ).then_inc(done, 1)
        dve.wait_ge(done, base + 3)
        nc.vector.scalar_tensor_tensor(out=z, in0=z, scalar=0.0, in1=e, op0=ALU.min,
                                       op1=ALU.subtract).then_inc(done, 1)
        dve.wait_ge(done, base + 4)
    if act is not None:
        act.wait_ge(done, base + 1)
        nc.scalar.activation(e, e, ACT.Exp).then_inc(done, 1)
        act.wait_ge(done, base + 2)
        nc.scalar.activation(e, e, ACT.Ln, bias=1.0).then_inc(done, 1)


def gla_prompt(nc, A, S, O, ident):
    TMs, FMs, GLs, OL = S["tm"], S["fm"], S["gl"], S["ol"]
    NP = GH // 2
    SLOTS = 4
    st, sb, pb, sem = scope(nc)
    with st:
        wa = sb("d_wa", [RANK, GH * GK])
        ba = sb("d_ba", [P, NP])
        glr = sb("d_glr", [RANK, SEQ])
        z = sb("d_z", [P, NP, SEQ])
        e = sb("d_e", [P, NP, SEQ])
        keep = sb("d_keep", [P, NP, SEQ])
        b = sb("d_b", [P, NP, SEQ])
        eb = sb("d_eb", [P, NP, SEQ])
        enb = sb("d_enb", [P, NP, SEQ])
        ed = sb("d_ed", [P, NP, SEQ])
        decay = sb("d_decay", [P, NP, SEQ // CHUNK])
        qk = sb("d_qk", [P, SLOTS, 2, NP, P])
        v = sb("d_v", [P, SLOTS, GH * GV_W])
        qe = sb("d_qe", [P, SLOTS, NP, P])
        ke = sb("d_ke", [P, SLOTS, NP, P])
        kd = sb("d_kd", [P, SLOTS, NP, P])
        kdT = sb("d_kdT", [P, 2, NP, P])
        att = sb("d_att", [P, 2, 2, NP, P])
        state = sb("d_state", [P, 4, NP, 2 * GV_W])
        out = sb("d_out", [P, 2, GH * GV_W])
        cmask = sb("d_cmask", [P, P], U32)
        p_kd = pb("d_p_kd", [P, NP, P])
        p_att = pb("d_p_att", [P, 2, CH])
        p_o = pb("d_p_o", [P, 2, GH * GV_W])
        p_u = pb("d_p_u", [P, 2, NP, 2 * GV_W])
        const_in = sem("d_const_in")
        qk_in = [sem(f"d_qk_in{q}") for q in range(SLOTS)]
        v_in = [sem(f"d_v_in{q}") for q in range(SLOTS)]
        stored = [sem("d_stored0"), sem("d_stored1")]
        state_out = sem("d_state_out")
        cleared = sem("d_cleared")
        gate_mm = sem("d_gate_mm")
        gate_z = sem("d_gate_z")
        negated = sem("d_negated")
        logs = sem("d_logs")
        log_decay = sem("d_log_decay")
        summed = sem("d_summed")
        e_ready = sem("d_e_ready")
        scaled = sem("d_scaled")
        turns = sem("d_turns")
        kd_done = sem("d_kd_done")
        kd_evacd = sem("d_kd_evacd")
        att_done = sem("d_att_done")
        att_masked = sem("d_att_masked")
        o_done = sem("d_o_done")
        o_evacd = sem("d_o_evacd")
        u_done = sem("d_u_done")
        st_done = sem("d_st_done")

        def in_order(eng, step):
            step(0, 0)
            with eng.Fori(0, NT // SLOTS - 1) as i:
                for k in range(1, SLOTS + 1):
                    step(SLOTS * i + k, k % SLOTS)
            for n in range(NT - SLOTS + 1, NT):
                step(n, n % SLOTS)

        def has(n):
            return not isinstance(n, int) or n < NT

        with nc.Block() as block:

            @block.sync
            def _(sp):
                for dst, src in ((glr, GLs), (wa, A["w_gla_a2"].rearrange("a r k -> (a r) k")), (ba, A["b_gla_a"]),
                                 (cmask, A["chunk_mask"])):
                    sp.dma_start(dst[:, :], src).then_inc(const_in, 16)
                for s in range(2):
                    sp.sem_inc(stored[s], 16)
                with sp.Fori(0, NT // SLOTS) as i:
                    for q in range(SLOTS):
                        n = SLOTS * i + q
                        sp.wait_ge(scaled, LEAD + n - 3)
                        for a, row in ((0, FM_GQ), (1, FM_GK)):
                            sp.dma_start(qk[:, q, a, :, :], FMs[row:row + NP * P, :].rearrange(
                                "(a p) t -> p a t", p=P)[:, :, ds(n * P, P)]).then_inc(qk_in[q], 16)
                        sp.wait_ge(o_done, LEAD + n - 3)
                        sp.dma_start(v[:, q, :], TMs[ds(n * P, P), TM_GV * CH:(TM_GV + 1) * CH]).then_inc(v_in[q], 16)
                sp.wait_ge(st_done, LEAD + 2 * NT)
                for h in range(GH):
                    r = slice(GK * (h % 2), GK * (h % 2) + GK)
                    sp.dma_start(O["gla_prompt"][0, 0, h],
                                 state[r, 2 * NT % 4, h // 2, GV_W * (h % 2):GV_W * (h % 2) + GV_W]
                                 ).then_inc(state_out, 16)
                sp.wait_ge(state_out, 16 * GH)
                for s in range(2):
                    sp.wait_ge(stored[s], 16 + 16 * NT // 2)

            @block.gpsimd
            def _(pool):
                nc.gpsimd.memset(keep[:, :, :], 1.0).then_inc(cleared, 1)
                pool.wait_ge(cleared, 1)
                nc.gpsimd.memset(keep[:, :, :].rearrange("p a (c t) -> p (a c) t", t=CHUNK)[:, :, 0:1], 0.0
                                 ).then_inc(cleared, 1)
                nc.gpsimd.memset(att[:, :, :, :, :], 0.0).then_inc(cleared, 1)
                nc.gpsimd.memset(state[:, :, :, :], 0.0).then_inc(cleared, 1)

            @block.tensor
            def _(pe):
                for s in (kd_done, att_done, o_done, u_done):
                    pe.sem_inc(s, LEAD)
                pe.wait_ge(const_in, 64)
                for a in range(NP):
                    for c in range(SEQ // CH):
                        k = (SEQ // CH) * a + c
                        if k >= 2:
                            pe.wait_ge(gate_z, k - 1)
                        nc.tensor.matmul(p_o[:, k % 2, :], wa[:, a * P:(a + 1) * P], glr[:, c * CH:(c + 1) * CH],
                                         start=True, stop=True).then_inc(gate_mm, 1)
                pe.wait_ge(gate_z, NP * SEQ // CH)
                pe.wait_ge(cleared, 4)

                def within(n, q):
                    pe.wait_ge(scaled, LEAD + n + 1)
                    pe.wait_ge(kd_evacd, LEAD + n)
                    for a in range(NP):
                        last = nc.tensor.transpose(p_kd[:, a, :], kd[:, q, a, :], ident[:, :])
                    last.then_inc(kd_done, 1)
                    pe.wait_ge(att_masked, LEAD + n)
                    for a in range(NP):
                        for h in range(2):
                            r = slice(GK * h, GK * h + GK)
                            last = nc.tensor.matmul(p_att[:, h, a * P:(a + 1) * P], ke[r, q, a, :], qe[r, q, a, :],
                                                    start=True, stop=True)
                    last.then_inc(att_done, 1)

                def step(n, q):
                    s = q % 2
                    if isinstance(n, int) and n == 0:
                        within(0, 0)
                    if has(n + 1):
                        within(n + 1, (q + 1) % SLOTS)
                    pe.wait_ge(v_in[q], 4 * (n - q) + 16)
                    pe.wait_ge(kd_evacd, LEAD + n + 1)
                    for c in range(2):
                        t = slice(CHUNK * c, CHUNK * c + CHUNK)
                        pe.wait_ge(st_done, LEAD + 2 * n + c - 1)
                        for a in range(NP):
                            cols = slice(2 * GV_W * a, 2 * GV_W * (a + 1))
                            last = nc.tensor.matmul(p_u[:, c, a, :], kdT[t, s, a, :], v[t, q, cols], start=True,
                                                    stop=True)
                        last.then_inc(u_done, 1)
                    pe.wait_ge(o_evacd, LEAD + n - 1)
                    pe.wait_ge(att_masked, LEAD + n + 1)
                    for h in range(GH):
                        cols = slice(GV_W * h, GV_W * (h + 1))
                        nc.tensor.matmul(p_o[:, s, cols], att[:, s, h % 2, h // 2, :], v[:, q, cols],
                                         start=(h == 0), stop=False)
                    for c in range(2):
                        t = slice(CHUNK * c, CHUNK * c + CHUNK)
                        pe.wait_ge(st_done, LEAD + 2 * n + c)
                        for a in range(NP):
                            cols = slice(2 * GV_W * a, 2 * GV_W * (a + 1))
                            last = nc.tensor.matmul(p_o[t, s, cols], qe[:, q, a, t], state[:, 2 * s + c, a, :],
                                                    start=False, stop=(a == NP - 1))
                    last.then_inc(o_done, 1)

                in_order(pe, step)

            @block.scalar
            def _(act):
                for s in (kd_evacd, o_evacd):
                    act.sem_inc(s, LEAD)
                for a in range(NP):
                    act.wait_ge(negated, a + 1)
                    nc.scalar.activation(e[:, a, :], e[:, a, :], ACT.Exp).then_inc(logs, 1)
                for a in range(NP):
                    act.wait_ge(logs, a + 1)
                    nc.scalar.activation(e[:, a, :], e[:, a, :], ACT.Ln, bias=1.0).then_inc(logs, 1)
                for a in range(NP):
                    act.wait_ge(summed, 2 * a + 1)
                    nc.scalar.activation(eb[:, a, :], b[:, a, :], ACT.Exp, scale=1.0 / TAU).then_inc(e_ready, 1)
                    nc.scalar.activation(enb[:, a, :], b[:, a, :], ACT.Exp, scale=-1.0 / TAU).then_inc(e_ready, 1)
                    ends = b[:, a, :].rearrange("p (c t) -> p c t", t=CHUNK)[:, :, CHUNK - 1]
                    nc.scalar.activation(decay[:, a, :], ends, ACT.Exp, scale=1.0 / TAU).then_inc(e_ready, 1)
                    act.wait_ge(summed, 2 * a + 2)
                    nc.scalar.activation(ed[:, a, :], e[:, a, :], ACT.Exp, scale=-1.0 / TAU).then_inc(e_ready, 1)

                def kd_evac(n, q):
                    act.wait_ge(kd_done, LEAD + n + 1)
                    act.wait_ge(u_done, LEAD + 2 * (n - 1))
                    nc.scalar.copy(kdT[:, q % 2, :, :], p_kd[:, :, :]).then_inc(kd_evacd, 1)

                def step(n, q):
                    s = q % 2
                    if isinstance(n, int) and n == 0:
                        kd_evac(0, 0)
                    if has(n + 1):
                        kd_evac(n + 1, q + 1)
                    act.wait_ge(o_done, LEAD + n + 1)
                    act.wait_ge(stored[s], 8 * (n - s) + 16)
                    nc.scalar.copy(out[:, s, :], p_o[:, s, :]).then_inc(o_evacd, 1)
                    act.wait_ge(o_evacd, LEAD + n + 1)
                    act.dma_start(OL[ds(n * P, P), :], out[:, s, :]).then_inc(stored[s], 16)

                in_order(act, step)

            @block.vector
            def _(dve):
                V = nc.vector
                for s in (scaled, att_masked, st_done):
                    dve.sem_inc(s, LEAD)
                for a in range(NP):
                    for c in range(SEQ // CH):
                        k = (SEQ // CH) * a + c
                        dve.wait_ge(gate_mm, k + 1)
                        V.tensor_scalar(z[:, a, c * CH:(c + 1) * CH], p_o[:, k % 2, :], ba[:, a:a + 1], None,
                                        ALU.add).then_inc(gate_z, 1)
                    dve.wait_ge(gate_z, (SEQ // CH) * (a + 1))
                    V.scalar_tensor_tensor(out=e[:, a, :], in0=z[:, a, :], scalar=-1.0, in1=z[:, a, :], op0=ALU.mult,
                                           op1=ALU.min).then_inc(negated, 1)
                dve.wait_ge(cleared, 4)
                for a in range(NP):
                    dve.wait_ge(logs, NP + a + 1)
                    V.scalar_tensor_tensor(out=z[:, a, :], in0=z[:, a, :], scalar=0.0, in1=e[:, a, :], op0=ALU.min,
                                           op1=ALU.subtract).then_inc(log_decay, 1)
                    dve.wait_ge(log_decay, a + 1)
                    V.tensor_tensor_scan(b[:, a, :], keep[:, a, :], z[:, a, :], 0.0, ALU.mult, ALU.add
                                         ).then_inc(summed, 1)
                    dve.wait_ge(summed, 2 * a + 1)
                    chunks = lambda x: x[:, a, :].rearrange("p (c t) -> p c t", t=CHUNK)
                    V.tensor_tensor(chunks(e), chunks(b), chunks(b)[:, :, CHUNK - 1:CHUNK].to_broadcast(
                        [P, SEQ // CHUNK, CHUNK]), ALU.subtract).then_inc(summed, 1)
                dve.wait_ge(e_ready, 4 * NP)

                def scale(n, q):
                    dve.wait_ge(qk_in[q], 8 * (n - q) + 32)
                    dve.wait_ge(o_done, LEAD + n - 3)
                    t = ds(n * P, P)
                    V.scalar_tensor_tensor(out=qe[:, q, :, :], in0=qk[:, q, 0, :, :], scalar=GK ** -0.5,
                                           in1=eb[:, :, t], op0=ALU.mult, op1=ALU.mult)
                    V.tensor_tensor(ke[:, q, :, :], qk[:, q, 1, :, :], enb[:, :, t], ALU.mult)
                    V.tensor_tensor(kd[:, q, :, :], qk[:, q, 1, :, :], ed[:, :, t], ALU.mult).then_inc(scaled, 1)

                def keep_causal(n, s):
                    dve.wait_ge(o_done, LEAD + n - 1)
                    dve.wait_ge(att_done, LEAD + n + 1)
                    dve.sem_inc(turns, 1)
                    for h in range(2):
                        last = V.copy_predicated(
                            att[:, s, h, :, :], cmask[:, :].unsqueeze(1).to_broadcast([P, NP, P]),
                            p_att[:, h, 0:NP * P].rearrange("p (a t) -> p a t", a=NP))
                    last.then_inc(att_masked, 1)

                def step(n, q):
                    s = q % 2
                    if isinstance(n, int) and n == 0:
                        scale(0, 0)
                        scale(1, 1)
                        keep_causal(0, 0)
                    if has(n + 2):
                        scale(n + 2, (q + 2) % SLOTS)
                    if has(n + 1):
                        keep_causal(n + 1, 1 - s)
                    for c in range(2):
                        if c == 1:
                            dve.wait_ge(o_done, LEAD + n)
                        dve.wait_ge(u_done, LEAD + 2 * n + c + 1)
                        for h in range(GH):
                            a, r = h // 2, slice(GK * (h % 2), GK * (h % 2) + GK)
                            cols = slice(GV_W * (h % 2), GV_W * (h % 2) + GV_W)
                            last = V.scalar_tensor_tensor(
                                out=state[r, (2 * s + c + 1) % 4, a, cols], in0=state[r, 2 * s + c, a, cols],
                                scalar=decay[r, a, ds(2 * n + c, 1)], in1=p_u[r, c, a, cols],
                                op0=ALU.mult, op1=ALU.add)
                        last.then_inc(st_done, 1)
                        dve.wait_ge(st_done, LEAD + 2 * n + c + 1)

                in_order(dve, step)


class MergeWeights:
    G4 = D // 2 // P
    SLOTS = 3

    def __init__(self, sb, sem):
        self.wb_hi = sb("w_wb_hi", [P, 2, self.G4, D], F32R)
        self.wb_lo = sb("w_wb_lo", [P, 2, self.G4, D], F32R)
        self.wo_hi = sb("w_wo_hi", [P, KC, D], F32R)
        self.wo_lo = sb("w_wo_lo", [P, KC, D], F32R)
        self.gw = sb("w_gw", [P, 1])
        self.gw_in = sem("w_gw_in")
        self.raw_in = [sem(f"w_raw_in{k}") for k in range(self.SLOTS)]
        self.hi_done = sem("w_hi_done")
        self.lo_done = [sem("w_lo_done0"), sem("w_lo_done1")]
        self.gw_done = sem("w_gw_done")
        self.pieces = [("b", a, c) for a in range(2) for c in range(0, self.G4, 2)] + \
                      [("o", 0, c) for c in range(0, KC, 2)]

    def piece(self, A, n):
        kind, a, c = self.pieces[n]
        if kind == "b":
            src = A["w_attn_out" if a == 0 else "w_gla_out"]
            hi, lo = self.wb_hi[:, a, c:c + 2, :], self.wb_lo[:, a, c:c + 2, :]
        else:
            src, hi, lo = A["w_out"], self.wo_hi[:, c:c + 2, :], self.wo_lo[:, c:c + 2, :]
        return hi, lo, src.rearrange("a (c p) e -> p (a c) e", p=P)[:, c:c + 2, :]

    def split_hi(self, nc, act, A, raw, n):
        hi, _, _ = self.piece(A, n)
        if self.pieces[n][:2] == ("b", 1):
            act.wait_ge(self.gw_done, n - 1)
        else:
            act.wait_ge(self.raw_in[n % self.SLOTS], 16 * (n // self.SLOTS) + 16)
        nc.scalar.copy(hi, raw[:, n % self.SLOTS, :, :]).then_inc(self.hi_done, 1)

    def load(self, sp, A, raw):
        sp.dma_start(self.gw[:, :], A["gla_norm_w"].rearrange("a (p b) -> p (a b)", b=1)).then_inc(self.gw_in, 16)
        for n in range(len(self.pieces)):
            last = n - self.SLOTS
            if last >= 0:
                sp.wait_ge(self.lo_done[last % 2], last // 2 + 1)
            _, _, src = self.piece(A, n)
            sp.dma_start(raw[:, n % self.SLOTS, :, :], src).then_inc(self.raw_in[n % self.SLOTS], 16)

    def scale(self, nc, dve, raw, n):
        buf = raw[:, n % self.SLOTS, :, :]
        dve.wait_ge(self.gw_in, 16)
        dve.wait_ge(self.raw_in[n % self.SLOTS], 16 * (n // self.SLOTS) + 16)
        nc.vector.tensor_scalar(buf, buf, self.gw[:, 0:1], None, ALU.mult).then_inc(self.gw_done, 1)

    def split_lo(self, eng, engine, A, raw, n):
        hi, lo, _ = self.piece(A, n)
        eng.wait_ge(self.hi_done, n + 1)
        engine.tensor_tensor(lo, raw[:, n % self.SLOTS, :, :], hi.bitcast(F32), ALU.subtract
                             ).then_inc(self.lo_done[n % 2], 1)


def merge(nc, A, S, O, ident, W):
    TMs, OG, OL = S["tm"], S["og"], S["ol"]
    TILES = NT + 1
    G4 = W.G4
    wb_hi, wb_lo, wo_hi, wo_lo = W.wb_hi, W.wb_lo, W.wo_hi, W.wo_lo
    st, sb, pb, sem = scope(nc)
    with st:
        gates = sb("f_gates", [P, 2, 6 * CH])
        og = sb("f_og", [P, 3, OG_W])
        ol = sb("f_ol", [P, CH])
        x = sb("f_x", [P, 2, D])
        sg = sb("f_sg", [P, 2 * CH])
        bT_hi = sb("f_bT_hi", [P, 2, G4, P], F32R)
        bT_lo = sb("f_bT_lo", [P, 2, G4, P], F32R)
        mT_hi = sb("f_mT_hi", [P, KC, P], F32R)
        mT_lo = sb("f_mT_lo", [P, KC, P], F32R)
        y = sb("f_y", [P, D])
        fw = sb("f_fw", [P, D])
        junk = sb("f_junk", [P, GV_W])
        low = sb("f_low", [P, NH])
        wg = sb("f_wg", [P, 3, NH])
        wd = sb("f_wd", [P, 3, NH])
        den = sb("f_den", [P, 2, NH])
        gn = sb("f_gn", [P, 6, GH])
        fn = sb("f_fn", [P, 6])
        p_t = pb("f_p_t", [P, 2, CH])
        p_b = pb("f_p_b", [P, 2, D])
        p_z = pb("f_p_z", [P, D])

        const_in = sem("f_const_in")
        branch_gates_in = [sem("f_branch_gates_in0"), sem("f_branch_gates_in1")]
        mix_gates_in = [sem("f_mix_gates_in0"), sem("f_mix_gates_in1")]
        x_in = [sem("f_x_in0"), sem("f_x_in1")]
        og_in = sem("f_og_in")
        ol_in = sem("f_ol_in")
        stored = sem("f_stored")
        sig_done = sem("f_sig_done")
        mix_sig_done = sem("f_mix_sig_done")
        diff_done = sem("f_diff_done")
        wexp_done = sem("f_wexp_done")
        gms_done = sem("f_gms_done")
        groot_done = sem("f_groot_done")
        branches = sem("f_branches")
        prep = sem("f_prep")
        t1_done = sem("f_t1_done")
        hi1_done = sem("f_hi1_done")
        lo1_done = sem("f_lo1_done")
        g1_done = sem("f_g1_done")
        mixing = sem("f_mixing")
        silu_done = sem("f_silu_done")
        turns = sem("f_turns")
        mixed = sem("f_mixed")
        t2_done = sem("f_t2_done")
        hi2_done = sem("f_hi2_done")
        lo2_done = sem("f_lo2_done")
        g2_done = sem("f_g2_done")
        y_done = sem("f_y_done")
        sq_done = sem("f_sq_done")
        fms_done = sem("f_fms_done")
        froot_done = sem("f_froot_done")
        fin = sem("f_fin")
        y_ready = sem("f_y_ready")
        L = LEAD
        PREP, FIN = 17, 4

        def rows(t):
            return slice(SEQ - NS, TOK) if isinstance(t, int) and t == NT else ds(t * P, P)

        def has(t):
            return not isinstance(t, int) or 0 <= t < TILES

        with nc.Block() as block:

            @block.sync
            def _(sp):
                sp.dma_start(fw[:, :], A["final_norm_w"].rearrange("(a d) -> a d", a=1).to_broadcast([P, D])
                             ).then_inc(const_in, 16)
                def load_mix_gates(t, s):
                    sp.wait_ge(t2_done, L + t - 1)
                    sp.dma_start(gates[:, s, 2 * CH:], TMs[rows(t), TM_MG * CH:]).then_inc(mix_gates_in[s], 16)

                def load(t, s):
                    sp.wait_ge(t1_done, L + t - 1)
                    sp.dma_start(gates[:, s, 0:2 * CH], TMs[rows(t), TM_AZ * CH:TM_MG * CH]
                                 ).then_inc(branch_gates_in[s], 16)
                    sp.wait_ge(branches, L + t)
                    sp.dma_start(og[:, :, :], OG[rows(t), :, :]).then_inc(og_in, 16)
                    sp.dma_start(ol[:, :], OL[rows(t), :]).then_inc(ol_in, 16)

                def load_x(t, s):
                    sp.wait_ge(sq_done, L + t - 1)
                    if isinstance(t, int) and t == NT:
                        sp.dma_start(x[0:NS, s, :], A["x_prompt"][0, SEQ - NS:SEQ, :]).then_inc(x_in[s], 16)
                        sp.dma_start(x[NS:P, s, :], A["x_sample"].rearrange("b t d -> (b t) d")).then_inc(x_in[s], 16)
                    else:
                        sp.dma_start(x[:, s, :], A["x_prompt"][0, rows(t), :]).then_inc(x_in[s], 16)

                load(0, 0)
                load(1, 1)
                load_mix_gates(0, 0)
                load_mix_gates(1, 1)
                load_x(0, 0)

                def step(t, s):
                    if has(t + 2):
                        load(t + 2, s)
                    if has(t + 1):
                        load_x(t + 1, 1 - s)
                    if has(t + 2):
                        load_mix_gates(t + 2, s)

                step(0, 0)
                with sp.Fori(0, (TILES - 5) // 2) as i:
                    step(2 * i + 1, 1)
                    step(2 * i + 2, 0)
                for t in range(TILES - 4, TILES):
                    step(t, t % 2)
                sp.wait_ge(stored, 16 + 16 * TILES)

            @block.tensor
            def _(pe):
                for s in (t1_done, g1_done, t2_done, g2_done):
                    pe.sem_inc(s, L)

                def transpose_branches(t, s):
                    pe.wait_ge(branches, L + t + 1)
                    for a in range(2):
                        if a == 0:
                            pe.wait_ge(lo2_done, L + t - 1)
                        for c in range(G4):
                            last = nc.tensor.transpose(p_t[:, a, c * P:(c + 1) * P],
                                                       gates[:, s, (G4 * a + c) * P:(G4 * a + c + 1) * P], ident[:, :])
                    last.then_inc(t1_done, 1)

                def product(out, stat_hi, stat_lo, mov_hi, mov_lo, first, last):
                    nc.tensor.matmul(out, stat_hi, mov_hi, start=first, stop=False)
                    nc.tensor.matmul(out, stat_hi, mov_lo, start=False, stop=False)
                    return nc.tensor.matmul(out, stat_lo, mov_hi, start=False, stop=last)

                def step(t, s):
                    if isinstance(t, int) and t == 0:
                        transpose_branches(0, 0)
                    pe.wait_ge(lo1_done, L + t + 1)
                    pe.wait_ge(mixed, L + t)
                    for a in range(2):
                        for e in range(0, D, CH):
                            for c in range(G4):
                                last = product(p_b[:, a, e:e + CH], bT_hi[:, a, c, :], bT_lo[:, a, c, :],
                                               wb_hi[:, a, c, e:e + CH], wb_lo[:, a, c, e:e + CH], c == 0, c == G4 - 1)
                    last.then_inc(g1_done, 1)
                    if has(t + 1):
                        transpose_branches(t + 1, 1 - s)
                    if has(t - 1):
                        out_product(t - 1)
                    pe.wait_ge(mixed, L + t + 1)
                    if has(t + 1):
                        pe.wait_ge(lo1_done, L + t + 2)
                    for c in range(KC):
                        last = nc.tensor.transpose(p_t[:, c // 4, (c % 4) * P:(c % 4 + 1) * P],
                                                   gates[:, s, 2 * CH + c * P:2 * CH + (c + 1) * P], ident[:, :])
                    last.then_inc(t2_done, 1)
                    if isinstance(t, int) and t == TILES - 1:
                        out_product(t)

                def out_product(t):
                    pe.wait_ge(lo2_done, L + t + 1)
                    pe.wait_ge(y_done, L + t)
                    for e in range(0, D, CH):
                        for c in range(KC):
                            last = product(p_z[:, e:e + CH], mT_hi[:, c, :], mT_lo[:, c, :],
                                           wo_hi[:, c, e:e + CH], wo_lo[:, c, e:e + CH], c == 0, c == KC - 1)
                    last.then_inc(g2_done, 1)

                step(0, 0)
                with pe.Fori(0, (TILES - 3) // 2) as i:
                    step(2 * i + 1, 1)
                    step(2 * i + 2, 0)
                step(TILES - 2, 1)
                step(TILES - 1, 0)

            @block.scalar
            def _(act):
                for s in (sig_done, mix_sig_done, wexp_done, groot_done, hi1_done, hi2_done, sq_done, froot_done):
                    act.sem_inc(s, L)
                act.sem_inc(stored, 16)

                def prepare(t, s):
                    act.wait_ge(branch_gates_in[s], 8 * (t - s) + 16)
                    act.wait_ge(branches, L + t)
                    nc.scalar.activation(sg[:, :], gates[:, s, 0:2 * CH], ACT.Sigmoid).then_inc(sig_done, 1)
                    act.wait_ge(diff_done, L + t + 1)
                    nc.scalar.activation(wg[:, :, :], wd[:, :, :], ACT.Exp).then_inc(wexp_done, 1)
                    act.wait_ge(gms_done, L + t + 1)
                    nc.scalar.activation(gn[:, 2, :], gn[:, 1, :], ACT.Sqrt).then_inc(groot_done, 1)

                def mix_gates(t, s):
                    act.wait_ge(mix_gates_in[s], 8 * (t - s) + 16)
                    nc.scalar.activation(gates[:, s, 2 * CH:], gates[:, s, 2 * CH:], ACT.Sigmoid
                                         ).then_inc(mix_sig_done, 1)

                def split_hi1(t):
                    act.wait_ge(t1_done, L + t + 1)
                    nc.scalar.copy(bT_hi[:, :, :, :], p_t[:, :, :]).then_inc(hi1_done, 1)

                def final(t, s):
                    act.wait_ge(y_done, L + t + 1)
                    nc.scalar.activation(x[:, s, :], y[:, :], ACT.Square, accum_out=fn[:, 0:1]).then_inc(sq_done, 1)
                    act.wait_ge(fms_done, L + t + 1)
                    nc.scalar.activation(fn[:, 2:3], fn[:, 1:2], ACT.Sqrt).then_inc(froot_done, 1)
                    act.wait_ge(y_ready, L + t + 1)
                    if isinstance(t, int) and t == NT:
                        act.dma_start(O["y_sample"].rearrange("b t d -> (b t) d"), y[NS:P, :]).then_inc(stored, 16)
                    else:
                        act.dma_start(O["y_prompt"][0, rows(t), :], y[:, :]).then_inc(stored, 16)

                def step(t, s):
                    if isinstance(t, int) and t == 0:
                        prepare(0, 0)
                        split_hi1(0)
                        prepare(1, 1)
                        mix_gates(0, 0)
                        mix_gates(1, 1)
                    if has(t + 1):
                        split_hi1(t + 1)
                    if has(t + 2):
                        prepare(t + 2, s)
                    if has(t - 1):
                        final(t - 1, 1 - s)
                    act.wait_ge(t2_done, L + t + 1)
                    nc.scalar.copy(mT_hi[:, :, :], p_t[:, :, :]).then_inc(hi2_done, 1)
                    if has(t + 2):
                        mix_gates(t + 2, s)
                    if isinstance(t, int) and t == TILES - 1:
                        final(t, s)

                step(0, 0)
                with act.Fori(0, (TILES - 5) // 2) as i:
                    step(2 * i + 1, 1)
                    step(2 * i + 2, 0)
                for t in range(TILES - 4, TILES):
                    step(t, t % 2)

            @block.vector
            def _(dve):
                for s in (diff_done, gms_done, branches, lo1_done, mixed, lo2_done, y_done, fms_done, y_ready):
                    dve.sem_inc(s, L)
                dve.wait_ge(const_in, 16)
                V = nc.vector

                def prepare(t, s):
                    link = Chain(dve, prep, PREP * t)
                    dve.wait_ge(og_in, 16 * t + 16)
                    nm, dn = og[:, :, CH:CH + NH], og[:, :, CH + NH:]
                    link(V.tensor_tensor(low[:, :], nm[:, 0, :], nm[:, 1, :], ALU.min))
                    link(V.tensor_tensor(low[:, :], low[:, :], nm[:, 2, :], ALU.min))
                    V.tensor_tensor(wd[:, :, :], low[:, :].unsqueeze(1).to_broadcast([P, 3, NH]), nm,
                                    ALU.subtract).then_inc(diff_done, 1)
                    dve.wait_ge(ol_in, 16 * t + 16)
                    for h in range(GH):
                        cols = slice(h * GV_W, (h + 1) * GV_W)
                        dve.sem_inc(turns, 1)
                        last = V.tensor_tensor_reduce(out=junk[:, :], in0=ol[:, cols], in1=ol[:, cols], scale=1.0,
                                                      scalar=0.0, op0=ALU.mult, op1=ALU.add, accum_out=gn[:, 0, h:h + 1])
                        link(last)
                    V.tensor_scalar(gn[:, 1, :], gn[:, 0, :], 1.0 / GV_W, EPS, ALU.mult, ALU.add).then_inc(gms_done, 1)
                    dve.wait_ge(wexp_done, L + t + 1)
                    link(V.tensor_tensor(wd[:, :, :], wg[:, :, :], dn, ALU.mult))
                    link(V.tensor_tensor(den[:, 0, :], wd[:, 0, :], wd[:, 1, :], ALU.add))
                    link(V.tensor_tensor(den[:, 0, :], den[:, 0, :], wd[:, 2, :], ALU.add))
                    link(V.reciprocal(den[:, 1, :], den[:, 0, :]))
                    link(V.tensor_tensor(wg[:, :, :], wg[:, :, :], den[:, 1:2, :].to_broadcast([P, 3, NH]), ALU.mult))
                    sums = og[:, :, 0:CH].rearrange("p g (h e) -> p g h e", h=NH)
                    link(V.tensor_tensor(sums, sums, wg[:, :, :].unsqueeze(3).to_broadcast([P, 3, NH, HD]), ALU.mult))
                    V.tensor_tensor(og[:, 0, 0:CH], og[:, 0, 0:CH], og[:, 1, 0:CH], ALU.add)
                    dve.wait_ge(groot_done, L + t + 1)
                    link(V.reciprocal(gn[:, 3, :], gn[:, 2, :]))
                    V.tensor_tensor(og[:, 0, 0:CH], og[:, 0, 0:CH], og[:, 2, 0:CH], ALU.add)
                    link(V.tensor_tensor(gn[:, 4, :], gn[:, 3, :], gn[:, 3, :], ALU.mult))
                    link(V.tensor_tensor(gn[:, 4, :], gn[:, 4, :], gn[:, 1, :], ALU.mult))
                    link(V.tensor_scalar(gn[:, 4, :], gn[:, 4, :], -0.5, 1.5, ALU.mult, ALU.add))
                    link(V.tensor_tensor(gn[:, 5, :], gn[:, 3, :], gn[:, 4, :], ALU.mult))
                    heads = ol[:, :].rearrange("p (h e) -> p h e", h=GH)
                    V.tensor_tensor(heads, heads, gn[:, 5, :].unsqueeze(2).to_broadcast([P, GH, GV_W]), ALU.mult)
                    dve.wait_ge(sig_done, L + t + 1)
                    link2 = V.tensor_tensor(gates[:, s, 0:2 * CH], gates[:, s, 0:2 * CH], sg[:, :], ALU.mult)
                    link2.then_inc(silu_done, 1)
                    dve.wait_ge(silu_done, t + 1)
                    V.tensor_tensor(gates[:, s, 0:CH], gates[:, s, 0:CH], og[:, 0, 0:CH], ALU.mult)
                    V.tensor_tensor(gates[:, s, CH:2 * CH], gates[:, s, CH:2 * CH], ol[:, :],
                                    ALU.mult).then_inc(branches, 1)
                    assert link.links == PREP, link.links

                def split_lo1(t):
                    dve.wait_ge(hi1_done, L + t + 1)
                    V.tensor_tensor(bT_lo[:, :, :, :], p_t[:, :, :].rearrange("p a (c t) -> p a c t", c=G4),
                                    bT_hi[:, :, :, :].bitcast(F32), ALU.subtract).then_inc(lo1_done, 1)

                def mix(t, s):
                    dve.wait_ge(mix_sig_done, L + t + 1)
                    dve.wait_ge(g1_done, L + t + 1)
                    m = gates[:, s, 2 * CH:].rearrange("p (a e) -> p a e", a=2)
                    V.tensor_tensor(m, m, p_b[:, :, :], ALU.mult).then_inc(mixing, 1)
                    dve.wait_ge(mixing, t + 1)
                    V.tensor_tensor(m[:, 0, :], m[:, 0, :], m[:, 1, :], ALU.add).then_inc(mixed, 1)

                def final(t, s):
                    link = Chain(dve, fin, FIN * t)
                    dve.wait_ge(g2_done, L + t + 1)
                    dve.wait_ge(x_in[s], 8 * (t - s) + (32 if isinstance(t, int) and t == NT else 16))
                    dve.wait_ge(stored, 16 * t + 16)
                    V.tensor_tensor(y[:, :], x[:, s, :], p_z[:, :], ALU.add).then_inc(y_done, 1)
                    dve.wait_ge(sq_done, L + t + 1)
                    m = [fn[:, j:j + 1] for j in range(6)]
                    V.tensor_scalar(m[1], m[0], 1.0 / D, EPS, ALU.mult, ALU.add).then_inc(fms_done, 1)
                    dve.wait_ge(froot_done, L + t + 1)
                    rsqrt_steps(nc, dve, fin, FIN * t, m)
                    V.scalar_tensor_tensor(out=y[:, :], in0=y[:, :], scalar=m[2], in1=fw[:, :], op0=ALU.mult,
                                           op1=ALU.mult).then_inc(y_ready, 1)

                def step(t, s):
                    if isinstance(t, int) and t == 0:
                        prepare(0, 0)
                        split_lo1(0)
                        prepare(1, 1)
                    mix(t, s)
                    if has(t + 1):
                        split_lo1(t + 1)
                    if has(t + 2):
                        prepare(t + 2, s)
                    if has(t - 1):
                        final(t - 1, 1 - s)
                    dve.wait_ge(hi2_done, L + t + 1)
                    V.tensor_tensor(mT_lo[:, :, :], p_t[:, :, :].rearrange("p a (c t) -> p (a c) t", c=4),
                                    mT_hi[:, :, :].bitcast(F32), ALU.subtract).then_inc(lo2_done, 1)
                    if isinstance(t, int) and t == TILES - 1:
                        final(t, s)

                step(0, 0)
                with dve.Fori(0, (TILES - 5) // 2) as i:
                    step(2 * i + 1, 1)
                    step(2 * i + 2, 0)
                for t in range(TILES - 4, TILES):
                    step(t, t % 2)


ROWS = 2 * T * NH


class SampleBuffers:

    def __init__(self, sb, sem):
        self.vc = sb("e_vc", [P, 2, 2, NU, CH])
        self.vn = sb("e_vn", [2 * T, 2, 3, CH])
        self.sn = sb("e_sn", [NS, 3, 2, T * NH])
        self.mask = sb("e_mask", [P, 3, P + T])
        self.diag = sb("e_diag", [P, CH])
        self.const_in = sem("e_const_in")
        self.kn_in = sem("e_kn_in")
        self.qn_in = sem("e_qn_in")
        self.v_in = [sem("e_v_in0"), sem("e_v_in1")]
        self.link = sem("e_link")

    V_IN = 16 * (2 * 3 + 1)

    def load_v(self, eng, A, S, i, s, pace=lambda m: None):
        for b in range(2):
            for g in range(3):
                pace(3 * b + g)
                eng.dma_start(self.vc[:, s, b, UNIT0[g]:UNIT0[g] + UNITS[g], :], cached(A, g, 2 * i + b, 1)
                              ).then_inc(self.v_in[s], 16)
        eng.dma_start(self.vn[:, s, :, :], S["tm"][ds(SEQ + 2 * i * T, 2 * T), 6 * CH:9 * CH]
                      ).then_inc(self.v_in[s], 16)

    def new_key_scores(self, nc, pool, A, S, kn, qn):
        TS = S["tm"][SEQ:TOK, :]
        pool.dma_start(self.mask[:, :, :], A["dec_mask"]).then_inc(self.const_in, 16)
        pool.dma_start(self.diag[:, :], A["dec_diag"]).then_inc(self.const_in, 16)
        pool.dma_start(kn[:, :, :], TS[:, 3 * CH:6 * CH]).then_inc(self.kn_in, 16)
        pool.wait_ge(self.kn_in, 16)
        link = Chain(pool, self.link, 0)
        for g in range(3):
            for b in range(DB):
                src = TS[T * b:T * b + T, g * CH:(g + 1) * CH]
                pool.dma_start(qn[T * b:T * b + T, :, :], src.unsqueeze(0).to_broadcast([T, T, CH])
                               ).then_inc(self.qn_in, 16)
            pool.wait_ge(self.qn_in, 16 * DB * (g + 1))
            link(nc.gpsimd.tensor_tensor(qn[:, :, :], qn[:, :, :], kn[:, g:g + 1, :].to_broadcast([NS, T, CH]),
                                         ALU.mult))
            prod = qn[:, :, :].rearrange("p t (h e) -> p (t h) e", h=NH)
            half = HD // 2
            while half:
                if half > 1:
                    link(nc.gpsimd.tensor_tensor(prod[:, :, 0:half], prod[:, :, 0:half], prod[:, :, half:2 * half],
                                                 ALU.add))
                else:
                    for twice in range(2):
                        last = nc.gpsimd.tensor_tensor(self.sn[:, g, twice, :].unsqueeze(2), prod[:, :, 0:1],
                                                       prod[:, :, 1:2], ALU.add)
                    link(last)
                half //= 2


def attend_sample(nc, A, S, ident, sT, E):
    OG, OA = S["og"], S["oa"]
    NB = DB // 2
    vc, vn, sn, mask, diag = E.vc, E.vn, E.sn, E.mask, E.diag
    st, sb, pb, sem = scope(nc)
    with st:
        sp_ = sb("e_sp", [P, 2, 3, ROWS])
        snT = sb("e_snT", [P, 3, NS])
        sn2 = sb("e_sn2", [P, 2, 3, T])
        s = sb("e_s", [P, 2, 3, P + T])
        mx = sb("e_mx", [P, 2, 2, 3])
        nm = sb("e_nm", [P, 2, 3])
        dn = sb("e_dn", [P, 2, 3])
        lw = sb("e_lw", [P, 2, 1])
        wg = sb("e_wg", [P, 2, 3])
        wd = sb("e_wd", [P, 2, 3])
        ds_ = sb("e_ds", [P, 2])
        pn = sb("e_pn", [P, 2, 3, 2 * T])
        pnT = sb("e_pnT", [2 * T, 2, 3, P])
        pm0 = sb("e_pm0", [P, 2, ROWS])
        pm1 = sb("e_pm1", [P, 2, 2, 4 * 72])
        pm2 = sb("e_pm2", [P, 2, 2, 8 * 72])
        po = sb("e_po", [P, 3, CH])
        oa = sb("e_oa", [P, 2, HD])
        fill = sb("e_fill", [NS, 3, OG_W])
        p_s = pb("e_p_s", [P, 2, 4, P])
        p_sn = pb("e_p_sn", [P, 3, NS])
        p_p = pb("e_p_p", [P, 3, P])
        p_pn = pb("e_p_pn", [2 * T, 3, P])
        p_o = pb("e_p_o", [P, 3, CH])

        stored = [sem("e_stored0"), sem("e_stored1")]
        filled = sem("e_filled")
        cleared = sem("e_cleared")
        turns = sem("e_turns")
        chain = sem("e_chain")
        snT_done = sem("e_snT_done")
        picked = sem("e_picked")
        sT_done = sem("e_sT_done")
        maxed = sem("e_maxed")
        exp_done = sem("e_exp_done")
        wexp_done = sem("e_wexp_done")
        p_ready = sem("e_p_ready")
        pT_done = sem("e_pT_done")
        pm_done = sem("e_pm_done")
        pv_done = sem("e_pv_done")
        lowest = sem("e_lowest")
        out_ready = sem("e_out_ready")
        L = LEAD
        LINKS = 12

        with nc.Block() as block:

            @block.sync
            def _(sp):
                sp.wait_ge(cleared, 6)
                sp.dma_start(OG[SEQ:TOK, :, :], fill[:, :, :]).then_inc(filled, 16)
                sp.wait_ge(filled, 16)
                for k in range(2):
                    sp.wait_ge(stored[k], 16 + 16 * NB // 2)
                sp.dma_start(OG[SEQ:TOK, 0, 0:CH], OA.rearrange("(t h) e -> t (h e)", h=NH)).then_inc(filled, 16)
                sp.wait_ge(filled, 32)

            @block.gpsimd
            def _(pool):
                nc.gpsimd.memset(pn[:, :, :, :], 0.0).then_inc(cleared, 1)
                nc.gpsimd.memset(pm1[:, :, :, :], 0.0).then_inc(cleared, 1)
                nc.gpsimd.memset(pm2[:, :, :, :], 0.0).then_inc(cleared, 1)
                nc.gpsimd.memset(fill[:, :, :], 0.0).then_inc(cleared, 1)
                pool.wait_ge(cleared, 4)
                nc.gpsimd.memset(fill[:, 0, CH + NH:], 1.0).then_inc(cleared, 1)
                pool.sem_inc(cleared, 1)
                pool.wait_ge(cleared, 6)
                for n in range(2, NB):
                    pool.wait_ge(pv_done, L + n - 1)
                    E.load_v(pool, A, S, n, n % 2)

            @block.tensor
            def _(pe):
                for x in (sT_done, pT_done, pv_done):
                    pe.sem_inc(x, L)
                for g in range(3):
                    last = nc.tensor.transpose(p_sn[:, g, :], sn[:, g, :, :], ident[0:NS, 0:NS])
                last.then_inc(snT_done, 1)
                with pe.Fori(0, NB // 2) as i:
                    for k in range(2):
                        n = 2 * i + k
                        pe.wait_ge(picked, L + n + 1)
                        pe.wait_ge(maxed, L + n - 1)
                        for g in range(3):
                            last = nc.tensor.transpose(p_s[:, k, g, :], sp_[:, k, g, :], ident[:, :])
                        last.then_inc(sT_done, 1)
                    for k in range(2):
                        n = 2 * i + k
                        pe.wait_ge(p_ready, L + n + 1)
                        pe.wait_ge(pm_done, L + n)
                        for g in range(3):
                            nc.tensor.transpose(p_p[:, g, :], s[:, k, g, 0:P], ident[:, :])
                            last = nc.tensor.transpose(p_pn[:, g, :], pn[:, k, g, :], ident[:, :])
                        last.then_inc(pT_done, 1)
                        pe.wait_ge(pm_done, L + n + 1)
                        pe.wait_ge(E.v_in[k], E.V_IN * i + E.V_IN)
                        pe.wait_ge(out_ready, L + n)
                        for g in range(3):
                            nc.tensor.matmul(p_o[:, g, :], pnT[:, k, g, :], vn[:, k, g, :], start=True, stop=False)
                            for b in range(2):
                                for c in range(UNITS[g]):
                                    if g == 0:
                                        stat = pm0[:, k, 64 * b:64 * b + 64]
                                    else:
                                        stat = (pm1, pm2)[g - 1][:, k, b, 64 * c:64 * c + 64]
                                    last = nc.tensor.matmul(p_o[64 * b:64 * b + 64, g, :], stat,
                                                            vc[:, k, b, UNIT0[g] + c, :], start=False,
                                                            stop=(c == UNITS[g] - 1))
                        last.then_inc(pv_done, 1)

            @block.scalar
            def _(act):
                for x in (picked, exp_done, wexp_done, pm_done):
                    act.sem_inc(x, L)
                for k in range(2):
                    act.sem_inc(stored[k], 16)
                act.wait_ge(cleared, 6)
                with act.Fori(0, NB // 2) as i:
                    for k in range(2):
                        n = 2 * i + k
                        act.wait_ge(sT_done, L + n - 1)
                        nc.scalar.copy(sp_[:, k, :, :], sT[:, :, ds(n * ROWS, ROWS)]).then_inc(picked, 1)
                    for k in range(2):
                        n = 2 * i + k
                        act.wait_ge(maxed, L + n + 1)
                        for g in range(3):
                            last = nc.scalar.activation(s[:, k, g, :], s[:, k, g, :], ACT.Exp, bias=nm[:, k, g:g + 1],
                                                        accum_out=dn[:, k, g:g + 1])
                        last.then_inc(exp_done, 1)
                        act.wait_ge(lowest, L + n + 1)
                        nc.scalar.activation(wg[:, k, :], wd[:, k, :], ACT.Exp).then_inc(wexp_done, 1)
                    for k in range(2):
                        n = 2 * i + k
                        act.wait_ge(pT_done, L + n + 1)
                        act.wait_ge(pv_done, L + n - 1)
                        nc.scalar.copy(pnT[:, k, :, :], p_pn[:, :, :])
                        nc.scalar.copy(pm0[:, k, :], p_p[:, 0, :])
                        d1 = pm1[:, k, :, :].rearrange("p b (c x) -> p b c x", x=72)
                        s1 = p_p[:, 1, :].rearrange("p (b a c h) -> p b a c h", b=2, a=2, c=4)
                        for a in range(2):
                            nc.scalar.copy(d1[:, :, :, 32 * a:32 * a + NH], s1[:, :, a, :, :])
                        d2 = pm2[:, k, :, :].rearrange("p b (c x) -> p b c x", x=72)
                        nc.scalar.copy(d2[:, :, :, 0:NH], p_p[:, 2, :].rearrange("p (b c h) -> p b c h", b=2, c=8)
                                       ).then_inc(pm_done, 1)
                    for k in range(2):
                        n = 2 * i + k
                        act.wait_ge(out_ready, L + n + 1)
                        act.dma_start(OA[ds(n * ROWS, ROWS), :], oa[:, k, :]).then_inc(stored[k], 16)

            @block.vector
            def _(dve):
                V = nc.vector
                for x in (maxed, p_ready, lowest, out_ready):
                    dve.sem_inc(x, L)
                dve.wait_ge(E.const_in, 32)
                dve.wait_ge(snT_done, 1)
                V.tensor_copy(snT[:, :, :], p_sn[:, :, :]).then_inc(chain, 1)
                dve.wait_ge(chain, 1)
                dve.wait_ge(cleared, 6)
                with dve.Fori(0, NB // 2) as i:
                    link = Chain(dve, chain, 1 + (2 * LINKS) * i)

                    def softmax(n, k):
                        for b in range(2):
                            last = V.tensor_copy(sn2[64 * b:64 * b + 64, k, :, :],
                                                 snT[64 * b:64 * b + 64, :, ds((2 * n + b) * T, T)])
                        link(last)
                        dve.wait_ge(pT_done, L + n - 1)
                        dve.wait_ge(sT_done, L + n + 1)
                        for g in range(3):
                            dve.sem_inc(turns, 1)
                            V.tensor_tensor_reduce(out=s[:, k, g, 0:P], in0=p_s[:, k, g, :], in1=mask[:, g, 0:P],
                                                   scale=HD ** -0.5, scalar=LOWEST, op0=ALU.add, op1=ALU.max,
                                                   accum_out=mx[:, k, 0, g:g + 1])
                            last = V.tensor_tensor_reduce(out=s[:, k, g, P:], in0=sn2[:, k, g, :], in1=mask[:, g, P:],
                                                          scale=HD ** -0.5, scalar=LOWEST, op0=ALU.add, op1=ALU.max,
                                                          accum_out=mx[:, k, 1, g:g + 1])
                        link(last)
                        link(V.tensor_tensor(nm[:, k, :], mx[:, k, 0, :], mx[:, k, 1, :], ALU.max))
                        link(V.tensor_scalar(nm[:, k, :], nm[:, k, :], -1.0, None, ALU.mult))
                        dve.sem_inc(maxed, 1)
                        link(V.tensor_reduce(lw[:, k, :], nm[:, k, :], AX_X, ALU.min))
                        link(V.tensor_scalar(wd[:, k, :], nm[:, k, :], -1.0, lw[:, k, 0:1], ALU.mult, ALU.add))
                        dve.sem_inc(lowest, 1)

                    def place(n, k):
                        dve.wait_ge(exp_done, L + n + 1)
                        for b in range(2):
                            last = V.tensor_copy(pn[64 * b:64 * b + 64, k, :, T * b:T * b + T],
                                                 s[64 * b:64 * b + 64, k, :, P:])
                        last.then_inc(p_ready, 1)

                    def weights(n, k):
                        dve.wait_ge(wexp_done, L + n + 1)
                        link(V.tensor_tensor(wd[:, k, :], wg[:, k, :], dn[:, k, :], ALU.mult))
                        link(V.tensor_reduce(ds_[:, 0:1], wd[:, k, :], AX_X, ALU.add))
                        link(V.reciprocal(ds_[:, 1:2], ds_[:, 0:1]))
                        link(V.tensor_scalar(wg[:, k, :], wg[:, k, :], ds_[:, 1:2], None, ALU.mult))

                    def output(n, k):
                        dve.wait_ge(pv_done, L + n + 1)
                        dve.wait_ge(stored[k], 16 * i + 16)
                        for g in range(3):
                            last = V.scalar_tensor_tensor(out=po[:, g, :], in0=p_o[:, g, :], scalar=wg[:, k, g:g + 1],
                                                          in1=diag[:, :], op0=ALU.mult, op1=ALU.mult)
                        link(last)
                        link(V.tensor_reduce(oa[:, k, :], po[:, :, :].rearrange("p g (h e) -> p e (g h)", h=NH), AX_X,
                                             ALU.add))
                        dve.sem_inc(out_ready, 1)

                    for k in range(2):
                        softmax(2 * i + k, k)
                    for k in range(2):
                        place(2 * i + k, k)
                    for k in range(2):
                        weights(2 * i + k, k)
                    for k in range(2):
                        output(2 * i + k, k)
                    assert link.links == 2 * LINKS, link.links


def gla_sample(nc, A, S, O, ident, W):
    TMs, TSs, OL = S["tm"], S["ts"], S["ol"]
    NP = GH // 2
    st, sb, pb, sem = scope(nc)
    with st:
        wa = sb("g_wa", [RANK, GH * GK])
        ba = sb("g_ba", [P, NP])
        raw = sb("g_raw", [NS, TS_W])
        v = sb("g_v", [NS, GH * GV_W])
        state = sb("g_state", [P, DB, NP, 2 * GV_W])
        new = sb("g_new", [P, DB, NP, GV_W])
        f = sb("g_f", [P, 4, NS])
        fr = sb("g_fr", [RANK, NS])
        z = sb("g_z", [P, NP, NS])
        e = sb("g_e", [P, NP, NS])
        keep = sb("g_keep", [P, NP, NS])
        b = sb("g_b", [P, NP, NS])
        eb = sb("g_eb", [P, 3, NP, NS])
        decay = sb("g_decay", [P, NP, DB])
        qe = sb("g_qe", [P, NP, NS])
        ke = sb("g_ke", [P, NP, NS])
        kd = sb("g_kd", [P, NP, NS])
        qm = sb("g_qm", [P, NP, DB * 72])
        km = sb("g_km", [NS, NP, DB, P])
        att = sb("g_att", [NS, 2, NP, NS])
        cmask = sb("g_cmask", [NS, NS], U32)
        bmask = sb("g_bmask", [NS, DB])
        out = sb("g_out", [NS, GH * GV_W])
        w_raw = sb("g_w_raw", [P, W.SLOTS, 2, D])
        p_f = pb("g_p_f", [P, 4, NS])
        p_r = pb("g_p_r", [RANK, NS])
        p_g = pb("g_p_g", [P, NP, NS])
        p_att = pb("g_p_att", [NS, 2, CH])
        p_o = pb("g_p_o", [NS, GH * GV_W])
        p_u = pb("g_p_u", [P, 2, CH])
        in_ = sem("g_in")
        st_in = sem("g_st_in")
        cleared = sem("g_cleared")
        t_done = sem("g_t_done")
        t_evacd = sem("g_t_evacd")
        g_done = sem("g_g_done")
        z_done = sem("g_z_done")
        gate = sem("g_gate")
        d = sem("g_d")
        e_ready = sem("g_e_ready")
        kd_ready = sem("g_kd_ready")
        kdT_done = sem("g_kdT_done")
        km_done = sem("g_km_done")
        att_done = sem("g_att_done")
        att_masked = sem("g_att_masked")
        o_done = sem("g_o_done")
        o_evacd = sem("g_o_evacd")
        u_done = sem("g_u_done")
        u_read = sem("g_u_read")
        stored = sem("g_stored")
        with nc.Block() as block:

            @block.sync
            def _(sp):
                for dst, src in ((raw[:, :], TSs), (v[:, :], TMs[SEQ:TOK, TM_GV * CH:(TM_GV + 1) * CH]),
                                 (wa[:, :], A["w_gla_a2"].rearrange("a r k -> (a r) k")), (ba[:, :], A["b_gla_a"]),
                                 (cmask[:, :], A["sample_mask"]), (bmask[:, :], A["batch_mask"])):
                    sp.dma_start(dst, src).then_inc(in_, 16)
                sp.wait_ge(cleared, 1)
                for h in range(GH):
                    r, c = slice(GK * (h % 2), GK * (h % 2) + GK), slice(GV_W * (h % 2), GV_W * (h % 2) + GV_W)
                    sp.dma_start(state[r, :, h // 2, c], A["state_gla"][0, :, h, :, :].rearrange("b k v -> k b v")
                                 ).then_inc(st_in, 16)
                W.load(sp, A, w_raw)
                sp.wait_ge(o_evacd, 1)
                sp.dma_start(OL[SEQ:TOK, :], out[:, :]).then_inc(stored, 16)
                sp.wait_ge(u_read, DB * NP)
                for h in range(GH):
                    r = slice(GK * (h % 2), GK * (h % 2) + GK)
                    sp.dma_start(O["gla_sample"][0, :, h, :, :].rearrange("b k v -> k b v"), new[r, :, h // 2, :]
                                 ).then_inc(stored, 16)
                sp.wait_ge(stored, 16 + 16 * GH)

            @block.gpsimd
            def _(pool):
                nc.gpsimd.memset(state[:, :, :, :], 0.0).then_inc(cleared, 1)
                nc.gpsimd.memset(keep[:, :, :], 1.0).then_inc(cleared, 1)
                nc.gpsimd.memset(qm[:, :, :], 0.0).then_inc(cleared, 1)
                nc.gpsimd.memset(att[:, :, :, :], 0.0).then_inc(cleared, 1)
                pool.wait_ge(cleared, 4)
                nc.gpsimd.memset(keep[:, :, :].rearrange("p a (c t) -> p (a c) t", t=T)[:, :, 0:1], 0.0
                                 ).then_inc(cleared, 1)
                for n in range(0, len(W.pieces), 2):
                    W.split_lo(pool, nc.gpsimd, A, w_raw, n)

            @block.tensor
            def _(pe):
                pe.wait_ge(in_, 96)
                for c in range(4):
                    nc.tensor.transpose(p_f[:, c, :], raw[:, c * P:(c + 1) * P], ident[0:NS, 0:NS])
                nc.tensor.transpose(p_r[:, :], raw[:, 4 * P:4 * P + RANK], ident[0:NS, 0:NS]).then_inc(t_done, 1)
                pe.wait_ge(t_evacd, 2)
                for a in range(NP):
                    last = nc.tensor.matmul(p_g[:, a, :], wa[:, a * P:(a + 1) * P], fr[:, :], start=True, stop=True)
                last.then_inc(g_done, 1)
                pe.wait_ge(kd_ready, 1)
                for a in range(NP):
                    last = nc.tensor.transpose(p_f[0:NS, 2 * a:2 * a + 2, :], kd[:, a, :], ident[:, :])
                last.then_inc(kdT_done, 1)
                for a in range(NP):
                    for h in range(2):
                        r = slice(GK * h, GK * h + GK)
                        last = nc.tensor.matmul(p_att[:, h, a * NS:(a + 1) * NS], ke[r, a, :], qe[r, a, :],
                                                start=True, stop=True)
                last.then_inc(att_done, 1)
                pe.wait_ge(st_in, 16 * GH)
                pe.wait_ge(km_done, NP)
                for a in range(NP):
                    for j in range(DB):
                        nc.tensor.matmul(p_o[:, 2 * GV_W * a:2 * GV_W * (a + 1)], qm[:, a, NS * j:NS * j + NS],
                                         state[:, j, a, :], start=(a == 0 and j == 0), stop=False)
                pe.wait_ge(att_masked, 1)
                for h in range(GH):
                    cols = slice(GV_W * h, GV_W * (h + 1))
                    last = nc.tensor.matmul(p_o[:, cols], att[:, h % 2, h // 2, :], v[:, cols], start=False,
                                            stop=(h == GH - 1))
                last.then_inc(o_done, 1)
                for j in range(DB):
                    for a in range(NP):
                        n = NP * j + a
                        if n >= 2:
                            pe.wait_ge(u_read, n - 1)
                        nc.tensor.matmul(p_u[:, n % 2, 0:2 * GV_W], km[:, a, j, :], v[:, 2 * GV_W * a:2 * GV_W * (a + 1)],
                                         start=True, stop=True).then_inc(u_done, 1)

            @block.scalar
            def _(act):
                hi = lambda n: W.split_hi(nc, act, A, w_raw, n)
                act.wait_ge(t_done, 1)
                nc.scalar.copy(f[:, :, :], p_f[:, :, :]).then_inc(t_evacd, 1)
                nc.scalar.copy(fr[:, :], p_r[:, :]).then_inc(t_evacd, 1)
                log_gates(nc, act, None, z[:, :, :], e[:, :, :], gate, None)
                hi(0)
                hi(1)
                act.wait_ge(d, 1)
                nc.scalar.activation(eb[:, 0, :, :], b[:, :, :], ACT.Exp, scale=1.0 / TAU).then_inc(e_ready, 1)
                nc.scalar.activation(eb[:, 1, :, :], b[:, :, :], ACT.Exp, scale=-1.0 / TAU).then_inc(e_ready, 1)
                ends = b[:, :, :].rearrange("p a (c t) -> p a c t", t=T)[:, :, :, T - 1]
                nc.scalar.activation(decay[:, :, :], ends, ACT.Exp, scale=1.0 / TAU).then_inc(e_ready, 1)
                act.wait_ge(d, 2)
                nc.scalar.activation(eb[:, 2, :, :], e[:, :, :], ACT.Exp, scale=-1.0 / TAU).then_inc(e_ready, 1)
                hi(2)
                hi(3)
                act.wait_ge(o_done, 1)
                nc.scalar.copy(out[:, :], p_o[:, :]).then_inc(o_evacd, 1)
                for n in range(4, len(W.pieces)):
                    hi(n)

            @block.vector
            def _(dve):
                V = nc.vector
                dve.wait_ge(in_, 96)
                dve.wait_ge(cleared, 5)
                dve.wait_ge(g_done, 1)
                for a in range(NP):
                    last = V.tensor_scalar(z[:, a, :], p_g[:, a, :], ba[:, a:a + 1], None, ALU.add)
                last.then_inc(z_done, 1)
                dve.wait_ge(z_done, 1)
                log_gates(nc, None, dve, z[:, :, :], e[:, :, :], gate, None)
                flat = lambda x: x[:, :, :].rearrange("p a t -> p (a t)")
                V.tensor_tensor_scan(flat(b), flat(keep), flat(z), 0.0, ALU.mult, ALU.add).then_inc(d, 1)
                dve.wait_ge(d, 1)
                chunks = lambda x: x[:, :, :].rearrange("p a (c t) -> p (a c) t", t=T)
                V.tensor_tensor(chunks(e), chunks(b), chunks(b)[:, :, T - 1:T].to_broadcast([P, NP * DB, T]),
                                ALU.subtract).then_inc(d, 1)
                dve.wait_ge(e_ready, 4)
                dve.wait_ge(t_evacd, 2)
                V.scalar_tensor_tensor(out=qe[:, :, :], in0=f[:, 0:2, :], scalar=GK ** -0.5, in1=eb[:, 0, :, :],
                                       op0=ALU.mult, op1=ALU.mult)
                V.tensor_tensor(ke[:, :, :], f[:, 2:4, :], eb[:, 1, :, :], ALU.mult)
                V.tensor_tensor(kd[:, :, :], f[:, 2:4, :], eb[:, 2, :, :], ALU.mult).then_inc(kd_ready, 1)
                W.scale(nc, dve, w_raw, 2)
                W.split_lo(dve, V, A, w_raw, 1)
                dve.wait_ge(kd_ready, 1)
                V.tensor_copy(qm[:, :, :].rearrange("p a (j x) -> p a j x", x=72)[:, :, :, 0:T],
                              qe[:, :, :].rearrange("p a (j t) -> p a j t", t=T))
                dve.wait_ge(kdT_done, 1)
                for a in range(NP):
                    V.tensor_tensor(km[:, a, :, :],
                                    p_f[0:NS, 2 * a:2 * a + 2, :].rearrange("p x t -> p (x t)").unsqueeze(1)
                                    .to_broadcast([NS, DB, P]),
                                    bmask[:, :].unsqueeze(2).to_broadcast([NS, DB, P]), ALU.mult).then_inc(km_done, 1)
                dve.wait_ge(att_done, 1)
                for h in range(2):
                    last = V.copy_predicated(att[:, h, :, :], cmask[:, :].unsqueeze(1).to_broadcast([NS, NP, NS]),
                                             p_att[:, h, 0:NP * NS].rearrange("p (a t) -> p a t", a=NP))
                last.then_inc(att_masked, 1)
                W.scale(nc, dve, w_raw, 3)
                W.split_lo(dve, V, A, w_raw, 3)
                dve.wait_ge(st_in, 16 * GH)
                for j in range(DB):
                    if j in (2, 5):
                        W.split_lo(dve, V, A, w_raw, 5 if j == 2 else 7)
                    for a in range(NP):
                        n = NP * j + a
                        dve.wait_ge(u_done, n + 1)
                        for h in range(2):
                            r, c = slice(GK * h, GK * h + GK), slice(GV_W * h, GV_W * h + GV_W)
                            last = V.scalar_tensor_tensor(out=new[r, j, a, :], in0=state[r, j, a, c],
                                                          scalar=decay[r, a, j:j + 1], in1=p_u[r, n % 2, c],
                                                          op0=ALU.mult, op1=ALU.add)
                        last.then_inc(u_read, 1)


def store_windows(pool, S, O, done, pace):
    TMs = S["tm"]
    n = 0
    for g, win in enumerate(WINDOWS):
        rows = min(win, SEQ)
        for kv in range(2):
            cols = slice((3 + 3 * kv + g) * CH, (4 + 3 * kv + g) * CH)
            new = O[f"kv_w{win}_sample"][0, :, :, kv, :, :].rearrange("b t h e -> (b t) (h e)")
            out = O[f"kv_w{win}_prompt"][0, 0, :, kv, :, :].rearrange("s h e -> s (h e)")
            for r in range(0, rows, 256):
                end = min(r + 256, rows)
                pace(n)
                pool.dma_start(out[r:end, :], TMs[SEQ - rows + r:SEQ - rows + end, cols]).then_inc(done, 16)
                n += 1
            pool.dma_start(new, TMs[SEQ:TOK, cols]).then_inc(done, 16)
            n += 1
    return n


def decoder_step(nc, A, O):
    S = {name: nc.dram_tensor(name, shape, F32, kind="Internal").ap()
         for name, shape in (("tm", (TOK, TM_W)), ("ts", (NS, TS_W)), ("fm", (CH, SEQ)), ("gl", (RANK, SEQ)),
                             ("og", (TOK, 3, OG_W)), ("ol", (TOK, GH * GV_W)), ("oa", (NS * NH, HD)))}
    st, sb, _, sem = scope(nc)
    with st:
        ident = sb("ident", [P, P])
        ident_in = sem("ident_in")
        with nc.Block() as block:
            @block.sync
            def _(sp):
                sp.dma_start(ident[:, :], A["ident"]).then_inc(ident_in, 16)
                sp.wait_ge(ident_in, 16)

        s_st, s_sb, _, _ = scope(nc)
        with s_st:
            sT = s_sb("sT", [P, 3, NS * NH])
            h_st, h_sb, _, h_sem = scope(nc)
            with h_st:
                hT_hi = h_sb("hT_hi", [P, KC, TOK], F32R)
                hT_lo = h_sb("hT_lo", [P, KC, TOK], F32R)
                raw = h_sb("w_raw", [P, KC, CH])
                w_in = [h_sem("w_in0"), h_sem("w_in1")]
                norm_and_transpose(nc, A, hT_hi, hT_lo, ident, raw, w_in)
                project(nc, A, S, hT_hi, hT_lo, sT, raw, w_in)
            e_st, e_sb, _, e_sem = scope(nc)
            with e_st:
                E = SampleBuffers(e_sb, e_sem)
                attend_prompt(nc, A, S, O, ident, E)
                attend_sample(nc, A, S, ident, sT, E)
        gla_prompt(nc, A, S, O, ident)
        w_st, w_sb, _, w_sem = scope(nc)
        with w_st:
            W = MergeWeights(w_sb, w_sem)
            gla_sample(nc, A, S, O, ident, W)
            merge(nc, A, S, O, ident, W)


_OUTS = [("y_prompt", (1, SEQ, D)), ("y_sample", (DB, T, D))] + \
        [(f"kv_w{w}_prompt", (1, 1, min(w, SEQ), 2, NH, HD)) for w in (128, 512, 2048)] + \
        [("gla_prompt", (1, 1, GH, GK, GV_W))] + \
        [(f"kv_w{w}_sample", (1, DB, T, 2, NH, HD)) for w in (128, 512, 2048)] + \
        [("gla_sample", (1, DB, GH, GK, GV_W))]


_INS = ["x_prompt", "x_sample", "cache_kv_w128", "cache_kv_w512", "cache_kv_w2048", "state_gla", "ln_w", "w_in",
        "w_gla_a2", "b_gla_a", "gla_norm_w", "w_attn_out", "w_gla_out", "w_out", "final_norm_w"]


def _constants():
    import numpy as np

    half = HALF
    inv = (1.0 / (np.float32(500000.0) ** (np.arange(half, dtype=np.float32) * np.float32(2.0 / 16)))).astype(np.float32)
    pos = np.concatenate([np.arange(SEQ), np.arange(SEQ - NS, SEQ), SEQ + np.arange(NS) % T]).astype(np.float32)
    ang = pos[:, None] * inv[None, :]
    rope = np.concatenate([np.cos(ang), np.sin(ang)], axis=1).astype(np.float32)
    q, k = np.arange(P)[:, None], np.arange(P)[None, :]
    own = np.where(k <= q, 0.0, NEG)
    masks = np.stack([np.concatenate([np.full((P, P), NEG), own], 1),
                      np.concatenate([np.where(k >= q, 0.0, NEG), own], 1)], axis=1).astype(np.float32)
    chunk_mask = ((k >= q) & (k // CHUNK == q // CHUNK)).astype(np.uint32)
    tok = (np.arange(ROWS) // NH % T)[:, None]
    j = np.arange(T)[None, :]
    seen = np.stack([np.concatenate([k >= tok, j <= tok], 1),
                     np.concatenate([k >= tok // 4, (j == tok) | (j == tok - 4)], 1),
                     np.concatenate([k >= 0 * tok, j == tok], 1)], axis=1)
    dec_mask = np.where(seen, 0.0, NEG).astype(np.float32)
    dec_diag = (np.arange(CH)[None, :] // HD == np.arange(ROWS)[:, None] % NH).astype(np.float32)
    n = np.arange(NS)
    sample_mask = ((n[None, :] >= n[:, None]) & (n[None, :] // T == n[:, None] // T)).astype(np.uint32)
    batch_mask = (n[:, None] // T == np.arange(DB)[None, :]).astype(np.float32)
    return {"rope": rope, "ident": np.eye(P, dtype=np.float32), "masks": masks, "chunk_mask": chunk_mask,
            "dec_mask": dec_mask, "dec_diag": dec_diag, "sample_mask": sample_mask, "batch_mask": batch_mask}


def kernel(**inputs):
    import numpy as np
    import concourse.bacc as bacc
    from concourse.bass_utils import run_bass_kernel_spmd as run

    nc = bacc.Bacc("TRN2", target_bir_lowering=False, num_devices=1)
    arrays, A = {}, {}
    inputs = dict(inputs)
    inputs["ln_w"] = np.asarray(inputs["ln_w"]).reshape(KC, P).T
    inputs["b_gla_a"] = np.asarray(inputs["b_gla_a"]).reshape(GH // 2, P).T
    for name, a in [(n, inputs[n]) for n in _INS] + sorted(_constants().items()):
        a = np.ascontiguousarray(a)
        arrays["in_" + name] = a
        A[name] = nc.dram_tensor("in_" + name, a.shape, mybir.dt.from_np(a.dtype), kind="ExternalInput").ap()
    O = {name: nc.dram_tensor("out_" + name, shape, F32, kind="ExternalOutput").ap() for name, shape in _OUTS}
    decoder_step(nc, A, O)
    r = run(nc, [arrays], core_ids=[0]).results[0]
    return tuple(r["out_" + name] for name, _ in _OUTS)
```
